# Optimizing a Trainium2 kernel written in Bass

```python
import math
import jax, jax.numpy as jnp
from jax import lax
import numpy as np
import jax
import jax.numpy as jnp

D_MODEL = 1024
BATCH = 1
SEQ = 512
DEPTH = 1

D_MIX = 2 * D_MODEL
D_ATT = D_MIX // 2
ATT_HEAD_DIM = 64
ATT_HEADS = D_ATT // ATT_HEAD_DIM
ATT_STEPS = 128
DILATIONS = (1, 4, 16)
D_SSM = D_MIX - D_ATT
SSM_HEAD_DIM = 64
SSM_HEADS = D_SSM // SSM_HEAD_DIM
SSM_GROUPS = 2
SSM_STATE = 128
CONV_WIDTH = 4
CHUNK = 128
D_CONV = D_SSM + 2 * SSM_GROUPS * SSM_STATE
D_IN_PROJ = 4 * D_ATT + D_SSM + D_CONV + SSM_HEADS
SPLITS = (D_ATT, 2 * D_ATT, 3 * D_ATT, 4 * D_ATT, 4 * D_ATT + D_SSM, 4 * D_ATT + D_SSM + D_CONV)
NORM_EPS = 1e-5


def rms_norm(u, g):
    uf = u.astype(jnp.float32)
    uf = uf * lax.rsqrt(jnp.mean(uf * uf, axis=-1, keepdims=True) + NORM_EPS)
    return (uf * g.astype(jnp.float32)).astype(u.dtype)

def layer_norm(u, g, b):
    uf = u.astype(jnp.float32)
    mu = jnp.mean(uf, axis=-1, keepdims=True)
    var = jnp.mean(jnp.square(uf - mu), axis=-1, keepdims=True)
    out = (uf - mu) * lax.rsqrt(var + NORM_EPS) * g.astype(jnp.float32) + b.astype(jnp.float32)
    return out.astype(u.dtype)

def alibi_slopes(n_heads):
    return jnp.asarray(2.0 ** (-8.0 * np.arange(1, n_heads + 1) / n_heads), dtype=jnp.float32)

def dilated_window_attention(q, k, v, slopes, dilation):
    B, S, H, E = q.shape
    unit = dilation * ATT_STEPS
    s_pad = -(-S // unit) * unit
    nb = s_pad // unit
    pad = ((0, 0), (0, s_pad - S), (0, 0), (0, 0))

    def to_blocks(t):
        return jnp.pad(t, pad).reshape(B, nb, ATT_STEPS, dilation, H, E)

    def with_prev(t):
        prev = jnp.pad(t, ((0, 0), (1, 0), (0, 0), (0, 0), (0, 0), (0, 0)))[:, :-1]
        return jnp.concatenate([prev, t], axis=2)

    qb = to_blocks(q)
    kk = with_prev(to_blocks(k))
    vv = with_prev(to_blocks(v))
    scores = jnp.einsum('bnqrhe,bnkrhe->bnrhqk', qb, kk).astype(jnp.float32)

    n_idx = jnp.arange(nb)[:, None, None]
    jq = n_idx * ATT_STEPS + jnp.arange(ATT_STEPS)[None, :, None]
    jk = (n_idx - 1) * ATT_STEPS + jnp.arange(2 * ATT_STEPS)[None, None, :]
    steps = jq - jk
    valid = (jk >= 0) & (steps >= 0) & (steps <= ATT_STEPS)
    dist = (steps * dilation).astype(jnp.float32)
    bias = -slopes[None, None, :, None, None] * dist[:, None, None, :, :]
    scores = jnp.where(valid[:, None, None], scores + bias, -jnp.inf)

    lse = jax.nn.logsumexp(scores, axis=-1)
    p = jnp.exp(scores - lse[..., None]).astype(vv.dtype)
    o = jnp.einsum('bnrhqk,bnkrhe->bnqrhe', p, vv)
    o = o.reshape(B, s_pad, H, E)[:, :S]
    lse = lse.transpose(0, 1, 4, 2, 3).reshape(B, s_pad, H)[:, :S]
    return o, lse

def causal_depthwise_conv(u, w, bias):
    out = lax.conv_general_dilated(
        u, w[:, None, :].astype(u.dtype), window_strides=(1,), padding=((CONV_WIDTH - 1, 0),),
        dimension_numbers=('NWC', 'WIO', 'NWC'), feature_group_count=u.shape[-1])
    return out + bias.astype(u.dtype)

def segsum(a):
    cs = jnp.cumsum(a, axis=-1)
    l = a.shape[-1]
    diff = cs[..., :, None] - cs[..., None, :]
    mask = jnp.tril(jnp.ones((l, l), dtype=bool))
    return jnp.where(mask, diff, -jnp.inf)

def ssd_chunked(x, dt, a, b, c):
    Bsz, S, H, P = x.shape
    G, N = b.shape[2], b.shape[3]
    J = H // G
    nc = S // CHUNK
    xg = (x * dt[..., None]).reshape(Bsz, nc, CHUNK, G, J, P)
    adt = (dt * a).reshape(Bsz, nc, CHUNK, G, J).transpose(0, 1, 3, 4, 2)
    bc = b.reshape(Bsz, nc, CHUNK, G, N)
    cc = c.reshape(Bsz, nc, CHUNK, G, N)
    a_cs = jnp.cumsum(adt, axis=-1)

    decay = jnp.exp(segsum(adt))
    cb = jnp.einsum('bclgn,bcsgn->bcgls', cc, bc)
    y_diag = jnp.einsum('bcgjls,bcsgjp->bclgjp', cb[:, :, :, None] * decay, xg)

    decay_to_end = jnp.exp(a_cs[..., -1:] - a_cs).transpose(0, 1, 4, 2, 3)[..., None]
    states = jnp.einsum('bcsgn,bcsgjp->bcgjpn', bc, xg * decay_to_end)

    chunk_decay = jnp.exp(a_cs[..., -1])

    def step(h, inp):
        st, dec = inp
        return h * dec[..., None, None] + st, h

    h0 = jnp.zeros((Bsz, G, J, P, N), dtype=jnp.float32)
    _, prev = lax.scan(step, h0, (jnp.moveaxis(states, 1, 0), jnp.moveaxis(chunk_decay, 1, 0)))
    prev = jnp.moveaxis(prev, 0, 1)

    state_decay = jnp.exp(a_cs).transpose(0, 1, 4, 2, 3)[..., None]
    y_off = jnp.einsum('bclgn,bcgjpn->bclgjp', cc, prev) * state_decay
    return (y_diag + y_off).reshape(Bsz, S, H, P)

def first_inputs(seed: int = 0) -> dict:
    key = jax.random.key(seed)
    ks = jax.random.split(key, 14)
    beta = (8.0 * DEPTH) ** -0.25
    f32 = jnp.float32
    x = jax.random.normal(ks[0], (BATCH, SEQ, D_MODEL), f32)
    col_scale = np.ones((D_IN_PROJ,), np.float32)
    col_scale[2 * D_ATT:3 * D_ATT] = beta
    col_scale[4 * D_ATT + D_SSM:4 * D_ATT + 2 * D_SSM] = beta
    w_in = jax.random.normal(ks[1], (DEPTH, D_MODEL, D_IN_PROJ), f32) * (D_MODEL ** -0.5) * jnp.asarray(col_scale)
    conv_w = jax.random.normal(ks[2], (DEPTH, CONV_WIDTH, D_CONV), f32) * (CONV_WIDTH ** -0.5)
    conv_b = 0.02 * jax.random.normal(ks[3], (DEPTH, D_CONV), f32)
    dt0 = jnp.exp(jax.random.uniform(ks[4], (DEPTH, SSM_HEADS), f32, math.log(1e-3), math.log(1e-1)))
    dt_bias = dt0 + jnp.log(-jnp.expm1(-dt0))
    a_log = jnp.log(jax.random.uniform(ks[5], (DEPTH, SSM_HEADS), f32, 1.0, 16.0))
    d_skip = 1.0 + 0.1 * jax.random.normal(ks[6], (DEPTH, SSM_HEADS), f32)
    att_norm_g = 1.0 + 0.1 * jax.random.normal(ks[7], (DEPTH, D_ATT), f32)
    ssm_norm_g = 1.0 + 0.1 * jax.random.normal(ks[8], (DEPTH, D_SSM), f32)
    w_out = jax.random.normal(ks[9], (DEPTH, D_MIX, D_MODEL), f32) * (D_MIX ** -0.5) * beta
    ln_g = 1.0 + 0.1 * jax.random.normal(ks[10], (DEPTH, D_MODEL), f32)
    ln_b = 0.02 * jax.random.normal(ks[11], (DEPTH, D_MODEL), f32)
    return {'x': x, 'w_in': w_in, 'conv_w': conv_w, 'conv_b': conv_b, 'dt_bias': dt_bias,
            'a_log': a_log, 'd_skip': d_skip, 'att_norm_g': att_norm_g, 'ssm_norm_g': ssm_norm_g,
            'w_out': w_out, 'ln_g': ln_g, 'ln_b': ln_b}

def first_block(x, w_in, conv_w, conv_b, dt_bias, a_log, d_skip, att_norm_g, ssm_norm_g, w_out, ln_g, ln_b):
    alpha = (2.0 * DEPTH) ** 0.25
    slopes = alibi_slopes(ATT_HEADS)
    Bsz, S, _ = x.shape
    for layer in range(DEPTH):
        proj = jnp.einsum('bsd,de->bse', x, w_in[layer])
        q, k, v, z_att, z_ssm, xbc, dt_raw = jnp.split(proj, list(SPLITS), axis=-1)

        q = q.reshape(Bsz, S, ATT_HEADS, ATT_HEAD_DIM) * (ATT_HEAD_DIM ** -0.5)
        k = k.reshape(Bsz, S, ATT_HEADS, ATT_HEAD_DIM)
        v = v.reshape(Bsz, S, ATT_HEADS, ATT_HEAD_DIM)
        o1, l1 = dilated_window_attention(q, k, v, slopes, DILATIONS[0])
        o2, l2 = dilated_window_attention(q, k, v, slopes, DILATIONS[1])
        o3, l3 = dilated_window_attention(q, k, v, slopes, DILATIONS[2])
        wts = jax.nn.softmax(jnp.stack([l1, l2, l3], axis=0), axis=0)
        y_att = (wts[0][..., None] * o1 + wts[1][..., None] * o2 + wts[2][..., None] * o3).astype(x.dtype)
        y_att = rms_norm(y_att.reshape(Bsz, S, D_ATT) * jax.nn.silu(z_att), att_norm_g[layer])

        xbc = jax.nn.silu(causal_depthwise_conv(xbc, conv_w[layer], conv_b[layer]))
        xs, bm, cm = jnp.split(xbc, [D_SSM, D_SSM + SSM_GROUPS * SSM_STATE], axis=-1)
        dt = jax.nn.softplus(dt_raw.astype(jnp.float32) + dt_bias[layer].astype(jnp.float32))
        a = -jnp.exp(a_log[layer].astype(jnp.float32))
        xs_h = xs.reshape(Bsz, S, SSM_HEADS, SSM_HEAD_DIM).astype(jnp.float32)
        y = ssd_chunked(xs_h, dt, a,
                        bm.reshape(Bsz, S, SSM_GROUPS, SSM_STATE).astype(jnp.float32),
                        cm.reshape(Bsz, S, SSM_GROUPS, SSM_STATE).astype(jnp.float32))
        y = y + d_skip[layer].astype(jnp.float32)[:, None] * xs_h
        y_ssm = rms_norm(y.reshape(Bsz, S, D_SSM).astype(x.dtype) * jax.nn.silu(z_ssm), ssm_norm_g[layer])

        mix = jnp.concatenate([y_att, y_ssm], axis=-1)
        out = jnp.einsum('bse,ed->bsd', mix, w_out[layer])
        x = layer_norm(alpha * x + out, ln_g[layer], ln_b[layer])
    return x


N_MIXERS = 2
EPS = 1e-6

GDN_QK_HEADS = 8
GDN_V_HEADS = 16
GDN_HEAD_DIM = 128
GDN_CONV = 4
GDN_CHUNK = 64
GDN_QK_W = GDN_QK_HEADS * GDN_HEAD_DIM
GDN_V_W = GDN_V_HEADS * GDN_HEAD_DIM
GDN_CONV_W = 2 * GDN_QK_W + GDN_V_W
GDN_IN = GDN_CONV_W + GDN_V_W + 2 * GDN_V_HEADS

NSA_HEADS = 16
NSA_GROUPS = 4
NSA_HPG = NSA_HEADS // NSA_GROUPS
NSA_HEAD_DIM = 64
NSA_CMP_LEN = 32
NSA_CMP_STRIDE = 16
NSA_SLC_LEN = 64
NSA_TOP_K = 8
NSA_WINDOW = 512
NSA_QBLOCK = 128
NSA_Q_W = NSA_HEADS * NSA_HEAD_DIM
NSA_KV_W = NSA_GROUPS * NSA_HEAD_DIM
NSA_IN = 2 * NSA_Q_W + 6 * NSA_KV_W + 3 * NSA_HEADS

REL_BUCKETS = 32
REL_MAX_DIST = 128
NEG_INF = -1e30


def rms_norm_2(x, g):
    xf = x.astype(jnp.float32)
    y = xf * lax.rsqrt(jnp.mean(xf * xf, axis=-1, keepdims=True) + EPS)
    return (y * g.astype(jnp.float32)).astype(x.dtype)

def l2norm(x):
    return x * lax.rsqrt(jnp.sum(x * x, axis=-1, keepdims=True) + EPS)

def rel_bucket(dist):
    n = jnp.maximum(dist, 0)
    max_exact = REL_BUCKETS // 2
    nf = jnp.maximum(n, 1).astype(jnp.float32)
    large = max_exact + (jnp.log(nf / max_exact) / math.log(REL_MAX_DIST / max_exact)
                         * (REL_BUCKETS - max_exact)).astype(jnp.int32)
    large = jnp.minimum(large, REL_BUCKETS - 1)
    return jnp.where(n < max_exact, n, large)

def head_bias(rel_bias, dist):
    b = rel_bias[rel_bucket(dist)]
    return jnp.transpose(b, (2, 0, 1)).reshape(NSA_GROUPS, NSA_HPG, dist.shape[0], dist.shape[1])

def causal_depthwise_conv_2(x, w):
    kw, ch = w.shape
    return lax.conv_general_dilated(x, w[:, None, :].astype(x.dtype), window_strides=(1,),
                                    padding=[(kw - 1, 0)], dimension_numbers=('NWC', 'WIO', 'NWC'),
                                    feature_group_count=ch)

def gated_deltanet(h, w_in, conv_w, a_log, dt_bias, norm_w, w_out):
    bsz, t, _ = h.shape
    nh, dh, cs = GDN_V_HEADS, GDN_HEAD_DIM, GDN_CHUNK
    nc = t // cs
    f32 = jnp.float32
    proj = h @ w_in
    qkv, z, b_lin, a_lin = jnp.split(proj, [GDN_CONV_W, GDN_CONV_W + GDN_V_W, GDN_CONV_W + GDN_V_W + nh], axis=-1)
    qkv = jax.nn.silu(causal_depthwise_conv_2(qkv, conv_w)).astype(f32)
    q, k, v = jnp.split(qkv, [GDN_QK_W, 2 * GDN_QK_W], axis=-1)
    rep = nh // GDN_QK_HEADS
    q = jnp.repeat(l2norm(q.reshape(bsz, t, GDN_QK_HEADS, dh)), rep, axis=2) * (dh ** -0.5)
    k = jnp.repeat(l2norm(k.reshape(bsz, t, GDN_QK_HEADS, dh)), rep, axis=2)
    v = v.reshape(bsz, t, nh, dh)
    beta = jax.nn.sigmoid(b_lin.astype(f32))
    g = -jnp.exp(a_log.astype(f32)) * jax.nn.softplus(a_lin.astype(f32) + dt_bias.astype(f32))
    to_chunks = lambda u: u.reshape(bsz, nc, cs, nh, -1).transpose(0, 3, 1, 2, 4)
    q, k, v = to_chunks(q), to_chunks(k), to_chunks(v)
    beta = to_chunks(beta)[..., 0]
    gc = jnp.cumsum(to_chunks(g)[..., 0], axis=-1)
    idx = jnp.arange(cs)
    lower = idx[:, None] >= idx[None, :]
    strict = idx[:, None] > idx[None, :]
    decay = jnp.exp(jnp.where(lower, gc[..., :, None] - gc[..., None, :], -jnp.inf))
    kb = k * beta[..., None]
    a_mat = jnp.where(strict, jnp.einsum('bhncd,bhnsd->bhncs', kb, k) * decay, 0.0)
    eye = jnp.eye(cs, dtype=f32)
    l_mat = a_mat + eye
    t_mat = lax.linalg.triangular_solve(l_mat, jnp.broadcast_to(eye, l_mat.shape), left_side=True,
                                        lower=True, unit_diagonal=True)
    u = jnp.einsum('bhncs,bhnsd->bhncd', t_mat, v * beta[..., None])
    w = jnp.einsum('bhncs,bhnsd->bhncd', t_mat, kb * jnp.exp(gc)[..., None])
    qk = jnp.where(lower, jnp.einsum('bhncd,bhnsd->bhncs', q, k) * decay, 0.0)
    g_last = gc[..., -1]
    k_dec = k * jnp.exp(g_last[..., None] - gc)[..., None]
    q_dec = q * jnp.exp(gc)[..., None]
    xs = tuple(jnp.moveaxis(a, 2, 0) for a in (q_dec, qk, u, w, k_dec, jnp.exp(g_last)))

    def step(state, inp):
        qd, qkc, uc, wc, kd, gl = inp
        v_new = uc - jnp.einsum('bhcd,bhde->bhce', wc, state)
        o = jnp.einsum('bhcd,bhde->bhce', qd, state) + jnp.einsum('bhcs,bhse->bhce', qkc, v_new)
        state = state * gl[..., None, None] + jnp.einsum('bhcd,bhce->bhde', kd, v_new)
        return state, o

    s0 = jnp.zeros((bsz, nh, dh, dh), f32)
    _, o = lax.scan(step, s0, xs)
    o = o.transpose(1, 0, 3, 2, 4).reshape(bsz, t, nh, dh)
    o = rms_norm_2(o, norm_w) * jax.nn.silu(z.reshape(bsz, t, nh, dh).astype(f32))
    return o.reshape(bsz, t, nh * dh).astype(h.dtype) @ w_out

def native_sparse_attention(h, w_in, cmp_pos, cmp_w1, cmp_w2, rel_bias, w_out):
    bsz, t, _ = h.shape
    nh, ng, hpg, dh = NSA_HEADS, NSA_GROUPS, NSA_HPG, NSA_HEAD_DIM
    f32 = jnp.float32
    proj = h @ w_in
    q = proj[..., :NSA_Q_W].reshape(bsz, t, ng, hpg, dh).transpose(0, 2, 3, 1, 4) * (dh ** -0.5)
    kv = proj[..., NSA_Q_W:NSA_Q_W + 6 * NSA_KV_W].reshape(bsz, t, 6, ng, dh)
    kc, vc, ks, vs, kw, vw = [kv[:, :, i] for i in range(6)]
    off = NSA_Q_W + 6 * NSA_KV_W
    gates = jax.nn.sigmoid(proj[..., off:off + 3 * nh].astype(f32)).reshape(bsz, t, ng, hpg, 3)
    gates = gates.transpose(0, 2, 3, 1, 4)
    z = proj[..., off + 3 * nh:]

    n_cmp = (t - NSA_CMP_LEN) // NSA_CMP_STRIDE + 1
    tok = jnp.arange(n_cmp)[:, None] * NSA_CMP_STRIDE + jnp.arange(NSA_CMP_LEN)[None, :]

    def compress(xk, i):
        blk = xk[:, tok] + cmp_pos[i][None, None, :, None, :]
        blk = blk.transpose(0, 1, 3, 2, 4).reshape(bsz, n_cmp, ng, NSA_CMP_LEN * dh)
        return (jax.nn.silu(blk @ cmp_w1[i]) @ cmp_w2[i]).transpose(0, 2, 1, 3)

    k_cmp = compress(kc, 0)
    v_cmp = compress(vc, 1)
    cmp_end = jnp.arange(n_cmp) * NSA_CMP_STRIDE + NSA_CMP_LEN - 1

    n_slc = t // NSA_SLC_LEN
    k_sel = min(NSA_TOP_K, n_slc)
    c_start = jnp.arange(n_cmp)[:, None] * NSA_CMP_STRIDE
    s_start = jnp.arange(n_slc)[None, :] * NSA_SLC_LEN
    overlap = (jnp.clip(jnp.minimum(c_start + NSA_CMP_LEN, s_start + NSA_SLC_LEN) - jnp.maximum(c_start, s_start), 0)
               .astype(f32) / NSA_CMP_LEN)
    ks_blk = ks.reshape(bsz, n_slc, NSA_SLC_LEN, ng, dh).transpose(0, 3, 1, 2, 4)
    vs_blk = vs.reshape(bsz, n_slc, NSA_SLC_LEN, ng, dh).transpose(0, 3, 1, 2, 4)
    gather = jax.vmap(jax.vmap(lambda kb, ix: kb[ix]))
    tbl = rel_bias.T.reshape(ng, hpg, REL_BUCKETS)
    gi = jnp.arange(ng)[None, :, None, None, None]
    hi = jnp.arange(hpg)[None, None, :, None, None]
    blk_id = jnp.arange(n_slc)

    pad = ((0, 0), (0, 0), (NSA_WINDOW, 0), (0, 0))
    kw_p = jnp.pad(kw.transpose(0, 2, 1, 3), pad)
    vw_p = jnp.pad(vw.transpose(0, 2, 1, 3), pad)

    def query_block(bi):
        q0 = bi * NSA_QBLOCK
        qb = lax.dynamic_slice_in_dim(q, q0, NSA_QBLOCK, axis=3)
        gb = lax.dynamic_slice_in_dim(gates, q0, NSA_QBLOCK, axis=3)
        tq = q0 + jnp.arange(NSA_QBLOCK)
        dist = tq[:, None] - cmp_end[None, :]
        valid = dist >= 0
        s = jnp.einsum('bghqd,bgkd->bghqk', qb, k_cmp).astype(f32) + head_bias(rel_bias, dist)
        s = jnp.where(valid, s, NEG_INF)
        p_cmp = jax.nn.softmax(s, axis=-1) * jnp.any(valid, axis=-1)[:, None].astype(f32)
        o_cmp = jnp.einsum('bghqk,bgkd->bghqd', p_cmp.astype(v_cmp.dtype), v_cmp)
        imp = jnp.einsum('bghqk,ks->bgqs', p_cmp, overlap)
        cur = tq // NSA_SLC_LEN
        forced = (blk_id[None, :] == 0) | (blk_id[None, :] == cur[:, None]) | (blk_id[None, :] == cur[:, None] - 1)
        causal_blk = blk_id[None, :] * NSA_SLC_LEN <= tq[:, None]
        imp = jnp.where(forced, jnp.inf, jnp.where(causal_blk, imp, -jnp.inf))
        _, sel = lax.top_k(imp, k_sel)
        n_s = k_sel * NSA_SLC_LEN
        k_g = gather(ks_blk, sel).reshape(bsz, ng, NSA_QBLOCK, n_s, dh)
        v_g = gather(vs_blk, sel).reshape(bsz, ng, NSA_QBLOCK, n_s, dh)
        pos = (sel[..., None] * NSA_SLC_LEN + jnp.arange(NSA_SLC_LEN)).reshape(bsz, ng, NSA_QBLOCK, n_s)
        dist_s = tq[None, None, :, None] - pos
        s = jnp.einsum('bghqd,bgqsd->bghqs', qb, k_g).astype(f32) + tbl[gi, hi, rel_bucket(dist_s)[:, :, None]]
        s = jnp.where((dist_s >= 0)[:, :, None], s, NEG_INF)
        o_slc = jnp.einsum('bghqs,bgqsd->bghqd', jax.nn.softmax(s, axis=-1).astype(v_g.dtype), v_g)
        kwb = lax.dynamic_slice_in_dim(kw_p, q0, NSA_WINDOW + NSA_QBLOCK, axis=2)
        vwb = lax.dynamic_slice_in_dim(vw_p, q0, NSA_WINDOW + NSA_QBLOCK, axis=2)
        tk = q0 - NSA_WINDOW + jnp.arange(NSA_WINDOW + NSA_QBLOCK)
        dist_w = tq[:, None] - tk[None, :]
        valid_w = (dist_w >= 0) & (dist_w < NSA_WINDOW) & (tk[None, :] >= 0)
        s = jnp.einsum('bghqd,bgkd->bghqk', qb, kwb).astype(f32) + head_bias(rel_bias, dist_w)
        s = jnp.where(valid_w, s, NEG_INF)
        o_win = jnp.einsum('bghqk,bgkd->bghqd', jax.nn.softmax(s, axis=-1).astype(vwb.dtype), vwb)
        return (gb[..., 0:1] * o_cmp.astype(f32) + gb[..., 1:2] * o_slc.astype(f32)
                + gb[..., 2:3] * o_win.astype(f32))

    outs = lax.map(query_block, jnp.arange(t // NSA_QBLOCK))
    o = outs.transpose(1, 0, 4, 2, 3, 5).reshape(bsz, t, nh * dh)
    o = o * jax.nn.silu(z.astype(f32))
    return o.astype(h.dtype) @ w_out

def second_inputs(seed: int = 0) -> dict:
    key = jax.random.key(seed)
    ks = jax.random.split(key, 20)
    n_a = (DEPTH + N_MIXERS - 1) // N_MIXERS
    n_b = DEPTH // N_MIXERS
    nrm = lambda k, shape, scale: jax.random.normal(k, shape, jnp.float32) * scale
    dt = jnp.exp(jax.random.uniform(ks[7], (n_a, GDN_V_HEADS), jnp.float32, math.log(1e-3), math.log(1e-1)))
    return {
        'x': nrm(ks[0], (BATCH, SEQ, D_MODEL), 1.0),
        'c': nrm(ks[1], (BATCH, D_MODEL), 1.0),
        'ada_w': nrm(ks[2], (DEPTH, D_MODEL, 3 * D_MODEL), D_MODEL ** -0.5),
        'ada_b': nrm(ks[3], (DEPTH, 3 * D_MODEL), 0.01),
        'norm_g': 1.0 + nrm(ks[4], (DEPTH, D_MODEL), 0.05),
        'gdn_w_in': nrm(ks[5], (n_a, D_MODEL, GDN_IN), D_MODEL ** -0.5),
        'gdn_conv_w': nrm(ks[6], (n_a, GDN_CONV, GDN_CONV_W), GDN_CONV ** -0.5),
        'gdn_a_log': jnp.log(jax.random.uniform(ks[8], (n_a, GDN_V_HEADS), jnp.float32, 1.0, 16.0)),
        'gdn_dt_bias': dt + jnp.log(-jnp.expm1(-dt)),
        'gdn_norm_w': 1.0 + nrm(ks[9], (n_a, GDN_HEAD_DIM), 0.05),
        'gdn_w_out': nrm(ks[10], (n_a, GDN_V_W, D_MODEL), GDN_V_W ** -0.5),
        'nsa_w_in': nrm(ks[11], (n_b, D_MODEL, NSA_IN), D_MODEL ** -0.5),
        'nsa_cmp_pos': nrm(ks[12], (n_b, 2, NSA_CMP_LEN, NSA_HEAD_DIM), 0.1),
        'nsa_cmp_w1': nrm(ks[13], (n_b, 2, NSA_CMP_LEN * NSA_HEAD_DIM, NSA_HEAD_DIM), (NSA_CMP_LEN * NSA_HEAD_DIM) ** -0.5),
        'nsa_cmp_w2': nrm(ks[14], (n_b, 2, NSA_HEAD_DIM, NSA_HEAD_DIM), NSA_HEAD_DIM ** -0.5),
        'nsa_w_out': nrm(ks[15], (n_b, NSA_Q_W, D_MODEL), NSA_Q_W ** -0.5),
        'rel_bias': nrm(ks[16], (REL_BUCKETS, NSA_HEADS), 0.5),
        'final_g': 1.0 + nrm(ks[17], (D_MODEL,), 0.05),
    }

def second_block(x, c, ada_w, ada_b, norm_g, gdn_w_in, gdn_conv_w, gdn_a_log, gdn_dt_bias, gdn_norm_w, gdn_w_out,
              nsa_w_in, nsa_cmp_pos, nsa_cmp_w1, nsa_cmp_w2, nsa_w_out, rel_bias, final_g):
    cond = jax.nn.silu(c)
    for i in range(DEPTH):
        mod = cond @ ada_w[i] + ada_b[i]
        shift, scale, gate = jnp.split(mod, 3, axis=-1)
        hdn = rms_norm_2(x, norm_g[i]) * (1.0 + scale[:, None, :]) + shift[:, None, :]
        j = i // N_MIXERS
        if i % N_MIXERS == 0:
            y = gated_deltanet(hdn, gdn_w_in[j], gdn_conv_w[j], gdn_a_log[j], gdn_dt_bias[j], gdn_norm_w[j], gdn_w_out[j])
        else:
            y = native_sparse_attention(hdn, nsa_w_in[j], nsa_cmp_pos[j], nsa_cmp_w1[j], nsa_cmp_w2[j], rel_bias, nsa_w_out[j])
        x = x + gate[:, None, :] * y
    return rms_norm_2(x, final_g)


def setup_inputs(seed=0):
    out = dict(first_inputs(seed))
    for name, value in second_inputs(seed + 1).items():
        if name != "x":
            out[name + "_2"] = value
    return out


def reference(
    x, w_in, conv_w, conv_b, dt_bias, a_log, d_skip, att_norm_g, ssm_norm_g, w_out, ln_g, ln_b,
    c_2, ada_w_2, ada_b_2, norm_g_2, gdn_w_in_2, gdn_conv_w_2, gdn_a_log_2, gdn_dt_bias_2,
    gdn_norm_w_2, gdn_w_out_2, nsa_w_in_2, nsa_cmp_pos_2, nsa_cmp_w1_2, nsa_cmp_w2_2,
    nsa_w_out_2, rel_bias_2, final_g_2,
):
    x = first_block(
        x, w_in, conv_w, conv_b, dt_bias, a_log, d_skip, att_norm_g, ssm_norm_g, w_out, ln_g,
        ln_b,
    )
    return second_block(
        x, c_2, ada_w_2, ada_b_2, norm_g_2, gdn_w_in_2, gdn_conv_w_2, gdn_a_log_2,
        gdn_dt_bias_2, gdn_norm_w_2, gdn_w_out_2, nsa_w_in_2, nsa_cmp_pos_2, nsa_cmp_w1_2,
        nsa_cmp_w2_2, nsa_w_out_2, rel_bias_2, final_g_2,
    )


_drawn_inputs = setup_inputs


def setup_inputs(seed=0):
    import zlib

    import numpy as np

    out = dict(_drawn_inputs(seed))
    spreads = {}
    factors = {'conv_b': 3.586, 'ada_b_2': 5.19, 'gdn_norm_w_2': 3.151}
    for name, (base, spread) in spreads.items():
        noise = np.random.default_rng([zlib.crc32(name.encode()), seed]).standard_normal(out[name].shape)
        drawn = base * np.exp(spread * noise) if base else spread * noise
        out[name] = jnp.asarray(drawn.astype(out[name].dtype))
    for name, factor in factors.items():
        out[name] = (out[name] * factor).astype(out[name].dtype)
    return out
```

```python
from contextlib import ExitStack

import numpy as np

import concourse.bass as bass
from concourse import mybir

F32 = mybir.dt.float32
F32R = mybir.dt.float32r
ALU = mybir.AluOpType
ACT = mybir.ActivationFunctionType

P = 128
SEQ, D_MODEL = 512, 1024
TT = SEQ // P
KT = D_MODEL // P
HALF = KT // 2
COLS = 512
ATT_HEADS, HD = 16, 64
SSM_HEADS, SSM_GROUPS = 16, 2
HPG = SSM_HEADS // SSM_GROUPS
D_CONV1 = 1536
CT1 = D_CONV1 // P
CONV = 4
COL_XBC = 5120
COL_DT = 6656
QK_SCALE = HD ** -0.5
S_OFF = {2: 0, 0: 384, 3: 512, 1: 1024}
S_LEN = 1280
EPS1 = 1e-5
QK_HEADS, V_HEADS = 8, 16
D_CONV2 = 4096
D_Z2 = V_HEADS * P
MOD_COLS = 1536
EPS2 = 1e-6
ALPHA = 2.0 ** 0.25


def attention_bias():
    dist = np.arange(P)[:, None] + 384 - np.arange(SEQ)[None, :]
    count = (((dist <= 128).astype(int) + (dist % 4 == 0) + (dist % 16 == 0)) * (dist >= 0))
    slopes = (2.0 ** (-8.0 * np.arange(1, ATT_HEADS + 1) / ATT_HEADS)).astype(np.float32)
    log_count = np.where(count > 0, np.log(np.maximum(count, 1)), -1e30)
    bias = (-slopes[:, None, None] * dist + log_count) / QK_SCALE
    return bias.astype(np.float32)


def square_masks():
    j, l = np.arange(P)[:, None], np.arange(P)[None, :]
    return np.stack([j == l, j <= l, j > l, j >= 0 * l], 1).astype(np.float32)


IDENT, UPPER, BELOW, ONES = range(4)


def block_masks():
    j, l = np.arange(P)[:, None], np.arange(P)[None, :]
    levels = [(j // (2 * b) == l // (2 * b)) & (j // b < l // b) for b in (16, 32, 64)]
    return np.stack([j < l, j // 32 == l // 32] + levels, 1).astype(np.float32)


def log1p_series():
    return [1.0 / (2 * k + 1) for k in range(1, 9)]


class Phase(ExitStack):

    used = []

    def __init__(self, nc, name):
        super().__init__()
        self.nc, self.name = nc, name

    @classmethod
    def clear_semaphores(cls, nc):
        nums = sorted(set(cls.used))
        cls.used.clear()
        with nc.Block() as block:
            @block.gpsimd
            def _(pool):
                start = 0
                for n in range(1, len(nums) + 1):
                    if n == len(nums) or nums[n] != nums[n - 1] + 1:
                        pool.sem_clear(range(nums[start], nums[n - 1] + 1))
                        start = n

    def sb(self, name, shape, dt=F32):
        return self.enter_context(self.nc.sbuf_tensor(f"{self.name}_{name}", shape, dt))

    def psum(self, name, shape, dt=F32):
        return self.enter_context(self.nc.psum_tensor(f"{self.name}_{name}", shape, dt))

    def sem(self, name):
        s = self.enter_context(self.nc.semaphore(f"{self.name}_{name}"))
        Phase.used.append(s.num)
        return s


class Own:

    def __init__(self, eng, sem, base=0):
        self.eng, self.sem, self.n, self.base = eng, sem, 0, base

    def did(self, ins):
        ins.then_inc(self.sem, 1)
        self.n += 1
        return self.n

    def wait(self, n=None):
        self.eng.wait_ge(self.sem, self.base + (self.n if n is None else n))


def three_products(nc, out, w_hi, w_lo, x_hi, x_lo, first, last):
    nc.tensor.matmul(out, w_hi, x_hi, start=first, stop=False, skip_group_check=True)
    nc.tensor.matmul(out, w_hi, x_lo, start=False, stop=False, skip_group_check=True)
    return nc.tensor.matmul(out, w_lo, x_hi, start=False, stop=last, skip_group_check=True)


def build(nc, a):
    ctx = ExitStack()
    with ctx:
        def sb(name, shape, dt=F32, c=ctx):
            return c.enter_context(nc.sbuf_tensor(name, shape, dt))

        masks = sb("masks", [P, 4, P])
        small = sb("small", [P, 16 * 5])
        cond = sb("cond", [P, KT])
        resid = sb("resid", [P, TT, D_MODEL])
        modc = sb("modc", [P, 3 * KT])
        row_f = sb("row_f", [P, TT])
        raw = [sb(f"raw{i}", [P, HALF, COLS]) for i in range(2)]
        pool_dmas = [ctx.enter_context(nc.semaphore(f"pool_dma{i}")) for i in range(3)]
        with ExitStack() as first:
            tok = sb("tok", [P, TT, 3 * 1024], c=first)
            with ExitStack() as scans:
                xbc = sb("xbc", [P, CT1, SEQ], c=scans)
                dt_raw = sb("dt_raw", [P, TT, SSM_HEADS], c=scans)
                with ExitStack() as heads:
                    qk = sb("qk", [P, 16, SEQ], c=heads)
                    projections1(nc, a, raw, masks, small, cond, resid, qk, tok, xbc, dt_raw)
                    attention(nc, a, raw, masks, cond, modc, qk, tok, pool_dmas)
                ssd(nc, a, masks, small, tok, xbc, dt_raw)
            output_projection(nc, a, raw, masks, resid, row_f, tok[:, :, 1024:], a["w_out"], False, None)
        with ExitStack() as second:
            z = sb("z", [P, TT, D_Z2], c=second)
            scan = second.enter_context(ExitStack())
            qkvT = sb("qkvT", [P, D_CONV2 // P, SEQ], c=scan)
            ba = sb("ba", [P, TT, 2 * V_HEADS], c=scan)
            hs = second.enter_context(ExitStack())
            h_hi = sb("h_hi", [P, KT, SEQ], F32R, c=hs)
            h_lo = sb("h_lo", [P, KT, SEQ], F32R, c=hs)
            modulate(nc, a, masks, resid, row_f, modc, h_hi, h_lo)
            projections2(nc, a, raw, masks, resid, h_hi, h_lo, qkvT, z, ba)
            hs.close()
            Phase.clear_semaphores(nc)
            gated_deltanet(nc, a, masks, small, resid, raw, qkvT, z, ba)
            scan.close()
            output_projection(nc, a, raw, masks, resid, row_f, z, a["gdn_w_out"], True, modc[:, 2 * KT:])


def conv_buffers(resid):
    spare = resid[:].rearrange("p t d -> p (t d)")
    pre = spare[:, 0:2 * (CONV - 1 + SEQ)].rearrange("p (j t) -> p j t", j=2)
    acc = spare[:, 2048:2048 + 2 * SEQ].rearrange("p (j t) -> p j t", j=2)
    return pre, acc


class ConvStream:

    def __init__(self, nc, sem, pre, acc, cw, banks, dst, bias):
        self.nc, self.pre, self.acc, self.cw, self.banks, self.dst, self.bias = nc, pre, acc, cw, banks, dst, bias
        self.pre_ready = sem("pre_ready")
        self.taps_done = sem("taps_done")
        self.conv_done = sem("conv_done")
        self.tap_step = sem("tap_step")

    def read_and_silu(self, act, b, par, banks_free):
        nc = self.nc
        for pair in range(2):
            tiles = [2 * pair + j for j in range(2)]
            for e in tiles:
                act.wait_ge(self.taps_done, b * 4 + (e + 1))
                nc.scalar.activation(self.pre[:, e % 2, CONV - 1:], self.banks[:, 4 * par + e, :], ACT.Copy)\
                    .then_inc(self.pre_ready, 1)
            if pair:
                act.wait_ge(self.pre_ready, b * 4 + 4)
                act.sem_inc(banks_free, 1)
            for e in tiles:
                act.wait_ge(self.taps_done, b * 4 + (e + 3))
                dst = self.dst[:, bass.ds(b * 4 + e, 1), :].rearrange("p o t -> p (o t)")
                if self.bias:
                    ins = nc.scalar.activation(dst, self.acc[:, e % 2, :], ACT.Silu,
                                               bias=self.cw[:, 4 * b + e, CONV:CONV + 1])
                else:
                    ins = nc.scalar.activation(dst, self.acc[:, e % 2, :], ACT.Silu)
                ins.then_inc(self.conv_done, 1)

    def sum_taps(self, dve, b):
        nc, step = self.nc, 0
        for pair in range(2):
            tiles = [2 * pair + j for j in range(2)]
            step_of = {}
            for k in range(CONV):
                for e in tiles:
                    tap = self.cw[:, bass.ds(b * 4 + e, 1), k:k + 1].rearrange("p o k -> p (o k)")
                    src = self.pre[:, e % 2, k:k + SEQ]
                    acc = self.acc[:, e % 2, :]
                    if k == 0:
                        dve.wait_ge(self.pre_ready, b * 4 + (e + 1))
                        dve.wait_ge(self.conv_done, b * 4 + (e + 1))
                        ins = nc.vector.tensor_scalar(acc, src, tap, None, ALU.mult)
                    else:
                        dve.wait_ge(self.tap_step, b * 12 + step_of[e])
                        ins = nc.vector.scalar_tensor_tensor(out=acc, in0=src, scalar=tap, in1=acc,
                                                             op0=ALU.mult, op1=ALU.add)
                    if k == CONV - 1:
                        ins.then_inc(self.taps_done, 1)
                    else:
                        ins.then_inc(self.tap_step, 1)
                        step += 1
                        step_of[e] = step


class WeightStream:

    def __init__(self, nc, sem, sb, raw, units_before):
        self.nc, self.raw, self.before = nc, raw, units_before
        self.hi = [sb(f"w_hi{i}", [P, HALF, COLS], F32R) for i in range(2)]
        self.lo = [sb(f"w_lo{i}", [P, HALF, COLS], F32R) for i in range(2)]
        self.landed = [sem(f"landed{i}") for i in range(2)]
        self.hi_ready = sem("hi_ready")
        self.lo_ready = sem("lo_ready")
        self.units_used = sem("units_used")

    def load(self, sp, s, n, src):
        sp.wait_ge(self.lo_ready, n * 2 + (s + 1))
        sp.dma_start(self.raw[s][:], src).then_inc(self.landed[s], 16)

    def round(self, act, s, n):
        act.wait_ge(self.landed[s], n * 16 + (16 + 8 * self.before))
        act.wait_ge(self.units_used, n * 2 + (s + 1))
        self.nc.scalar.activation(self.hi[s][:], self.raw[s][:], ACT.Copy).then_inc(self.hi_ready, 1)

    def rest(self, dve, s, n):
        dve.wait_ge(self.hi_ready, n * 2 + (s + 1 + self.before))
        self.nc.vector.tensor_tensor(self.lo[s][:], self.raw[s][:], self.hi[s][:], ALU.subtract)\
            .then_inc(self.lo_ready, 1)

    def wait_unit(self, pe, s, n):
        pe.wait_ge(self.lo_ready, n * 2 + (s + 3))

    def channels(self, pe, n, par, banks, x_hi, x_lo, banks_free):
        pe.wait_ge(banks_free, n + 1)
        for s in range(2):
            self.wait_unit(pe, s, n)
            for e in range(4):
                for kk in range(HALF):
                    k = HALF * s + kk
                    cols = slice(e * P, (e + 1) * P)
                    mm = three_products(self.nc, banks[:, 4 * par + e, :], self.hi[s][:, kk, cols],
                                        self.lo[s][:, kk, cols], x_hi[:, k, :], x_lo[:, k, :], k == 0, k == KT - 1)
            mm.then_inc(self.units_used, 1)

    def tokens(self, pe, n, par, banks, x_hi, x_lo, banks_free):
        pe.wait_ge(banks_free, n + 1)
        for s in range(2):
            self.wait_unit(pe, s, n)
            for t in range(TT):
                for kk in range(HALF):
                    k = HALF * s + kk
                    rows = slice(t * P, (t + 1) * P)
                    mm = three_products(self.nc, banks[:, 4 * par + t, :], x_hi[:, k, rows], x_lo[:, k, rows],
                                        self.hi[s][:, kk, :], self.lo[s][:, kk, :], k == 0, k == KT - 1)
            mm.then_inc(self.units_used, 1)


def projections1(nc, a, raw, masks, small, cond, resid, qk, tok, xbc, dt_raw):
    w_in = a["w_in"][0].rearrange("(k p) c -> p k c", p=P)
    xT = a["xT"].rearrange("(k p) t -> p k t", p=P)
    B_QK, B_V, B_X, B_Z = 4, 2, D_CONV1 // COLS, 4
    N_X = B_QK + B_V
    N_Z = N_X + B_X
    ctx = Phase(nc, "projections1")
    with ctx:
        sb, sem = ctx.sb, ctx.sem
        w = WeightStream(nc, sem, sb, raw, 2)
        x_hi = sb("x_hi", [P, KT, SEQ], F32R)
        x_lo = sb("x_lo", [P, KT, SEQ], F32R)
        wdt = sb("wdt", [P, KT, SSM_HEADS])
        wdt_hi = sb("wdt_hi", [P, KT, SSM_HEADS], F32R)
        wdt_lo = sb("wdt_lo", [P, KT, SSM_HEADS], F32R)
        cw = sb("cw", [P, CT1, CONV + 1])
        pre, acc = conv_buffers(resid)
        ps = ctx.psum("ps1", [P, 8, COLS], F32)
        banks_free = sem("banks_free")
        consts_in = sem("consts_in")
        cond_ok = sem("cond_ok")
        dt_split = sem("dt_split")
        dt_made = sem("dt_made")
        dt_out = sem("dt_out")
        zeroed = sem("zeroed")
        conv = ConvStream(nc, sem, pre, acc, cw, ps, xbc, True)

        block = ctx.enter_context(nc.Block())

        @block.sync
        def _(sp):
            for s in range(2):
                sp.dma_start(raw[s][:], xT[:, HALF * s:HALF * (s + 1), :]).then_inc(w.landed[s], 16)

            def load(n, col):
                for s in range(2):
                    w.load(sp, s, n, w_in[:, HALF * s:HALF * (s + 1), bass.ds(col, COLS)])

            load(0, 0)
            sp.dma_start(masks[:], a["masks"]).then_inc(consts_in, 16)
            sp.dma_start(small[:], a["small"].partition_broadcast(P)).then_inc(consts_in, 16)
            sp.dma_start(cw[:], a["conv1"]).then_inc(consts_in, 16)
            sp.dma_start(cond[:], a["c"]).then_inc(consts_in, 16)
            with nc.allow_non_contiguous_dma(reason="16 columns of w_in"):
                sp.dma_start(wdt[:], w_in[:, :, COL_DT:COL_DT + SSM_HEADS]).then_inc(consts_in, 16)
            with nc.sync.Fori(1, B_QK + B_V) as n:
                load(n, n * COLS)
            with nc.sync.Fori(0, B_X) as j:
                load(j + N_X, j * COLS + COL_XBC)
            with nc.sync.Fori(0, B_Z) as j:
                load(j + N_Z, j * COLS + (B_QK + B_V) * COLS)

        @block.scalar
        def _(act):
            for s in range(2):
                act.wait_ge(w.landed[s], 16)
                nc.scalar.activation(x_hi[:, HALF * s:HALF * (s + 1), :], raw[s][:], ACT.Copy).then_inc(w.hi_ready, 1)
            act.sem_inc(banks_free, 2)

            def round_block(n):
                for s in range(2):
                    w.round(act, s, n)

            def read_out(n, par, dst, func):
                act.wait_ge(w.units_used, n * 2 + 4)
                nc.scalar.activation(dst, ps[:, 4 * par:4 * par + 4, :], func).then_inc(banks_free, 1)

            round_block(0)
            act.wait_ge(consts_in, 80)
            nc.scalar.activation(wdt_hi[:], wdt[:], ACT.Copy).then_inc(dt_split, 1)
            nc.scalar.activation(cond[:], cond[:], ACT.Silu).then_inc(cond_ok, 1)
            with nc.scalar.Fori(0, B_QK // 2) as i:
                for par in range(2):
                    round_block(i * 2 + (par + 1))
                    read_out(i * 2 + par, par, qk[:, bass.ds((i * 2 + par) * 4, 4), :], ACT.Copy)
            for par in range(2):
                round_block(B_QK + par + 1)
                read_out(B_QK + par, par, tok[:, :, par * COLS:(par + 1) * COLS], ACT.Copy)
            act.wait_ge(zeroed, 1)
            act.sem_inc(conv.conv_done, 2)
            for b in range(B_X):
                n = N_X + b
                round_block(n + 1)
                act.wait_ge(w.units_used, 2 * n + 4)
                conv.read_and_silu(act, b, n % 2, banks_free)
            with nc.scalar.Fori(0, B_Z // 2 - 1) as i:
                for j in range(2):
                    round_block(i * 2 + (N_Z + j + 1))
                    read_out(i * 2 + (N_Z + j), (N_Z + j) % 2,
                             tok[:, :, bass.ds(i * (2 * COLS) + (B_V + j) * COLS, COLS)], ACT.Silu)
            round_block(N_Z + B_Z - 1)
            read_out(N_Z + B_Z - 2, (N_Z + B_Z) % 2, tok[:, :, 4 * COLS:5 * COLS], ACT.Silu)
            act.wait_ge(dt_made, 1)
            nc.scalar.activation(dt_raw[:], ps[:, 7, 0:TT * SSM_HEADS].rearrange("p (t h) -> p t h", t=TT), ACT.Copy)\
                .then_inc(dt_out, 1)
            read_out(N_Z + B_Z - 1, (N_Z + B_Z - 1) % 2, tok[:, :, 5 * COLS:6 * COLS], ACT.Silu)

        @block.vector
        def _(dve):
            nc.vector.memset(pre, 0.0).then_inc(zeroed, 1)
            for s in range(2):
                dve.wait_ge(w.hi_ready, s + 1)
                nc.vector.tensor_tensor(x_lo[:, HALF * s:HALF * (s + 1), :], raw[s][:],
                                        x_hi[:, HALF * s:HALF * (s + 1), :], ALU.subtract).then_inc(w.lo_ready, 1)
            for s in range(2):
                w.rest(dve, s, 0)
            dve.wait_ge(dt_split, 1)
            nc.vector.tensor_tensor(wdt_lo[:], wdt[:], wdt_hi[:], ALU.subtract).then_inc(dt_split, 1)
            with nc.vector.Fori(1, N_X + 1) as n:
                for s in range(2):
                    w.rest(dve, s, n)
            dve.sem_inc(conv.taps_done, 2)
            for b in range(B_X):
                for s in range(2):
                    w.rest(dve, s, N_X + 1 + b)
                conv.sum_taps(dve, b)
            with nc.vector.Fori(N_Z + 1, N_Z + B_Z) as n:
                for s in range(2):
                    w.rest(dve, s, n)

        @block.tensor
        def _(pe):
            pe.sem_inc(w.units_used, 2)
            with nc.tensor.Fori(0, B_QK // 2) as i:
                for par in range(2):
                    w.channels(pe, i * 2 + par, par, ps, x_hi, x_lo, banks_free)
            for par in range(2):
                w.tokens(pe, B_QK + par, par, ps, x_hi, x_lo, banks_free)
            for b in range(B_X):
                w.channels(pe, N_X + b, (N_X + b) % 2, ps, x_hi, x_lo, banks_free)
            with nc.tensor.Fori(0, B_Z // 2) as i:
                for j in range(2):
                    w.tokens(pe, i * 2 + (N_Z + j), (N_Z + j) % 2, ps, x_hi, x_lo, banks_free)
            assert (N_Z + B_Z - 2) % 2 == 1
            pe.wait_ge(dt_split, 2)
            pe.wait_ge(banks_free, N_Z + B_Z + 1)
            for t in range(TT):
                for k in range(KT):
                    rows = slice(t * P, (t + 1) * P)
                    mm = three_products(nc, ps[:, 7, t * SSM_HEADS:(t + 1) * SSM_HEADS],
                                        x_hi[:, k, rows], x_lo[:, k, rows], wdt_hi[:, k, :], wdt_lo[:, k, :],
                                        k == 0, k == KT - 1)
            mm.then_inc(dt_made, 1)


def attention(nc, a, raw, masks, cond, modc, qk, tok, pool_dmas):
    ctx = Phase(nc, "attention")
    with ctx:
        sb, sem = ctx.sb, ctx.sem
        ident = masks[:, IDENT, :]
        q_pad = sb("q_pad", [P, 2, 2, SEQ])
        k_st = sb("k_st", [P, 2, SEQ])
        v_st = sb("v_st", [P, 2, TT, P])
        bias = sb("bias", [P, 4, SEQ])
        probs = sb("probs", [P, 4, S_LEN])
        probsT = sb("probsT", [P, 2, S_LEN])
        maxes = sb("maxes", [P, 4, TT])
        negmax = sb("negmax", [P, 4, TT])
        sums = sb("sums", [P, 4, TT])
        recip = sb("recip", [P, 2, TT])
        y_raw = sb("y_raw", [P, 2, TT, HD])
        ps_s = ctx.psum("ps_s", [P, 3 * 512], F32)
        ps_t = ctx.psum("ps_t", [P, 3 * 512], F32)
        ps_o = ctx.psum("ps_o", [P, 2, TT, P], F32)
        zeroed = sem("zeroed")
        qk_in = [sem(f"qk_in{i}") for i in range(2)]
        v_in = [sem(f"v_in{i}") for i in range(2)]
        bias_in = [sem(f"bias_in{i}") for i in range(4)]
        scored = sem("scored")
        biased = sem("biased")
        negmax_ok = sem("negmax_ok")
        exped = sem("exped")
        turned = sem("turned")
        turned_out = sem("turned_out")
        valued = sem("valued")
        recip_ok = sem("recip_ok")
        y_norm = sem("y_norm")
        y_done = sem("y_done")
        gate = sem("gate")
        mod_acc = sb("mod_acc", [P, 3 * D_MODEL])
        ada = [raw[i][:].rearrange("p k c -> p (k c)")[:, 0:MOD_COLS] for i in range(2)]
        mod_b = sb("mod_b", [P, 3 * KT])
        ada_in, mod_b_in = pool_dmas[0:2], pool_dmas[2]
        mod_step = sem("mod_step")
        mod_scaled = sem("mod_scaled")
        mod_gate = sem("mod_gate")
        mod_sum = sem("mod_sum")
        mod_out = sem("mod_out")
        ITER = ATT_HEADS // 4

        block = ctx.enter_context(nc.Block())

        @block.sync
        def _(sp):
            def stage_qk(j, slot):
                sp.dma_start(q_pad[0:64, slot, 0, :], qk[0:64, bass.ds(j, 1), :]).then_inc(qk_in[slot], 16)
                sp.dma_start(q_pad[64:128, slot, 1, :], qk[64:128, bass.ds(j, 1), :]).then_inc(qk_in[slot], 16)
                sp.dma_start(k_st[:, slot, :], qk[:, bass.ds(j + 8, 1), :]).then_inc(qk_in[slot], 16)

            def stage_v(j, slot):
                sp.dma_start(v_st[:, slot, :, :], tok[:, :, bass.ds(j * P, P)]).then_inc(v_in[slot], 16)

            def stage_bias(h, slot):
                sp.dma_start(bias[:, slot, :], a["att_bias"][bass.ds(h, 1)].rearrange("o p c -> p (o c)"))\
                  .then_inc(bias_in[slot], 16)

            sp.wait_ge(zeroed, 1)
            stage_qk(0, 0)
            for h in range(2):
                stage_bias(h, h)
            stage_qk(1, 1)
            for h in range(2, 4):
                stage_bias(h, h)
            for j in range(2):
                stage_v(j, j)
            with nc.sync.Fori(1, ITER) as i:
                for pp in range(2):
                    sp.wait_ge(scored, i * 16 + (8 * pp - 8))
                    stage_qk(i * 2 + pp, pp)
                    sp.wait_ge(biased, i * 16 + (8 * pp - 8))
                    for hh in (2 * pp, 2 * pp + 1):
                        stage_bias(i * 4 + hh, hh)
                    sp.wait_ge(valued, i * 4 + 2 * pp)
                    stage_v(i * 2 + pp, pp)

        def query_tiles():
            return (3, 2, 0, 1)

        @block.tensor
        def _(pe):
            def scores(i, hh, first=False):
                slot = hh // 2
                pe.wait_ge(qk_in[slot], i * 48 + 48)
                if not first:
                    pe.wait_ge(biased, i * 16 + 4 * hh)
                for qt in query_tiles():
                    keys = (qt + 1) * P
                    nc.tensor.matmul(ps_s[:, S_OFF[qt]:S_OFF[qt] + keys],
                                     q_pad[:, slot, hh % 2, qt * P:(qt + 1) * P], k_st[:, slot, 0:keys],
                                     start=True, stop=True).then_inc(scored, 1)

            def turn(i, hh):
                for n, tiles in enumerate(((3,), (2, 0), (1,))):
                    pe.wait_ge(turned_out, i * 12 + (3 * hh + n + 1))
                    for qt in tiles:
                        pe.wait_ge(exped, i * 16 + (4 * hh + 1 + query_tiles().index(qt)))
                        for kt in range(qt + 1):
                            at = S_OFF[qt] + kt * P
                            tr = nc.tensor.transpose(ps_t[:, at:at + P], probs[:, hh, at:at + P], ident)
                    tr.then_inc(turned, 1)

            def values(i, hh):
                pe.wait_ge(v_in[hh // 2], i * 16 + 16)
                pe.wait_ge(y_norm, i * 4 + (hh + 1))
                for n, tiles in enumerate(((3,), (2, 0), (1,))):
                    pe.wait_ge(turned_out, i * 12 + (3 * hh + n + 4))
                    for qt in tiles:
                        for kt in range(qt + 1):
                            at = S_OFF[qt] + kt * P
                            mm = nc.tensor.matmul(ps_o[:, hh % 2, qt, :], probsT[:, hh % 2, at:at + P],
                                                  v_st[:, hh // 2, kt, :], start=(kt == 0), stop=(kt == qt))
                mm.then_inc(valued, 1)

            scores(0, 0, first=True)
            scores(0, 1)

            def heads(i, last):
                for hh in range(4):
                    turn(i, hh)
                    if hh < 2:
                        scores(i, hh + 2)
                    elif not last:
                        scores(i + 1, hh - 2)
                    values(i, hh)

            with nc.tensor.Fori(0, ITER - 1) as i:
                heads(i, False)
            heads(ITER - 1, True)
            pe.wait_ge(mod_step, 2 * KT + 2)
            for j in range(3 * KT):
                where = (ps_s, ps_t)[j // 12][:, (j % 12) * P:(j % 12 + 1) * P]
                mm = nc.tensor.matmul(where, mod_acc[:, j * P:(j + 1) * P], masks[:, ONES, :], start=True, stop=True)
            mm.then_inc(mod_sum, 1)

        @block.gpsimd
        def _(pool):
            for part in range(2):
                nc.gpsimd.memset(mod_acc[:, part * MOD_COLS:(part + 1) * MOD_COLS], 0.0).then_inc(mod_step, 1)
            pool.dma_start(mod_b[:], a["ada_b"]).then_inc(mod_b_in, 16)
            rows = a["ada_w"][0].rearrange("(k p) c -> p k c", p=P)

            def load(k, part):
                pool.dma_start(ada[part], rows[:, bass.ds(k, 1), part * MOD_COLS:(part + 1) * MOD_COLS]
                               .rearrange("p k c -> p (k c)")).then_inc(ada_in[part], 16)

            def add(k, part):
                pool.wait_ge(mod_scaled, k * 2 + (part + 1))
                pool.wait_ge(mod_step, k * 2 + (part + 1))
                acc = mod_acc[:, part * MOD_COLS:(part + 1) * MOD_COLS]
                nc.gpsimd.tensor_tensor(acc, acc, ada[part], ALU.add).then_inc(mod_step, 1)

            for part in range(2):
                load(0, part)
            with nc.gpsimd.Fori(0, KT - 1) as k:
                for part in range(2):
                    add(k, part)
                    pool.wait_ge(mod_step, k * 2 + (part + 3))
                    load(k + 1, part)
            for part in range(2):
                add(KT - 1, part)

        @block.vector
        def _(dve):
            nc.vector.memset(q_pad[:], 0.0).then_inc(zeroed, 1)
            dve.sem_inc(turned_out, 3)
            dve.sem_inc(y_norm, 2)

            def add_bias(i, hh):
                dve.wait_ge(bias_in[hh], i * 16 + 16)
                dve.wait_ge(turned, i * 12 + (3 * hh + 3))
                for n, qt in enumerate(query_tiles()):
                    dve.wait_ge(scored, i * 16 + (4 * hh + (3 if n == 1 else n + 1)))
                    dve.sem_inc(gate, 1)
                    keys = (qt + 1) * P
                    at = S_OFF[qt]
                    nc.vector.tensor_tensor_reduce(
                        probs[:, hh, at:at + keys], ps_s[:, at:at + keys], bias[:, hh, SEQ - keys:SEQ],
                        QK_SCALE, -3e38, ALU.add, ALU.max, maxes[:, hh, qt:qt + 1]).then_inc(biased, 1)
                dve.wait_ge(biased, i * 16 + (4 * hh + 4))
                nc.vector.tensor_scalar(negmax[:, hh, :], maxes[:, hh, :], -1.0, None, ALU.mult).then_inc(negmax_ok, 1)

            def turned_to_sbuf(i, hh):
                for n, (at, size) in enumerate(((512, 512), (0, 512), (1024, 256))):
                    dve.wait_ge(turned, i * 12 + (3 * hh + n + 13))
                    if n == 0:
                        dve.wait_ge(valued, i * 4 + (hh + 1))
                    nc.vector.tensor_copy(probsT[:, hh % 2, at:at + size], ps_t[:, at:at + size])\
                        .then_inc(turned_out, 1)

            def finish(i, hh):
                col = (i * 4 + hh) * HD + 1024
                dve.wait_ge(valued, i * 4 + (hh + 3))
                nc.vector.reciprocal(recip[:, hh % 2, :], sums[:, hh, :]).then_inc(recip_ok, 1)
                dve.wait_ge(recip_ok, i * 4 + (hh + 5))
                half = (hh % 2) * HD
                nc.vector.tensor_tensor(y_raw[:, hh % 2, :, :], ps_o[:, hh % 2, :, half:half + HD],
                                        recip[:, hh % 2, :].unsqueeze(2).broadcast_to([P, TT, HD]),
                                        ALU.mult).then_inc(y_norm, 1)
                dve.wait_ge(y_norm, i * 4 + (hh + 3))
                y = tok[:, :, bass.ds(col, HD)]
                nc.vector.tensor_tensor(y, y_raw[:, hh % 2, :, :], y, ALU.mult).then_inc(y_done, 1)

            add_bias(0, 0)
            add_bias(0, 1)

            def heads(i, last, start=0):
                for hh in range(4):
                    turned_to_sbuf(i, hh)
                    if hh < 2:
                        add_bias(i, hh + 2)
                    elif not last:
                        add_bias(i + 1, hh - 2)
                    finish(i, hh)

            with nc.vector.Fori(0, ITER - 1) as i:
                heads(i, False)
            heads(ITER - 1, True)
            dve.wait_ge(mod_sum, 1)
            dve.wait_ge(mod_b_in, 16)
            for part, where in enumerate((ps_s, ps_t)):
                sums_col = where[:].rearrange("p (j c) -> p j c", c=P)[:, :, 0]
                cols = slice(12 * part, 12 * part + 12)
                nc.vector.tensor_tensor(modc[:, cols], sums_col, mod_b[:, cols], ALU.add).then_inc(mod_out, 1)

        @block.scalar
        def _(act):
            act.sem_inc(turned, 12)
            act.sem_inc(valued, 2)
            act.sem_inc(recip_ok, 4)

            def exponentials(i, hh):
                act.wait_ge(negmax_ok, i * 4 + (hh + 1))
                for n, qt in enumerate(query_tiles()):
                    keys = (qt + 1) * P
                    at = S_OFF[qt]
                    if n == 0:
                        act.wait_ge(recip_ok, i * 4 + (hh + 1))
                    nc.scalar.activation(probs[:, hh, at:at + keys], probs[:, hh, at:at + keys], ACT.Exp,
                                         bias=negmax[:, hh, qt:qt + 1],
                                         accum_out=sums[:, hh, qt:qt + 1]).then_inc(exped, 1)

            with nc.scalar.Fori(0, ITER) as i:
                for hh in range(4):
                    exponentials(i, hh)
                    part, k = hh % 2, i * 2 + hh // 2
                    act.wait_ge(ada_in[part], k * 16 + 16)
                    act.sem_inc(mod_gate, 1)
                    nc.scalar.activation(ada[part], ada[part], ACT.Copy,
                                         scale=cond[:, bass.ds(k, 1)]).then_inc(mod_scaled, 1)


def softplus_head(nc, dve, own, x, ax, raw, bias_row, n):
    own.did(nc.vector.tensor_tensor(x, raw, bias_row, ALU.add))
    own.wait()
    return own.did(nc.vector.scalar_tensor_tensor(out=ax, in0=x, scalar=-1.0, in1=x, op0=ALU.mult, op1=ALU.max))


def softplus_tail(nc, dve, own, dt, x, u, t):
    z, z2, q = t
    own.did(nc.vector.tensor_scalar(q, u, 2.0, None, ALU.add))
    own.wait()
    own.did(nc.vector.reciprocal(z2, q))
    own.wait()
    own.did(nc.vector.tensor_tensor(z, u, z2, ALU.mult))
    own.wait()
    own.did(nc.vector.tensor_tensor(z2, z, z, ALU.mult))
    own.wait()
    series = log1p_series()
    own.did(nc.vector.tensor_scalar(q, z2, series[-1], None, ALU.mult))
    for c in reversed(series[:-1]):
        own.wait()
        own.did(nc.vector.scalar_tensor_tensor(out=q, in0=q, scalar=c, in1=z2, op0=ALU.add, op1=ALU.mult))
    own.wait()
    own.did(nc.vector.scalar_tensor_tensor(out=q, in0=q, scalar=1.0, in1=z, op0=ALU.add, op1=ALU.mult))
    own.wait()
    own.did(nc.vector.tensor_scalar(q, q, 2.0, None, ALU.mult))
    own.wait()
    own.did(nc.vector.scalar_tensor_tensor(out=dt, in0=x, scalar=0.0, in1=q, op0=ALU.max, op1=ALU.add))
    own.wait()


def ssd(nc, a, masks, small, tok, xbc, dt_raw):
    ctx = Phase(nc, "ssd")
    with ctx:
        sb, sem = ctx.sb, ctx.sem
        G, GW = SSM_GROUPS, HPG * HD
        ident, upper, below, ones = (masks[:, m, :] for m in (IDENT, UPPER, BELOW, ONES))
        soft = sb("soft", [P, 6, TT, SSM_HEADS])
        dt = sb("dt", [P, TT, SSM_HEADS])
        a_exp = sb("a_exp", [P, SSM_HEADS])
        adt = sb("adt", [P, TT, SSM_HEADS])
        decays = sb("decays", [P, 3, TT, SSM_HEADS])
        stage = sb("stage", [P, G, 6, P])
        c_st = sb("c_st", [P, G, P])
        steps_in = sb("steps_in", [P, G, HPG, P])
        E = sb("E", [P, G, HPG, P])
        M = sb("M", [P, G, HPG, P])
        cb = sb("cb", [P, G, P])
        xs_tok = sb("xs_tok", [P, G, HPG, HD])
        b_tok = sb("b_tok", [P, G, P])
        xdt = sb("xdt", [P, G, HPG, HD])
        xdte = sb("xdte", [P, G, HPG, HD])
        xskip = sb("xskip", [P, G, HPG, HD])
        state = sb("state", [P, G, HPG, HD])
        y = sb("y", [P, G, HPG, HD])
        ps_x = ctx.psum("ps_x", [P, HPG, HD], F32)
        ps_c = ctx.psum("ps_c", [P, 4, P], F32)
        ps_seg = ctx.psum("ps_seg", [P, HPG, P], F32)
        ps_yd = ctx.psum("ps_yd", [P, HPG, P], F32)
        ps_yo = ctx.psum("ps_yo", [P, HPG, HD], F32)
        ps_st = ctx.psum("ps_st", [P, HPG, HD], F32)
        own_s = sem("own_s")
        abs_ok = sem("abs_ok")
        u_ok = sem("u_ok")
        adt_ok = sem("adt_ok")
        sums_ok = sem("sums_ok")
        decays_ok = sem("decays_ok")
        state_zero = sem("state_zero")
        ab_in = [sem(f"ab_in{g}") for g in range(G)]
        c_in = [sem(f"c_in{g}") for g in range(G)]
        steps_ok = sem("steps_ok")
        xs_turned = sem("xs_turned")
        cb_made = sem("cb_made")
        seg_made = sem("seg_made")
        xs_out = sem("xs_out")
        b_out = sem("b_out")
        e_ok = sem("e_ok")
        cb_ok = sem("cb_ok")
        m_ok = sem("m_ok")
        xdt_ok = sem("xdt_ok")
        xdte_ok = sem("xdte_ok")
        xskip_ok = sem("xskip_ok")
        gate = sem("gate")
        yd_made = sem("yd_made")
        yo_made = sem("yo_made")
        st_made = sem("st_made")
        y_step = sem("y_step")
        st_step = sem("st_step")

        block = ctx.enter_context(nc.Block())

        def head_row(values):
            return values.unsqueeze(2).broadcast_to([P, HPG, HD])

        @block.sync
        def _(sp):
            def stage_ab(c, g):
                at = bass.ds(c * P, P)
                sp.dma_start(stage[:, g, 0:4, :], xbc[:, 4 * g:4 * g + 4, at]).then_inc(ab_in[g], 16)
                sp.dma_start(stage[:, g, 4:6, :], xbc[:, 8 + g:12:2, at]).then_inc(ab_in[g], 16)

            def stage_c(c, g):
                sp.dma_start(c_st[:, g, :], xbc[:, 10 + g, bass.ds(c * P, P)]).then_inc(c_in[g], 16)

            for g in range(G):
                stage_ab(0, g)
                stage_c(0, g)
            with nc.sync.Fori(1, TT) as c:
                for g in range(G):
                    sp.wait_ge(cb_made, c * 2 + (g - 1))
                    stage_ab(c, g)
                    sp.wait_ge(yo_made, c * 2 + (g - 1))
                    stage_c(c, g)

        @block.tensor
        def _(pe):
            pe.wait_ge(adt_ok, 1)
            flat = adt[:].rearrange("p c h -> p (c h)")
            for n, mask in enumerate((upper, below, ones)):
                mm = nc.tensor.matmul(ps_c[:, n, 0:TT * SSM_HEADS], mask, flat, start=True, stop=True)
            mm.then_inc(sums_ok, 1)
            pe.wait_ge(decays_ok, 1)
            pe.sem_inc(st_made, G)
            pe.sem_inc(yd_made, G)
            pe.sem_inc(seg_made, G)

            def ahead(c, g):
                pe.wait_ge(ab_in[g], c * 32 + 32)
                pe.wait_ge(xs_out, c * 2 + (g + 1))
                for t in range(4):
                    tr = nc.tensor.transpose(ps_x[:, 2 * t:2 * t + 2, :].rearrange("p a b -> p (a b)"),
                                             stage[:, g, t, :], ident)
                tr.then_inc(xs_turned, 1)
                pe.wait_ge(b_out, c * 2 + (g + 1))
                pe.wait_ge(cb_ok, c * 2 + (g + 1))
                nc.tensor.transpose(ps_c[:, 0, :], stage[:, g, 4, :], ident)
                nc.tensor.matmul(ps_c[:, 1, :], stage[:, g, 4, :], stage[:, g, 5, :], start=True, stop=True)\
                    .then_inc(cb_made, 1)
                pe.wait_ge(steps_ok, c * 2 + (g + 1))
                pe.wait_ge(e_ok, c * 2 + (g + 1))
                for n in range(2):
                    mm = nc.tensor.matmul(ps_seg[:, 4 * n:4 * n + 4, :].rearrange("p a b -> p (a b)"), below,
                                          steps_in[:, g, 4 * n:4 * n + 4, :].rearrange("p a b -> p (a b)"),
                                          start=True, stop=True)
                mm.then_inc(seg_made, 1)

            def outputs(c, g):
                pe.wait_ge(c_in[g], c * 16 + 16)
                pe.wait_ge(st_step, c * 4 + (2 * g + 2))
                pe.wait_ge(y_step, c * 8 + (4 * g + 5))
                nc.tensor.matmul(ps_yo[:].rearrange("p a b -> p (a b)"), c_st[:, g, :],
                                 state[:, g, :, :].rearrange("p a b -> p (a b)"), start=True, stop=True)\
                    .then_inc(yo_made, 1)
                pe.wait_ge(b_out, c * 2 + (g + 2))
                pe.wait_ge(xdte_ok, c * 2 + (g + 3))
                pe.wait_ge(st_step, c * 4 + (2 * g + 4))
                nc.tensor.matmul(ps_st[:].rearrange("p a b -> p (a b)"), b_tok[:, g, :],
                                 xdte[:, g, :, :].rearrange("p a b -> p (a b)"), start=True, stop=True)\
                    .then_inc(st_made, 1)
                pe.wait_ge(m_ok, c * 2 + (g + 3))
                for h in range(HPG):
                    pair = xdt[:, g, h - h % 2:h - h % 2 + 2, :].rearrange("p a b -> p (a b)")
                    mm = nc.tensor.matmul(ps_yd[:, h, :], M[:, g, h, :], pair, start=True, stop=True)
                mm.then_inc(yd_made, 1)

            ahead(0, 0)
            with nc.tensor.Fori(0, TT - 1) as c:
                ahead(c, 1)
                outputs(c, 0)
                ahead(c + 1, 0)
                outputs(c, 1)
            ahead(TT - 1, 1)
            outputs(TT - 1, 0)
            outputs(TT - 1, 1)

        @block.scalar
        def _(act):
            act.wait_ge(abs_ok, 1)
            nc.scalar.activation(soft[:, 2], soft[:, 1], ACT.Exp, scale=-1.0).then_inc(u_ok, 1)
            nc.scalar.activation(a_exp[:], small[:, SSM_HEADS:2 * SSM_HEADS], ACT.Exp).then_inc(u_ok, 1)
            act.wait_ge(sums_ok, 1)
            nc.scalar.activation(decays[:].rearrange("p n c h -> p n (c h)"), ps_c[:, 0:3, 0:TT * SSM_HEADS],
                                 ACT.Exp).then_inc(decays_ok, 1)
            act.wait_ge(decays_ok, 1)
            act.sem_inc(xs_out, 1)
            act.sem_inc(b_out, 1)
            act.sem_inc(e_ok, 1)
            with nc.scalar.Fori(0, TT) as c:
                for g in range(G):
                    act.wait_ge(xs_turned, c * 2 + (g + 1))
                    act.wait_ge(xskip_ok, c * 2 + (g + 1))
                    act.wait_ge(xdt_ok, c * 2 + (g + 1))
                    nc.scalar.activation(xs_tok[:, g], ps_x[:], ACT.Copy).then_inc(xs_out, 1)
                    act.wait_ge(cb_made, c * 2 + (g + 1))
                    act.wait_ge(st_made, c * 2 + (g + 1))
                    nc.scalar.activation(b_tok[:, g, :], ps_c[:, 0, :], ACT.Copy).then_inc(b_out, 1)
                    act.wait_ge(seg_made, c * 2 + (g + 3))
                    act.wait_ge(m_ok, c * 2 + (g + 1))
                    nc.scalar.activation(E[:, g], ps_seg[:], ACT.Exp).then_inc(e_ok, 1)

        @block.vector
        def _(dve):
            own = Own(dve, own_s)
            own.did(nc.vector.memset(state[:], 0.0))
            softplus_head(nc, dve, own, soft[:, 0], soft[:, 1], dt_raw[:],
                          small[:, 0:SSM_HEADS].unsqueeze(1).broadcast_to([P, TT, SSM_HEADS]), TT)
            own.wait()
            dve.sem_inc(abs_ok, 1)
            dve.wait_ge(u_ok, 2)
            softplus_tail(nc, dve, own, dt[:], soft[:, 0], soft[:, 2], (soft[:, 3], soft[:, 4], soft[:, 5]))
            nc.vector.scalar_tensor_tensor(out=adt[:], in0=dt[:], scalar=-1.0,
                                           in1=a_exp[:].unsqueeze(1).broadcast_to([P, TT, SSM_HEADS]),
                                           op0=ALU.mult, op1=ALU.mult).then_inc(adt_ok, 1)
            dve.sem_inc(cb_ok, 1)
            dve.sem_inc(m_ok, G)
            dve.sem_inc(xdt_ok, G)
            dve.sem_inc(y_step, 7)
            dve.sem_inc(st_step, 4)
            dve.wait_ge(decays_ok, 1)

            def chunk_heads(values, c, g):
                return values[:, bass.ds(c, 1), g * HPG:(g + 1) * HPG].rearrange("p c h -> p (c h)")

            def ahead(c, g):
                dve.wait_ge(xs_out, c * 2 + (g + 2))
                dve.wait_ge(yd_made, c * 2 + (g + 1))
                dve.wait_ge(xdte_ok, c * 2 + (g + 1))
                nc.vector.tensor_tensor(xdt[:, g], xs_tok[:, g], head_row(chunk_heads(dt, c, g)), ALU.mult)\
                    .then_inc(xdt_ok, 1)
                dve.wait_ge(b_out, c * 2 + (g + 2))
                dve.wait_ge(m_ok, c * 2 + (g + 1))
                nc.vector.tensor_tensor(cb[:, g, :], ps_c[:, 1, :], upper, ALU.mult).then_inc(cb_ok, 1)
                dve.wait_ge(cb_ok, c * 2 + (g + 2))
                dve.wait_ge(e_ok, c * 2 + (g + 2))
                nc.vector.tensor_tensor(M[:, g], E[:, g], cb[:, g, :].unsqueeze(1).broadcast_to([P, HPG, P]),
                                        ALU.mult).then_inc(m_ok, 1)

            def outputs(c, g):
                dve.wait_ge(yo_made, c * 2 + (g + 1))
                nc.vector.tensor_tensor(y[:, g], ps_yo[:], head_row(chunk_heads(decays[:, 0], c, g)), ALU.mult)\
                    .then_inc(y_step, 1)
                nc.vector.tensor_tensor(state[:, g], state[:, g], head_row(chunk_heads(decays[:, 2], c, g)), ALU.mult)\
                    .then_inc(st_step, 1)
                dve.wait_ge(yd_made, c * 2 + (g + 3))
                dve.wait_ge(y_step, c * 8 + (4 * g + 8))
                own_half = ps_yd[:].rearrange("p h c -> p (h c)").rearrange("p (q j c) -> p q j c", j=4, c=HD)[:, :, 0:4:3, :]
                nc.vector.tensor_tensor(y[:, g].rearrange("p (q j) c -> p q j c", j=2),
                                        own_half, y[:, g].rearrange("p (q j) c -> p q j c", j=2), ALU.add)\
                    .then_inc(y_step, 1)
                dve.wait_ge(st_made, c * 2 + (g + 3))
                dve.wait_ge(st_step, c * 4 + (2 * g + 5))
                nc.vector.tensor_tensor(state[:, g], ps_st[:], state[:, g], ALU.add).then_inc(st_step, 1)
                dve.wait_ge(xskip_ok, c * 2 + (g + 3))
                dve.wait_ge(y_step, c * 8 + (4 * g + 9))
                nc.vector.tensor_tensor(y[:, g], y[:, g], xskip[:, g], ALU.add).then_inc(y_step, 1)
                z = tok[:, bass.ds(c, 1), 2048 + g * GW:2048 + (g + 1) * GW].rearrange("p c (h e) -> p (c h) e", h=HPG)
                dve.wait_ge(y_step, c * 8 + (4 * g + 10))
                nc.vector.tensor_tensor(z, y[:, g], z, ALU.mult).then_inc(y_step, 1)

            ahead(0, 0)
            with nc.vector.Fori(0, TT - 1) as c:
                ahead(c, 1)
                outputs(c, 0)
                ahead(c + 1, 0)
                outputs(c, 1)
            ahead(TT - 1, 1)
            outputs(TT - 1, 0)
            outputs(TT - 1, 1)

        @block.gpsimd
        def _(pool):
            pool.sem_inc(xskip_ok, G)
            pool.sem_inc(xdte_ok, G)
            pool.wait_ge(decays_ok, 1)

            def step(c, g):
                heads = slice(g * HPG, (g + 1) * HPG)
                pool.wait_ge(seg_made, c * 2 + (g + 1))
                pool.sem_inc(gate, 1)
                a_row = adt[:, bass.ds(c, 1), heads].rearrange("p c h -> p (c h)")
                nc.gpsimd.tensor_tensor(steps_in[:, g], upper.unsqueeze(1).broadcast_to([P, HPG, P]),
                                        a_row.unsqueeze(2).broadcast_to([P, HPG, P]), ALU.mult)\
                    .then_inc(steps_ok, 1)
                pool.wait_ge(xs_out, c * 2 + (g + 2))
                pool.wait_ge(y_step, c * 8 + (4 * g + 2))
                pool.sem_inc(gate, 1)
                nc.gpsimd.tensor_tensor(xskip[:, g], xs_tok[:, g], head_row(small[:, 2 * SSM_HEADS:3 * SSM_HEADS][:, heads]),
                                        ALU.mult).then_inc(xskip_ok, 1)
                pool.wait_ge(xdt_ok, c * 2 + (g + 3))
                pool.wait_ge(st_made, c * 2 + (g + 1))
                pool.sem_inc(gate, 1)
                e_row = decays[:, 1, bass.ds(c, 1), heads].rearrange("p c h -> p (c h)")
                nc.gpsimd.tensor_tensor(xdte[:, g], xdt[:, g], head_row(e_row), ALU.mult).then_inc(xdte_ok, 1)

            with nc.gpsimd.Fori(0, TT) as c:
                for g in range(G):
                    step(c, g)


def output_projection(nc, a, raw, masks, resid, row_f, tokens, w_out, second, gate_col):
    w_v = w_out[0].rearrange("(k p) c -> p k c", p=P)
    MT = 16
    UNITS = MT // HALF
    NH = D_MODEL // COLS
    ctx = Phase(nc, "output2" if second else "output1")
    with ctx:
        sb, sem = ctx.sb, ctx.sem
        ident = masks[:, IDENT, :]
        w = WeightStream(nc, sem, sb, raw, 0)
        m_hi = sb("m_hi", [P, MT, SEQ], F32R)
        m_lo = sb("m_lo", [P, MT, SEQ], F32R)
        m_g = sb("m_g", [P, MT])
        row_g = sb("row_g", [P, D_MODEL])
        row_b = sb("row_b", [P, D_MODEL])
        junk = sb("junk", [P, D_MODEL])
        stats = sb("stats", [P, TT, 2, 6])
        mean_var = sb("mean_var", [P, TT, 2])
        sumsq = sb("sumsq", [P, 2 * TT])
        ln_f = sb("ln_f", [P, TT])
        junk2 = sb("junk2", [P, D_MODEL])
        half_neg = sb("half_neg", [P, 2 * TT])
        ps_m = ctx.psum("ps_m", [P, 4, COLS], F32)
        ps_t = ctx.psum("ps_t", [P, 4, COLS], F32)
        consts_in = sem("consts_in")
        x_in = sem("x_in")
        sum_ok = sem("sum_ok")
        pool_step = sem("pool_step")
        factor_ok = sem("factor_ok")
        scaled = sem("scaled")
        turned = sem("turned")
        m_hi_ok = sem("m_hi_ok")
        m_lo_ok = sem("m_lo_ok")
        acc_made = sem("acc_made")
        added = sem("added")
        own_s = sem("own_s")
        gate_row = sem("gate_row")
        last_ok = sem("last_ok")
        out_s = sem("out_s")

        block = ctx.enter_context(nc.Block())

        @block.sync
        def _(sp):
            def load_unit(u):
                half, j = divmod(u, UNITS)
                src = w_v[:, HALF * j:HALF * (j + 1), half * COLS:(half + 1) * COLS]
                if u < 2:
                    sp.dma_start(raw[u][:], src).then_inc(w.landed[u], 16)
                else:
                    w.load(sp, u % 2, u // 2 - 1, src)

            for u in range(2):
                load_unit(u)
            if second:
                sp.dma_start(resid[:], a["x1"].rearrange("(t p) d -> p t d", p=P)).then_inc(x_in, 16)
                sp.dma_start(m_g[:], a["gdn_g"]).then_inc(consts_in, 16)
                sp.dma_start(row_g[:], a["final_g"].partition_broadcast(P)).then_inc(consts_in, 16)
            else:
                sp.dma_start(resid[:], a["x"].rearrange("(t p) d -> p t d", p=P)).then_inc(x_in, 16)
                sp.dma_start(m_g[:], a["mix_g"]).then_inc(consts_in, 16)
                sp.dma_start(row_g[:], a["ln_g"].partition_broadcast(P)).then_inc(consts_in, 16)
                sp.dma_start(row_b[:], a["ln_b"].partition_broadcast(P)).then_inc(consts_in, 16)
            for u in range(2, NH * UNITS):
                load_unit(u)
            if second:
                for t in range(TT):
                    sp.wait_ge(last_ok, t + 1)
                    sp.dma_start(a["out"].rearrange("(t p) d -> p t d", p=P)[:, t, :], resid[:, t, :]).then_inc(out_s, 16)
                sp.wait_ge(out_s, 16 * TT)

        TURNS = (8, 4, 4)

        @block.tensor
        def _(pe):
            pe.sem_inc(w.units_used, 2)
            done = 0

            def turn(n):
                nonlocal done
                for e in range(done, done + n):
                    if not second:
                        pe.wait_ge(scaled, 4 if e < MT // 2 else 8)
                    if e >= 4:
                        pe.wait_ge(m_lo_ok, e - 3)
                    for t in range(TT):
                        tr = nc.tensor.transpose(ps_t[:, e % 4, t * P:(t + 1) * P], tokens[:, t, e * P:(e + 1) * P], ident)
                    tr.then_inc(turned, 1)
                done += n

            if second:
                pe.wait_ge(gate_row, 1)
                for j in range(2):
                    mm = nc.tensor.matmul(ps_m[:, j, :], masks[:, ONES, :], junk[:, j * COLS:(j + 1) * COLS],
                                          start=True, stop=True)
                mm.then_inc(gate_row, 1)
            turn(TURNS[0])
            if second:
                pe.wait_ge(gate_row, 3)
            for half in range(NH):
                for j in range(UNITS):
                    u = half * UNITS + j
                    s = u % 2
                    pe.wait_ge(w.lo_ready, u + 1)
                    if half == 0:
                        pe.wait_ge(m_lo_ok, HALF * (j + 1))
                    for t in range(TT):
                        if half and j == 0:
                            pe.wait_ge(added, (half - 1) * TT + t + 1)
                        for kk in range(HALF):
                            k = HALF * j + kk
                            rows = slice(t * P, (t + 1) * P)
                            mm = three_products(nc, ps_m[:, t, :], m_hi[:, k, rows], m_lo[:, k, rows],
                                                w.hi[s][:, kk, :], w.lo[s][:, kk, :], k == 0, k == MT - 1)
                        if j == UNITS - 1 and t < TT - 1:
                            mm.then_inc(acc_made, 1)
                    mm.then_inc(w.units_used, 1)
                    if half == 0 and j < 2:
                        turn(TURNS[j + 1])

        @block.scalar
        def _(act):
            def round_unit(u):
                act.wait_ge(w.landed[u % 2], 16 * (u // 2 + 1))
                act.wait_ge(w.units_used, u + 1)
                nc.scalar.activation(w.hi[u % 2][:], raw[u % 2][:], ACT.Copy).then_inc(w.hi_ready, 1)

            def high(e):
                act.wait_ge(turned, e + 1)
                nc.scalar.activation(m_hi[:, e, :], ps_t[:, e % 4, :], ACT.Identity, scale=m_g[:, e:e + 1]).then_inc(m_hi_ok, 1)

            if not second:
                for t in range(TT):
                    if t:
                        act.wait_ge(sum_ok, t)
                    nc.scalar.activation(junk[:], tokens[:, t, 0:D_MODEL], ACT.Square,
                                         accum_out=sumsq[:, t:t + 1]).then_inc(sum_ok, 1)
            round_unit(0)
            round_unit(1)
            act.wait_ge(consts_in, 32 if second else 48)
            for e in range(12):
                high(e)
            round_unit(2)
            for e in range(12, MT):
                high(e)
            for u in range(3, NH * UNITS):
                round_unit(u)
            for t in range(TT):
                act.wait_ge(added, (1 if second else NH) * TT + t + 1)
                nc.scalar.activation(junk[:], resid[:, t, :], ACT.Square, accum_out=row_f[:, t:t + 1])\
                    .then_inc(sum_ok, 1)
                act.wait_ge(sum_ok, (0 if second else TT) + t + 1)

        @block.gpsimd
        def _(pool):
            nc.gpsimd.memset(half_neg[:], -0.5).then_inc(pool_step, 1)
            steps = 1

            def rsqrt(values, scale, eps):
                nonlocal steps
                pool.wait_ge(pool_step, steps)
                nc.gpsimd.tensor_scalar(values, values, scale, eps, ALU.mult, ALU.add).then_inc(pool_step, 1)
                steps += 1
                pool.wait_ge(pool_step, steps)
                nc.gpsimd.tensor_tensor(values, values, half_neg[:, 0:values.shape[-1]], ALU.pow).then_inc(factor_ok, 1)

            if not second:
                pool.wait_ge(sum_ok, TT)
                pool.wait_ge(own_s, TT)
                rsqrt(sumsq[:], 1.0 / D_MODEL, EPS1)
                pool.wait_ge(last_ok, 1)
                nc.gpsimd.tensor_copy(ln_f[:], mean_var[:, :, 1]).then_inc(pool_step, 1)
                steps += 1
                rsqrt(ln_f[:], 1.0, EPS1)
            pool.wait_ge(sum_ok, TT if second else 2 * TT)
            rsqrt(row_f[:], 1.0 / D_MODEL, EPS2)

        @block.vector
        def _(dve):
            own = Own(dve, own_s)

            def rest(u):
                dve.wait_ge(w.hi_ready, u + 1)
                nc.vector.tensor_tensor(w.lo[u % 2][:], raw[u % 2][:], w.hi[u % 2][:], ALU.subtract)\
                    .then_inc(w.lo_ready, 1)

            def low(e):
                dve.wait_ge(m_hi_ok, e + 1)
                nc.vector.scalar_tensor_tensor(out=m_lo[:, e, :], in0=ps_t[:, e % 4, :], scalar=m_g[:, e:e + 1],
                                               in1=m_hi[:, e, :], op0=ALU.mult, op1=ALU.subtract).then_inc(m_lo_ok, 1)

            def wait_products(half, t):
                if t < TT - 1:
                    dve.wait_ge(acc_made, (TT - 1) * half + t + 1)
                else:
                    dve.wait_ge(w.units_used, UNITS * (half + 1) + 2)

            if second:
                junk_v = junk[:].rearrange("p (j c) -> p j c", c=P)
                nc.vector.tensor_tensor(junk_v, ident.unsqueeze(1).broadcast_to([P, KT, P]),
                                        gate_col.unsqueeze(2).broadcast_to([P, KT, P]), ALU.mult).then_inc(gate_row, 1)
                dve.wait_ge(gate_row, 2)
                nc.vector.tensor_copy(row_b[:], ps_m[:, 0:2, :].rearrange("p a b -> p (a b)")).then_inc(gate_row, 1)
                dve.wait_ge(gate_row, 3)
            else:
                for t in range(TT):
                    own.did(nc.vector.tensor_tensor_reduce(junk2[:], tokens[:, t, D_MODEL:], tokens[:, t, D_MODEL:],
                                                           1.0, 0.0, ALU.mult, ALU.add, sumsq[:, TT + t:TT + t + 1]))
                    own.wait()
                dve.wait_ge(factor_ok, 1)
                for half in range(2):
                    for t in range(TT):
                        rows = tokens[:, t, half * D_MODEL:(half + 1) * D_MODEL]
                        nc.vector.tensor_scalar(rows, rows, sumsq[:, half * TT + t:half * TT + t + 1], None,
                                                ALU.mult).then_inc(scaled, 1)
            def residual(half):
                cols = slice(half * COLS, (half + 1) * COLS)
                for t in range(TT):
                    wait_products(half, t)
                    x = resid[:, t, cols]
                    if second:
                        own.did(nc.vector.tensor_tensor(junk2[:, (t % 2) * COLS:(t % 2 + 1) * COLS], ps_m[:, t, :],
                                                        row_b[:, cols], ALU.mult))
                        own.wait()
                        nc.vector.tensor_tensor(x, x, junk2[:, (t % 2) * COLS:(t % 2 + 1) * COLS], ALU.add)\
                            .then_inc(added, 1)
                    else:
                        nc.vector.scalar_tensor_tensor(out=x, in0=x, scalar=ALPHA, in1=ps_m[:, t, :],
                                                       op0=ALU.mult, op1=ALU.add).then_inc(added, 1)
                if not second:
                    for t in range(TT):
                        dve.wait_ge(added, half * TT + t + 1)
                        own.did(nc.vector.bn_stats(stats[:, t, half, :], resid[:, t, cols]))

            rest(0)
            rest(1)
            for e in range(12):
                low(e)
            rest(2)
            for e in range(12, MT):
                low(e)
            dve.wait_ge(x_in, 16)
            for u in range(3, NH * UNITS):
                rest(u)
                if u == UNITS:
                    residual(0)
            residual(1)
            if second:
                dve.wait_ge(factor_ok, 1)
                for t in range(TT):
                    nc.vector.scalar_tensor_tensor(out=resid[:, t, :], in0=resid[:, t, :], scalar=row_f[:, t:t + 1],
                                                   in1=row_g[:], op0=ALU.mult, op1=ALU.mult).then_inc(last_ok, 1)
            else:
                own.wait()
                for t in range(TT):
                    own.did(nc.vector.bn_aggr(mean_var[:, t, :], stats[:, t, :, :].rearrange("p a b -> p (a b)")))
                own.wait()
                dve.sem_inc(last_ok, 1)
                for t in range(TT):
                    own.did(nc.vector.scalar_tensor_tensor(out=resid[:, t, :], in0=resid[:, t, :],
                                                           scalar=mean_var[:, t, 0:1], in1=row_g[:],
                                                           op0=ALU.subtract, op1=ALU.mult))
                dve.wait_ge(factor_ok, 2)
                for t in range(TT):
                    own.wait(own.n - TT + 1 + t)
                    nc.vector.scalar_tensor_tensor(out=resid[:, t, :], in0=resid[:, t, :], scalar=ln_f[:, t:t + 1],
                                                   in1=row_b[:], op0=ALU.mult, op1=ALU.add).then_inc(added, 1)


def projections2(nc, a, raw, masks, resid, h_hi, h_lo, qkvT, z, ba):
    w_in = a["gdn_w_in"][0].rearrange("(k p) c -> p k c", p=P)
    B_CONV, B_Z, N_BA = D_CONV2 // COLS, D_Z2 // COLS, 2 * V_HEADS
    ctx = Phase(nc, "project2")
    with ctx:
        sb, sem = ctx.sb, ctx.sem
        w = WeightStream(nc, sem, sb, raw, 0)
        wba = sb("wba", [P, KT, N_BA])
        wba_hi = sb("wba_hi", [P, KT, N_BA], F32R)
        wba_lo = sb("wba_lo", [P, KT, N_BA], F32R)
        ba_rows = sb("ba_rows", [N_BA, SEQ])
        cw = sb("cw", [P, D_CONV2 // P, CONV])
        pre, acc = conv_buffers(resid)
        ps = ctx.psum("ps", [P, 8, COLS])
        banks_free = sem("banks_free")
        wba_in = sem("wba_in")
        cw_in = sem("cw_in")
        ba_split = sem("ba_split")
        ba_made = sem("ba_made")
        ba_out = sem("ba_out")
        zeroed = sem("zeroed")
        conv = ConvStream(nc, sem, pre, acc, cw, ps, qkvT, False)
        block = ctx.enter_context(nc.Block())

        @block.sync
        def _(sp):
            with nc.allow_non_contiguous_dma(reason="32 columns of w_in"):
                sp.dma_start(wba[:], w_in[:, :, D_CONV2 + D_Z2:]).then_inc(wba_in, 16)

            def load(n):
                for s in range(2):
                    w.load(sp, s, n, w_in[:, HALF * s:HALF * (s + 1), bass.ds(n * COLS, COLS)])

            load(0)
            sp.dma_start(cw[:], a["conv2"]).then_inc(cw_in, 16)
            with nc.sync.Fori(1, B_CONV + B_Z) as n:
                load(n)

        @block.scalar
        def _(act):
            act.wait_ge(wba_in, 16)
            nc.scalar.activation(wba_hi[:], wba[:], ACT.Copy).then_inc(ba_split, 1)
            w.round(act, 0, 0)
            act.wait_ge(ba_made, 1)
            nc.scalar.activation(ba_rows[:], ps[0:N_BA, 7, :], ACT.Copy).then_inc(ba_out, 1)
            w.round(act, 1, 0)
            act.wait_ge(ba_made, 2)
            nc.scalar.activation(ba[:], ps[:, 6, 0:TT * N_BA].rearrange("p (t h) -> p t h", t=TT), ACT.Copy)\
                .then_inc(ba_out, 1)
            act.wait_ge(ba_out, 2)
            act.sem_inc(banks_free, 1)
            act.wait_ge(cw_in, 16)
            act.wait_ge(zeroed, 1)
            act.sem_inc(conv.conv_done, 2)
            with nc.scalar.Fori(0, B_CONV // 2) as i:
                for par in range(2):
                    b = i * 2 + par
                    for s in range(2):
                        w.round(act, s, b + 1)
                    act.wait_ge(w.units_used, b * 2 + 4)
                    conv.read_and_silu(act, b, par, banks_free)

            def read_z(j, par):
                act.wait_ge(w.units_used, j * 2 + (2 * B_CONV + 4))
                nc.scalar.activation(z[:, :, bass.ds(j * COLS, COLS)], ps[:, 4 * par:4 * par + 4, :], ACT.Silu)\
                    .then_inc(banks_free, 1)

            for j in range(B_Z):
                if j + 1 < B_Z:
                    for s in range(2):
                        w.round(act, s, B_CONV + j + 1)
                read_z(j, j % 2)

        @block.vector
        def _(dve):
            nc.vector.memset(pre, 0.0).then_inc(zeroed, 1)
            dve.sem_inc(w.lo_ready, 2)
            dve.wait_ge(ba_split, 1)
            nc.vector.tensor_tensor(wba_lo[:], wba[:], wba_hi[:], ALU.subtract).then_inc(ba_split, 1)
            for s in range(2):
                w.rest(dve, s, 0)
            dve.sem_inc(conv.taps_done, 2)
            dve.wait_ge(cw_in, 16)
            with nc.vector.Fori(0, B_CONV) as b:
                for s in range(2):
                    w.rest(dve, s, b + 1)
                conv.sum_taps(dve, b)
            with nc.vector.Fori(B_CONV + 1, B_CONV + B_Z) as n:
                for s in range(2):
                    w.rest(dve, s, n)

        @block.tensor
        def _(pe):
            pe.sem_inc(w.units_used, 2)
            pe.sem_inc(banks_free, 1)
            pe.wait_ge(ba_split, 2)
            for k in range(KT):
                mm = three_products(nc, ps[0:N_BA, 7, :], wba_hi[:, k, :], wba_lo[:, k, :], h_hi[:, k, :],
                                    h_lo[:, k, :], k == 0, k == KT - 1)
            mm.then_inc(ba_made, 1)
            pe.wait_ge(ba_out, 1)
            for t in range(TT):
                tr = nc.tensor.transpose(ps[:, 6, t * N_BA:(t + 1) * N_BA], ba_rows[:, t * P:(t + 1) * P],
                                         masks[0:N_BA, IDENT, 0:N_BA])
            tr.then_inc(ba_made, 1)
            with nc.tensor.Fori(0, B_CONV // 2) as i:
                for par in range(2):
                    w.channels(pe, i * 2 + par, par, ps, h_hi, h_lo, banks_free)
            with nc.tensor.Fori(0, B_Z // 2) as i:
                for par in range(2):
                    w.tokens(pe, i * 2 + (B_CONV + par), par, ps, h_hi, h_lo, banks_free)


def gated_deltanet(nc, a, masks, small, resid, raw, qkvT, z, ba):
    ctx = Phase(nc, "gdn")
    with ctx:
        sb, sem = ctx.sb, ctx.sem
        NB, HB = 2, 4
        ident, upper, below, ones = (masks[:, m, :] for m in (IDENT, UPPER, BELOW, ONES))
        flat = lambda t: t.rearrange("p a b -> p (a b)")
        masks2 = sb("masks2", [P, 5, P])
        strict, block32 = masks2[:, 0, :], masks2[:, 1, :]
        soft = sb("soft", [P, 6, TT, V_HEADS])
        beta = sb("beta", [P, TT, V_HEADS])
        g = sb("g", [P, TT, V_HEADS])
        a_exp = sb("a_exp", [P, V_HEADS])
        decays = sb("decays", [P, 3, TT, V_HEADS])
        dsel = sb("dsel", [P, 3, 2 * HB, TT])
        gsel = sb("gsel", [P, 2 * HB, TT])
        bsel = sb("bsel", [P, 2 * HB, TT])
        st = sb("st", [P, 2, 2, SEQ])
        C = resid[:].rearrange("p t (m c) -> p (t m) c", c=P)
        PT = sb("PT", [P, 8 * HB, P])
        ktok = sb("ktok", [P, HB, TT, P])
        ssq = sb("ssq", [P, HB, TT])
        ssk = sb("ssk", [P, HB, TT])
        kss = sb("kss", [P, HB, TT])
        r2 = sb("r2", [P, HB, TT])
        qe = sb("qe", [P, HB, TT])
        rinv = sb("rinv", [P, HB, TT])
        nbp = sb("nbp", [P, HB, 2, TT])
        sign = sb("sign", [P, TT])
        wsc = sb("wsc", [P, HB, 2, TT])
        Uc = sb("Uc", [P, 8 * HB, 32])
        Tc = sb("Tc", [P, 8 * HB, 32])
        tmp = sb("tmp", [P, 2 * 64])
        half = sb("half", [P, 2, HB * TT])
        vst = sb("vst", [P, 2, SEQ])
        R = sb("R", [P, 2, P])
        w_sb = sb("w_sb", [P, 2, P])
        we = sb("we", [P, 2, P])
        qt = sb("qt", [P, 2, P])
        S = sb("S", [P, 2, P])
        junk = sb("junk", [P, 2, P])
        sums = sb("sums", [P, 2, 2, TT])
        ms = sb("ms", [P, 2, TT])
        rs = sb("rs", [P, 2, 2, TT])
        space_u = sb("space_u", [P, 2, 8, P])
        space_t = sb("space_t", [P, 2, 1056])
        U = [space_u[:, s] for s in range(2)]
        KKm = space_u[:, 0, 0:4]
        KQm = space_u[:, 0, 4:8]
        Cc = flat(space_u[:, 1]).rearrange("p (m c) -> p m c", c=32)
        T, V = (space_t[:, s, 0:1024].rearrange("p (m c) -> p m c", c=P) for s in range(2))
        Cf, Uf = space_t[:, 0], space_t[:, 1]
        O = [flat(raw[0][:])[:, s * 1024:(s + 1) * 1024].rearrange("p (h c e) -> p h c e", h=2, c=TT) for s in range(2)]
        E, steps = (flat(raw[0][:])[:, s * 1024:(s + 1) * 1024].rearrange("p (m c) -> p m c", c=P) for s in range(2))
        vr = [flat(raw[1][:])[:, s * 1024:(s + 1) * 1024].rearrange("p (h c e) -> p h c e", h=2, c=TT) for s in range(2)]
        psA = ctx.psum("psA", [P, 2, COLS])
        psZ = ctx.psum("psZ", [P, 2, COLS])
        psK = ctx.psum("psK", [P, 4, P])
        psO = ctx.psum("psO", [P, 4, P])
        psW = ctx.psum("psW", [P, 4, P])

        consts_in = sem("consts_in")
        own_p = sem("own_p")
        abs_ok, u_ok, g_ok, sums_ok, decays_ok = (sem(n) for n in ("abs_ok", "u_ok", "g_ok", "sums_ok", "decays_ok"))
        own_s = sem("own_s")
        pool_s = sem("pool_s")
        sel_ok = sem("sel_ok")
        st_in = [sem(f"st_in{i}") for i in range(2)]
        turned = sem("turned")
        sq_ok = sem("sq_ok")
        tok_out = sem("tok_out")
        kk_made = sem("kk_made")
        kk_out = sem("kk_out")
        steps_ok = sem("steps_ok")
        seg_made = sem("seg_made")
        e_ok = sem("e_ok")
        c_ok = sem("c_ok")
        pt_ok = sem("pt_ok")
        cc_ok = sem("cc_ok")
        kss_ok = sem("kss_ok")
        rinv_ok = sem("rinv_ok")
        scales_ok = sem("scales_ok")
        eye_ok = sem("eye_ok")
        uc_ok = sem("uc_ok")
        vst_in = sem("vst_in")
        vt_made = sem("vt_made")
        vr_ok = sem("vr_ok")
        tx_ok = sem("tx_ok")
        ux_ok = sem("ux_ok")
        v_made, v_out, z_made, u_ok2 = (sem(n) for n in ("v_made", "v_out", "z_made", "u_ok2"))
        t_made, t_out = sem("t_made"), sem("t_out")
        ks_made, qs_made, ds_made = sem("ks_made"), sem("qs_made"), sem("ds_made")
        r_ok, we_ok, qt_ok = sem("r_ok"), sem("we_ok"), sem("qt_ok")
        w_made, w_ok, o_made, o_ok = (sem(n) for n in ("w_made", "w_ok", "o_made", "o_ok"))
        s_ok = sem("s_ok")
        osq_ok = sem("osq_ok")
        rs_ok = sem("rs_ok")
        gate, gate_v = sem("gate"), sem("gate_v")
        z_ok = sem("z_ok")
        S_COUNT = (0, 1, 3, 5)

        block = ctx.enter_context(nc.Block())

        def at(i, per_head, j, k):
            return i * (HB * per_head) + (per_head * j + k)

        def doubling_parts(j):
            parts = []
            for lv in range(3):
                for kind in ("V", "Z", "T"):
                    if kind == "T" and lv == 2:
                        continue
                    parts += [(kind, lv, grp) for grp in range(2)]
            return parts

        @block.sync
        def _(sp):
            sp.dma_start(masks2[:], a["masks2"]).then_inc(consts_in, 16)

            def stage(i, j):
                sp.dma_start(st[:, j % 2, 0, :], qkvT[:, bass.ds(i * HB + j, 1), :].rearrange("p o t -> p (o t)"))\
                    .then_inc(st_in[j % 2], 16)
                sp.dma_start(st[:, j % 2, 1, :], qkvT[:, bass.ds(i * HB + (QK_HEADS + j), 1), :].rearrange("p o t -> p (o t)"))\
                    .then_inc(st_in[j % 2], 16)

            def stage_v(i, j):
                sp.dma_start(vst[:], qkvT[:, bass.ds(i * (2 * HB) + (2 * QK_HEADS + 2 * j), 2), :]).then_inc(vst_in, 16)

            with nc.sync.Fori(0, NB) as i:
                sp.wait_ge(z_ok, i * (8 * HB) + 1)
                for j in range(2):
                    stage(i, j)
                stage_v(i, 0)
                for j in range(2, HB):
                    sp.wait_ge(kk_made, at(i, 1, j - 2, 1))
                    stage(i, j)
                for j in range(2):
                    sp.wait_ge(kk_made, at(i, 1, j + 2, 1))
                    stage(i, j)
                for j in range(1, HB):
                    sp.wait_ge(vt_made, at(i, 1, j - 1, 1))
                    stage_v(i, j)
                    if j >= 2:
                        sp.wait_ge(qs_made, at(i, 3, j - 2, 3))
                        stage(i, j)

        @block.tensor
        def _(pe):
            pe.wait_ge(g_ok, 1)
            for n, mask in enumerate((upper, below, ones)):
                mm = nc.tensor.matmul(psA[:, 0, n * P:n * P + TT * V_HEADS], mask, flat(g[:]), start=True, stop=True)
            mm.then_inc(sums_ok, 1)
            pe.wait_ge(decays_ok, 1)

            def build(i, j):
                slot = j % 2
                pe.wait_ge(st_in[slot], i * 128 + 32 * (j // 2 + 1))
                if j:
                    pe.wait_ge(sq_ok, at(i, 8, j - 1, 8))
                    pe.wait_ge(tok_out, at(i, 1, j - 1, 1))
                for x, ps in enumerate((psO, psW)):
                    for c in range(TT):
                        tr = nc.tensor.transpose(ps[:, c, :], st[:, slot, x, c * P:(c + 1) * P], ident)
                tr.then_inc(turned, 1)
                if j:
                    pe.wait_ge(kk_out, at(i, 2, j - 1, 2))
                for c in range(TT):
                    cols = slice(c * P, (c + 1) * P)
                    for x in range(2):
                        mm = nc.tensor.matmul(psA[:, 1 - x, cols], st[:, slot, 1, cols], st[:, slot, x, cols],
                                              start=True, stop=True)
                mm.then_inc(kk_made, 1)
                pe.wait_ge(steps_ok, at(i, 1, j, 1))
                if j:
                    pe.wait_ge(e_ok, at(i, 1, j - 1, 1))
                for n in range(2):
                    mm = nc.tensor.matmul(psZ[:, n, :], below, flat(steps[:, 4 * n:4 * n + 4, :]), start=True, stop=True)
                mm.then_inc(seg_made, 1)

            def turn_v(i, j):
                pe.wait_ge(vst_in, at(i, 16, j, 16))
                if j:
                    pe.wait_ge(u_ok2, at(i, 6, j - 1, 6))
                else:
                    pe.wait_ge(e_ok, at(i, 1, HB - 1, 1))
                for h in range(2):
                    for c in range(TT):
                        tr = nc.tensor.transpose(psZ[:, h, c * P:(c + 1) * P], vst[:, h, c * P:(c + 1) * P], ident)
                tr.then_inc(vt_made, 1)

            def double(i, j, kind, lv, grp):
                bank = psZ if kind == "Z" else psA
                q = 2 * lv + grp + 1
                if kind == "V":
                    if lv == 0:
                        pe.wait_ge(tx_ok, at(i, 2, j, grp + 1))
                        if j:
                            pe.wait_ge(v_out, at(i, 6, j - 1, 4 + grp + 1))
                    else:
                        pe.wait_ge(t_out, at(i, 4, j, q - 2))
                elif kind == "Z":
                    pe.wait_ge(v_out, at(i, 6, j, q))
                    if lv == 0:
                        pe.wait_ge(ux_ok, at(i, 2, j, grp + 1))
                        pe.wait_ge(vr_ok, at(i, 2, j, grp + 1))
                    else:
                        pe.wait_ge(u_ok2, at(i, 6, j, q - 2))
                else:
                    pe.wait_ge(u_ok2, at(i, 6, j, q))
                for c in range(TT):
                    m = 4 * grp + c
                    out = bank[:, grp, c * P:(c + 1) * P]
                    if kind == "V":
                        mm = nc.tensor.matmul(out, C[:, 8 * j + m, :], T[:, m, :], start=True, stop=True)
                    elif kind == "Z":
                        mm = nc.tensor.matmul(out, V[:, m, :], U[j % 2][:, m, :], start=True, stop=True)
                    else:
                        mm = nc.tensor.transpose(out, U[j % 2][:, m, :], ident)
                mm.then_inc({"V": v_made, "Z": z_made, "T": t_made}[kind], 1)

            def chunk_products(i, j, c, fill):
                slot, cols = j % 2, slice(c * P, (c + 1) * P)
                if c:
                    pe.wait_ge(s_ok, at(i, 5, j, S_COUNT[c]))
                    nc.tensor.matmul(flat(psK[:, 0:2, :]), st[:, slot, 1, cols], flat(S[:]), start=True, stop=True)\
                        .then_inc(ks_made, 1)
                    pe.wait_ge(o_ok, at(i, 4, j, c))
                    nc.tensor.matmul(flat(psO[:, 0:2, :]), st[:, slot, 0, cols], flat(S[:]), start=True, stop=True)\
                        .then_inc(qs_made, 1)
                else:
                    pe.wait_ge(st_in[slot], i * 128 + 32 * (j // 2 + 3))
                fill(4 * c)
                if c:
                    pe.wait_ge(r_ok, at(i, 6, j, 2 * c))
                else:
                    pe.wait_ge(vr_ok, at(i, 2, j, 2))
                    pe.wait_ge(u_ok2, at(i, 6, j, 6))
                if c or j:
                    pe.wait_ge(w_ok, at(i, 4, j, c))
                for h in range(2):
                    rhs = R[:, h, :] if c else vr[slot][:, h, 0, :]
                    mm = nc.tensor.matmul(psW[:, h, :], U[slot][:, 4 * h + c, :], rhs, start=True, stop=True)
                mm.then_inc(w_made, 1)
                fill(4 * c + 1)
                if c < TT - 1:
                    pe.wait_ge(we_ok, at(i, 6, j, 2 * c + 2))
                    nc.tensor.matmul(flat(psK[:, 2:4, :]), ktok[:, j, c, :], flat(we[:]), start=True, stop=True)\
                        .then_inc(ds_made, 1)
                fill(4 * c + 2)
                pe.wait_ge(w_ok, at(i, 4, j, c + 1))
                if c:
                    pe.wait_ge(qt_ok, at(i, 6, j, 2 * c))
                elif j:
                    pe.wait_ge(o_ok, at(i, 4, j, 0))
                for h in range(2):
                    mm = nc.tensor.matmul(psO[:, 2 + h, :], PT[:, 8 * j + 4 * h + c, :], w_sb[:, h, :], start=True, stop=True)
                mm.then_inc(o_made, 1)
                fill(4 * c + 3)

            with nc.tensor.Fori(0, NB) as i:
                pe.wait_ge(z_ok, i * (8 * HB) + 1)
                for j in range(HB):
                    build(i, j)
                pe.wait_ge(sq_ok, at(i, 8, HB - 1, 8))
                pe.wait_ge(tok_out, at(i, 1, HB - 1, 1))
                pe.wait_ge(kk_out, at(i, 2, HB - 1, 2))
                pe.wait_ge(pt_ok, at(i, 1, HB - 1, 1))
                turn_v(i, 0)
                for kind, lv, grp in doubling_parts(0):
                    double(i, 0, kind, lv, grp)
                for j in range(HB):
                    parts = doubling_parts(j + 1) if j + 1 < HB else None

                    def fill(n):
                        if parts:
                            if n == 0:
                                turn_v(i, j + 1)
                            double(i, j + 1, *parts[n])

                    for c in range(TT):
                        chunk_products(i, j, c, fill)

        @block.scalar
        def _(act):
            act.wait_ge(abs_ok, 1)
            nc.scalar.activation(soft[:, 2], soft[:, 1], ACT.Exp, scale=-1.0).then_inc(u_ok, 1)
            nc.scalar.activation(a_exp[:], small[:, 4 * V_HEADS:5 * V_HEADS], ACT.Exp).then_inc(u_ok, 1)
            nc.scalar.activation(beta[:], ba[:, :, 0:V_HEADS], ACT.Exp, scale=-1.0).then_inc(u_ok, 1)
            act.wait_ge(sums_ok, 1)
            nc.scalar.activation(decays[:].rearrange("p n c h -> p n (c h)"),
                                 psA[:, 0, :].rearrange("p (n c) -> p n c", c=P)[:, 0:3, 0:TT * V_HEADS],
                                 ACT.Exp).then_inc(decays_ok, 1)

            def squares(i, j):
                act.wait_ge(turned, at(i, 1, j, 1))
                nc.scalar.activation(ktok[:, j], psW[:], ACT.Copy).then_inc(tok_out, 1)
                act.wait_ge(tok_out, at(i, 1, j, 1))
                for ps, to in ((psO, ssq), (psW, ssk)):
                    for c in range(TT):
                        nc.scalar.activation(ps[:, c, :], ps[:, c, :], ACT.Square, accum_out=to[:, j, c:c + 1])\
                            .then_inc(sq_ok, 1)

            def exps(i, j):
                act.wait_ge(seg_made, at(i, 1, j, 1))
                if j:
                    act.wait_ge(c_ok, at(i, 8, j - 1, 8))
                    act.wait_ge(pt_ok, at(i, 1, j - 1, 1))
                nc.scalar.activation(E, psZ[:].rearrange("p n (m c) -> p (n m) c", c=P), ACT.Exp).then_inc(e_ok, 1)

            def compact(i, j):
                act.wait_ge(c_ok, at(i, 8, j, 8))
                for r in range(4):
                    rows = slice(32 * r, 32 * r + 32)
                    nc.scalar.activation(Cc[rows, 8 * j:8 * j + 8, :], C[rows, 8 * j:8 * j + 8, rows], ACT.Copy)\
                        .then_inc(cc_ok, 1)

            def evacuate(i, j, kind, lv, grp):
                q = 2 * lv + grp + 1
                ms4 = slice(4 * grp, 4 * grp + 4)
                src = psA[:, grp, :].rearrange("p (m c) -> p m c", c=P)
                if kind == "V":
                    act.wait_ge(v_made, at(i, 6, j, q))
                    if lv:
                        act.wait_ge(z_made, at(i, 6, j, q - 2))
                    elif j:
                        act.wait_ge(z_made, at(i, 6, j - 1, 4 + q))
                    nc.scalar.activation(V[:, ms4, :], src, ACT.Copy).then_inc(v_out, 1)
                elif kind == "T":
                    act.wait_ge(t_made, at(i, 4, j, q))
                    nc.scalar.activation(T[:, ms4, :], src, ACT.Copy).then_inc(t_out, 1)

            def out_squares(i, j, c):
                act.wait_ge(o_ok, at(i, 4, j, c + 1))
                if j or c:
                    act.wait_ge(osq_ok, at(i, 8, j, 2 * c))
                for h in range(2):
                    nc.scalar.activation(junk[:, h, :], O[j % 2][:, h, c, :], ACT.Square, scale=P ** -0.5,
                                         accum_out=sums[:, j % 2, h, c:c + 1]).then_inc(osq_ok, 1)

            def chunk_part(i, j, c, fill):
                if c:
                    act.wait_ge(qs_made, at(i, 3, j, c))
                    act.wait_ge(o_ok, at(i, 4, j, c))
                    for h in range(2):
                        nc.scalar.activation(qt[:, h, :], psO[:, h, :], ACT.Copy,
                                             scale=dsel[:, 0, 2 * j + h, c:c + 1]).then_inc(qt_ok, 1)
                fill(4 * c)
                if c < TT - 1:
                    act.wait_ge(w_ok, at(i, 4, j, c + 1))
                    if c or j:
                        act.wait_ge(ds_made, at(i, 3, j, c))
                    for h in range(2):
                        nc.scalar.activation(we[:, h, :], w_sb[:, h, :], ACT.Copy,
                                             scale=dsel[:, 1, 2 * j + h, c:c + 1]).then_inc(we_ok, 1)
                fill(4 * c + 1)
                if c:
                    out_squares(i, j, c - 1)
                elif j:
                    out_squares(i, j - 1, TT - 1)
                fill(4 * c + 2)
                fill(4 * c + 3)

            with nc.scalar.Fori(0, NB) as i:
                act.wait_ge(z_ok, i * (8 * HB) + 1)
                squares(i, 0)
                for j in range(HB):
                    exps(i, j)
                    if j + 1 < HB:
                        squares(i, j + 1)
                    compact(i, j)
                act.wait_ge(scales_ok, i * 2 + 2)
                for kind, lv, grp in doubling_parts(0):
                    evacuate(i, 0, kind, lv, grp)
                for j in range(HB):
                    parts = doubling_parts(j + 1) if j + 1 < HB else None

                    def fill(n):
                        if parts:
                            evacuate(i, j + 1, *parts[n])

                    for c in range(TT):
                        chunk_part(i, j, c, fill)
                out_squares(i, HB - 1, TT - 1)

        @block.gpsimd
        def _(pool):
            for n, e in enumerate((0.5, -0.5)):
                nc.gpsimd.memset(half[:, n, :], e).then_inc(pool_s, 1)
            pool.wait_ge(pool_s, 2)

            def log_decay_steps(i, j):
                if j:
                    pool.wait_ge(seg_made, at(i, 1, j - 1, 1))
                gs = gsel[:, 2 * j:2 * j + 2, :].rearrange("p h c -> p (h c)")
                nc.gpsimd.tensor_tensor(steps, upper.unsqueeze(1).broadcast_to([P, 8, P]),
                                        gs.unsqueeze(2).broadcast_to([P, 8, P]), ALU.mult).then_inc(steps_ok, 1)

            def expand(i, j, compact, full, done):
                for grp in range(2):
                    if j and done is tx_ok:
                        pool.wait_ge(v_made, at(i, 6, j - 1, 4 + grp + 1))
                    src = compact[:, 8 * j + 4 * grp:8 * j + 4 * grp + 4, :]
                    nc.gpsimd.tensor_tensor(full[:, 4 * grp:4 * grp + 4, :].rearrange("p m (r c) -> p m r c", c=32),
                                            src.unsqueeze(2).broadcast_to([P, 4, 4, 32]),
                                            block32.rearrange("p (r c) -> p r c", c=32).unsqueeze(1).broadcast_to([P, 4, 4, 32]),
                                            ALU.mult).then_inc(done, 1)

            def norm_factor(i, j):
                pool.wait_ge(osq_ok, at(i, 8, j, 8))
                nc.gpsimd.tensor_tensor(ms[:], sums[:, j % 2], qe[:, j, :].unsqueeze(1).broadcast_to([P, 2, TT]),
                                        ALU.add).then_inc(pool_s, 1)
                pool.wait_ge(pool_s, at(i, 1, j, 3))
                nc.gpsimd.tensor_tensor(rs[:, j % 2], ms[:],
                                        half[:, 1, 0:2 * TT].rearrange("p (h c) -> p h c", c=TT), ALU.pow).then_inc(rs_ok, 1)

            with nc.gpsimd.Fori(0, NB) as i:
                pool.wait_ge(z_ok, i * (8 * HB) + 1)
                pool.sem_inc(gate, 1)
                nc.gpsimd.memset(Uf, 0.0).then_inc(eye_ok, 1)
                pool.wait_ge(eye_ok, i * 2 + 1)
                pool.sem_inc(gate, 1)
                nc.gpsimd.memset(Uf.rearrange("p (a b) -> p a b", b=33)[:, :, 0], 1.0).then_inc(eye_ok, 1)
                pool.wait_ge(sel_ok, i * 3 + 3)
                log_decay_steps(i, 0)
                for j in range(HB):
                    if j + 1 < HB:
                        log_decay_steps(i, j + 1)
                    pool.wait_ge(e_ok, at(i, 1, j, 1))
                    pool.wait_ge(kk_out, at(i, 2, j, 2))
                    nc.gpsimd.tensor_tensor(PT[:, 8 * j:8 * j + 8, :].rearrange("p (h c) e -> p h c e", h=2),
                                            E.rearrange("p (h c) e -> p h c e", h=2),
                                            KQm.unsqueeze(1).broadcast_to([P, 2, TT, P]), ALU.mult).then_inc(pt_ok, 1)
                pool.wait_ge(kss_ok, at(i, 1, HB - 1, 1))
                nc.gpsimd.tensor_tensor(flat(rinv[:]), flat(kss[:]), half[:, 0, :], ALU.pow).then_inc(rinv_ok, 1)
                pool.wait_ge(uc_ok, i * 2 + 2)
                pool.wait_ge(pt_ok, at(i, 1, HB - 1, 1))
                for j in range(2):
                    expand(i, j, Tc, T, tx_ok)
                    expand(i, j, Uc, U[j % 2], ux_ok)
                for j in range(HB):
                    if j:
                        norm_factor(i, j - 1)
                    if j + 2 < HB:
                        expand(i, j + 2, Tc, T, tx_ok)
                        pool.wait_ge(w_made, at(i, 4, j, 4))
                        expand(i, j + 2, Uc, U[j % 2], ux_ok)
                norm_factor(i, HB - 1)

        @block.vector
        def _(dve):
            own = Own(dve, own_p)
            dve.sem_inc(z_ok, 1)
            nc.vector.memset(sign[:], 1.0).then_inc(own_p, 1)
            own.n += 1
            own.wait()
            own.did(nc.vector.memset(sign[:, 0:1], -1.0))
            softplus_head(nc, dve, own, soft[:, 0], soft[:, 1], ba[:, :, V_HEADS:],
                          small[:, 3 * V_HEADS:4 * V_HEADS].unsqueeze(1).broadcast_to([P, TT, V_HEADS]), TT)
            own.wait()
            dve.sem_inc(abs_ok, 1)
            dve.wait_ge(u_ok, 3)
            own.did(nc.vector.tensor_scalar(beta[:], beta[:], 1.0, None, ALU.add))
            own.wait()
            own.did(nc.vector.reciprocal(beta[:], beta[:]))
            softplus_tail(nc, dve, own, g[:], soft[:, 0], soft[:, 2], (soft[:, 3], soft[:, 4], soft[:, 5]))
            own.did(nc.vector.scalar_tensor_tensor(out=g[:], in0=g[:], scalar=-1.0,
                                                   in1=a_exp[:].unsqueeze(1).broadcast_to([P, TT, V_HEADS]),
                                                   op0=ALU.mult, op1=ALU.mult))
            own.wait()
            dve.sem_inc(g_ok, 1)
            dve.wait_ge(decays_ok, 1)
            dve.wait_ge(consts_in, 16)

            def scale_kq(i, j, own):
                dve.wait_ge(sq_ok, at(i, 8, j, 8))
                nc.vector.tensor_scalar(kss[:, j, :], ssk[:, j, :], EPS2, None, ALU.add).then_inc(kss_ok, 1)
                dve.wait_ge(kss_ok, at(i, 1, j, 1))
                own.did(nc.vector.reciprocal(r2[:, j, :], kss[:, j, :]))
                own.wait()
                own.did(nc.vector.scalar_tensor_tensor(out=nbp[:, j], in0=bsel[:, 2 * j:2 * j + 2, :], scalar=-1.0,
                                                       in1=r2[:, j, :].unsqueeze(1).broadcast_to([P, 2, TT]),
                                                       op0=ALU.mult, op1=ALU.mult))
                dve.wait_ge(kk_made, at(i, 1, j, 1))
                four = psA[:].rearrange("p n (m c) -> p n m c", c=P)
                nc.vector.tensor_tensor(KKm, four[:, 0], strict.unsqueeze(1).broadcast_to([P, TT, P]), ALU.mult)\
                    .then_inc(kk_out, 1)
                if j:
                    dve.wait_ge(pt_ok, at(i, 1, j - 1, 1))
                nc.vector.tensor_tensor(KQm, four[:, 1], upper.unsqueeze(1).broadcast_to([P, TT, P]), ALU.mult)\
                    .then_inc(kk_out, 1)
                dve.wait_ge(kk_out, at(i, 2, j, 2))
                dve.wait_ge(e_ok, at(i, 1, j, 1))
                own.wait()
                for h in range(2):
                    for c in range(TT):
                        nc.vector.scalar_tensor_tensor(out=C[:, 8 * j + 4 * h + c, :], in0=E[:, 4 * h + c, :],
                                                       scalar=nbp[:, j, h, c:c + 1], in1=KKm[:, c, :],
                                                       op0=ALU.mult, op1=ALU.mult).then_inc(c_ok, 1)

            def invert_16(i, own):
                dve.wait_ge(cc_ok, at(i, 4, HB - 1, 4))
                own.did(nc.vector.transpose(Cf[:, 0:1024].rearrange("p (c s) -> p c s", s=32),
                                            Cc.rearrange("p m c -> p c m")))
                dve.wait_ge(eye_ok, i * 2 + 2)
                cd, ud = (f.rearrange("p (a x) -> p a x", a=2)[:, :, 0:512].rearrange("p a (c s) -> p a c s", s=32)
                          for f in (Cf, Uf))
                for s in range(15):
                    later, rows = slice(s + 1, 16), s + 1
                    shape = [P, 2, 15 - s, rows]
                    t = tmp[:, 0:2 * (15 - s) * rows].rearrange("p (a c r) -> p a c r", a=2, r=rows)
                    own.wait()
                    own.did(nc.vector.tensor_tensor(t, cd[:, :, later, s:s + 1].broadcast_to(shape),
                                                    ud[:, :, s:s + 1, 0:rows].broadcast_to(shape), ALU.mult))
                    own.wait()
                    own.did(nc.vector.tensor_tensor(ud[:, :, later, 0:rows], ud[:, :, later, 0:rows], t, ALU.add))
                own.wait()
                blocks = Uf[:, 0:1024].rearrange("p (c s) -> p c s", s=32)
                nc.vector.transpose(Uc[:].rearrange("p m c -> p c m"), blocks).then_inc(uc_ok, 1)
                nc.vector.transpose(Tc[:].rearrange("p m s -> p s m"), blocks.rearrange("p c s -> p s c")).then_inc(uc_ok, 1)

            def doubled(i, j, kind, lv, grp):
                if kind == "V" and lv == 0:
                    dve.wait_ge(vt_made, at(i, 1, j, 1))
                    dve.wait_ge(rinv_ok, i + 1)
                    nc.vector.tensor_tensor(vr[j % 2][:, grp], psZ[:, grp, :].rearrange("p (c e) -> p c e", e=P),
                                            rinv[:, j, :].unsqueeze(2).broadcast_to([P, TT, P]), ALU.mult).then_inc(vr_ok, 1)
                elif kind == "Z":
                    dve.wait_ge(z_made, at(i, 6, j, 2 * lv + grp + 1))
                    dve.sem_inc(gate_v, 1)
                    level = masks2[:, 2 + lv, :].bitcast(mybir.dt.int32)
                    nc.vector.copy_predicated(U[j % 2][:, 4 * grp:4 * grp + 4, :], level.unsqueeze(1).broadcast_to([P, 4, P]),
                                              psZ[:, grp, :].rearrange("p (m c) -> p m c", c=P)).then_inc(u_ok2, 1)

            def chunk_part(i, j, c, fill):
                slot = j % 2
                if c:
                    dve.wait_ge(ks_made, at(i, 3, j, c))
                    for h in range(2):
                        nc.vector.scalar_tensor_tensor(out=R[:, h, :], in0=psK[:, h, :],
                                                       scalar=dsel[:, 0, 2 * j + h, c:c + 1], in1=vr[slot][:, h, c, :],
                                                       op0=ALU.mult, op1=ALU.subtract).then_inc(r_ok, 1)
                fill(4 * c)
                dve.wait_ge(w_made, at(i, 4, j, c + 1))
                if c or j:
                    dve.wait_ge(o_made, at(i, 4, j, c))
                    dve.wait_ge(we_ok, at(i, 6, j, 2 * c))
                nc.vector.tensor_tensor(w_sb[:], psW[:, 0:2, :], wsc[:, j, :, c:c + 1].broadcast_to([P, 2, P]), ALU.mult)\
                    .then_inc(w_ok, 1)
                fill(4 * c + 1)
                if c < TT - 1:
                    dve.wait_ge(ds_made, at(i, 3, j, c + 1))
                    if c or j:
                        dve.wait_ge(qs_made, at(i, 3, j, c))
                    if c:
                        dve.wait_ge(s_ok, at(i, 5, j, S_COUNT[c]))
                        for h in range(2):
                            nc.vector.scalar_tensor_tensor(out=S[:, h, :], in0=S[:, h, :],
                                                           scalar=dsel[:, 2, 2 * j + h, c:c + 1], in1=psK[:, 2 + h, :],
                                                           op0=ALU.mult, op1=ALU.add).then_inc(s_ok, 1)
                    else:
                        nc.vector.tensor_copy(S[:], psK[:, 2:4, :]).then_inc(s_ok, 1)
                fill(4 * c + 2)
                dve.wait_ge(o_made, at(i, 4, j, c + 1))
                out = O[slot][:, :, c, :]
                if c:
                    dve.wait_ge(qt_ok, at(i, 6, j, 2 * c))
                    nc.vector.tensor_tensor(out, psO[:, 2:4, :], qt[:], ALU.add).then_inc(o_ok, 1)
                else:
                    nc.vector.tensor_copy(out, psO[:, 2:4, :]).then_inc(o_ok, 1)
                fill(4 * c + 3)

            def finish(i, j):
                dve.wait_ge(rs_ok, at(i, 1, j, 1))
                for h in range(2):
                    for c in range(TT):
                        zz = z[:, c, bass.ds(i * (2 * HB * P) + (2 * j + h) * P, P)]
                        nc.vector.scalar_tensor_tensor(out=zz, in0=O[j % 2][:, h, c, :], scalar=rs[:, j % 2, h, c:c + 1],
                                                       in1=zz, op0=ALU.mult, op1=ALU.mult).then_inc(z_ok, 1)

            OWN_STEPS = 39
            with nc.vector.Fori(0, NB) as i:
                own = Own(dve, own_s, i * OWN_STEPS)
                dve.wait_ge(z_ok, i * (8 * HB) + 1)
                heads = bass.ds(i * (2 * HB), 2 * HB)
                for to, src in ((dsel[:].rearrange("p n h c -> p n c h"), decays[:, :, :, heads]),
                                (gsel[:].rearrange("p h c -> p c h"), g[:, :, heads]),
                                (bsel[:].rearrange("p h c -> p c h"), beta[:, :, heads])):
                    nc.vector.tensor_copy(to, src).then_inc(sel_ok, 1)
                dve.wait_ge(sel_ok, i * 3 + 3)
                for j in range(HB):
                    scale_kq(i, j, own)
                nc.vector.tensor_scalar(qe[:], ssq[:], EPS2, P * EPS2, ALU.add, ALU.mult).then_inc(scales_ok, 1)
                nc.vector.tensor_tensor(wsc[:], nbp[:], sign[:].unsqueeze(1).unsqueeze(1).broadcast_to([P, HB, 2, TT]),
                                        ALU.mult).then_inc(scales_ok, 1)
                invert_16(i, own)
                for kind, lv, grp in doubling_parts(0):
                    doubled(i, 0, kind, lv, grp)
                for j in range(HB):
                    parts = doubling_parts(j + 1) if j + 1 < HB else None

                    def fill(n):
                        if parts:
                            doubled(i, j + 1, *parts[n])

                    for c in range(TT):
                        chunk_part(i, j, c, fill)
                        if c == 1 and j:
                            finish(i, j - 1)
                finish(i, HB - 1)
                assert own.n == OWN_STEPS, own.n


def modulate(nc, a, masks, resid, row_f, modc, h_hi, h_lo):
    ctx = Phase(nc, "modulate")
    with ctx:
        sb, sem = ctx.sb, ctx.sem
        ident = masks[:, IDENT, :]
        xn = sb("xn", [P, TT, D_MODEL])
        g_col = sb("g_col", [P, KT])
        gain = sb("gain", [P, KT])
        h = sb("h", [P, 2, SEQ])
        ps_t = ctx.psum("ps_h", [P, 4, COLS], F32)
        g_in = sem("g_in")
        x1_out = sem("x1_out")
        xn_ok = sem("xn_ok")
        gain_ok = sem("gain_ok")
        turned = sem("turned")
        high_ok = sem("high_ok")
        h_ok = sem("h_ok")
        low_ok = sem("low_ok")
        block = ctx.enter_context(nc.Block())

        @block.sync
        def _(sp):
            sp.dma_start(g_col[:], a["norm_g"]).then_inc(g_in, 16)
            sp.dma_start(a["x1"].rearrange("(t p) d -> p t d", p=P), resid[:]).then_inc(x1_out, 16)
            sp.wait_ge(x1_out, 16)

        @block.tensor
        def _(pe):
            for e in range(KT):
                if e >= 4:
                    pe.wait_ge(low_ok, e - 3)
                for t in range(TT):
                    if e == 0:
                        pe.wait_ge(xn_ok, t + 1)
                    tr = nc.tensor.transpose(ps_t[:, e % 4, t * P:(t + 1) * P], xn[:, t, e * P:(e + 1) * P], ident)
                tr.then_inc(turned, 1)

        @block.scalar
        def _(act):
            act.wait_ge(gain_ok, 1)
            for e in range(KT):
                act.wait_ge(turned, e + 1)
                nc.scalar.activation(h_hi[:, e, :], ps_t[:, e % 4, :], ACT.Identity, scale=gain[:, e:e + 1],
                                     bias=modc[:, e:e + 1]).then_inc(high_ok, 1)

        @block.vector
        def _(dve):
            dve.wait_ge(g_in, 16)
            nc.vector.scalar_tensor_tensor(out=gain[:], in0=modc[:, KT:2 * KT], scalar=1.0, in1=g_col[:],
                                           op0=ALU.add, op1=ALU.mult).then_inc(gain_ok, 1)
            for t in range(TT):
                nc.vector.tensor_scalar(xn[:, t, :], resid[:, t, :], row_f[:, t:t + 1], None, ALU.mult)\
                    .then_inc(xn_ok, 1)
            dve.wait_ge(gain_ok, 1)
            for e in range(KT):
                dve.wait_ge(high_ok, e + 1)
                if e >= 2:
                    dve.wait_ge(low_ok, e - 1)
                nc.vector.tensor_scalar(h[:, e % 2, :], ps_t[:, e % 4, :], gain[:, e:e + 1], modc[:, e:e + 1],
                                        ALU.mult, ALU.add).then_inc(h_ok, 1)
                dve.wait_ge(h_ok, e + 1)
                nc.vector.tensor_tensor(h_lo[:, e, :], h[:, e % 2, :], h_hi[:, e, :], ALU.subtract).then_inc(low_ok, 1)


def kernel(**inputs):
    import numpy as _np
    import concourse.bacc as _bacc
    from concourse.bass_utils import run_bass_kernel_spmd as _run

    nc = _bacc.Bacc("TRN2", target_bir_lowering=False, num_devices=1)
    f = {k: _np.ascontiguousarray(v) for k, v in inputs.items()}

    def by_channel(v):
        return _np.ascontiguousarray(v.reshape(-1, P).T)

    def taps(w):
        return _np.ascontiguousarray(w.reshape(w.shape[0], -1, P).transpose(2, 1, 0))

    arrays = {
        "x": f["x"][0],
        "xT": _np.ascontiguousarray(f["x"][0].T),
        "w_in": f["w_in"],
        "masks": square_masks(),
        "masks2": block_masks(),
        "att_bias": attention_bias(),
        "small": _np.concatenate([f["dt_bias"][0], f["a_log"][0], f["d_skip"][0],
                                  f["gdn_dt_bias_2"][0], f["gdn_a_log_2"][0]]),
        "conv1": taps(_np.concatenate([f["conv_w"][0], f["conv_b"]], 0)),
        "mix_g": by_channel(_np.concatenate([f["att_norm_g"][0], f["ssm_norm_g"][0]])),
        "w_out": f["w_out"],
        "ln_g": f["ln_g"][0],
        "ln_b": f["ln_b"][0],
        "c": by_channel(f["c_2"][0]),
        "ada_w": f["ada_w_2"],
        "ada_b": by_channel(f["ada_b_2"][0]),
        "norm_g": by_channel(f["norm_g_2"][0]),
        "gdn_w_in": f["gdn_w_in_2"],
        "conv2": taps(f["gdn_conv_w_2"][0]),
        "gdn_g": by_channel(_np.tile(f["gdn_norm_w_2"][0], V_HEADS)),
        "gdn_w_out": f["gdn_w_out_2"],
        "final_g": f["final_g_2"],
    }
    a = {k: nc.dram_tensor("in_" + k, v.shape, F32, kind="ExternalInput").ap() for k, v in arrays.items()}
    a["x1"] = nc.dram_tensor("x1_kept", (SEQ, D_MODEL), F32, kind="Internal").ap()
    a["out"] = nc.dram_tensor("out_0", (1, SEQ, D_MODEL), F32, kind="ExternalOutput").ap()[0]
    build(nc, a)
    r = _run(nc, [{"in_" + k: v for k, v in arrays.items()}], core_ids=[0])
    return r.results[0]["out_0"]
```

```python
from contextlib import ExitStack

import numpy as np

import concourse.bass as bass
from concourse import mybir

F32 = mybir.dt.float32
F32R = mybir.dt.float32r
ALU = mybir.AluOpType
ACT = mybir.ActivationFunctionType

P = 128
SEQ, D_MODEL = 512, 1024
TT = SEQ // P
KT = D_MODEL // P
HALF = KT // 2
COLS = 512
ATT_HEADS, HD = 16, 64
SSM_HEADS, SSM_GROUPS = 16, 2
HPG = SSM_HEADS // SSM_GROUPS
D_CONV1 = 1536
CT1 = D_CONV1 // P
CONV = 4
COL_XBC = 5120
COL_DT = 6656
QK_SCALE = HD ** -0.5
S_OFF = {2: 0, 0: 384, 3: 512, 1: 1024}
S_LEN = 1280
EPS1 = 1e-5
QK_HEADS, V_HEADS = 8, 16
D_CONV2 = 4096
D_Z2 = V_HEADS * P
MOD_COLS = 1536
EPS2 = 1e-6
ALPHA = 2.0 ** 0.25


def attention_bias():
    dist = np.arange(P)[:, None] + 384 - np.arange(SEQ)[None, :]
    count = (((dist <= 128).astype(int) + (dist % 4 == 0) + (dist % 16 == 0)) * (dist >= 0))
    slopes = (2.0 ** (-8.0 * np.arange(1, ATT_HEADS + 1) / ATT_HEADS)).astype(np.float32)
    log_count = np.where(count > 0, np.log(np.maximum(count, 1)), -1e30)
    bias = (-slopes[:, None, None] * dist + log_count) / QK_SCALE
    return bias.astype(np.float32)


def square_masks():
    j, l = np.arange(P)[:, None], np.arange(P)[None, :]
    return np.stack([j == l, j <= l, j > l, j >= 0 * l], 1).astype(np.float32)


IDENT, UPPER, BELOW, ONES = range(4)


def block_masks():
    j, l = np.arange(P)[:, None], np.arange(P)[None, :]
    levels = [(j // (2 * b) == l // (2 * b)) & (j // b < l // b) for b in (16, 32, 64)]
    return np.stack([j < l, j // 32 == l // 32] + levels, 1).astype(np.float32)


def log1p_series():
    return [1.0 / (2 * k + 1) for k in range(1, 9)]


class Phase(ExitStack):

    used = []

    def __init__(self, nc, name):
        super().__init__()
        self.nc, self.name = nc, name

    def sb(self, name, shape, dt=F32):
        return self.enter_context(self.nc.sbuf_tensor(f"{self.name}_{name}", shape, dt))

    def psum(self, name, shape, dt=F32):
        return self.enter_context(self.nc.psum_tensor(f"{self.name}_{name}", shape, dt))

    def sem(self, name):
        s = self.enter_context(self.nc.semaphore(f"{self.name}_{name}"))
        Phase.used.append(s.num)
        return s

    @classmethod
    def take_used(cls):
        nums = sorted(set(cls.used))
        cls.used.clear()
        return nums


def clear_semaphores(pool, nums):
    start = 0
    for n in range(1, len(nums) + 1):
        if n == len(nums) or nums[n] != nums[n - 1] + 1:
            pool.sem_clear(range(nums[start], nums[n - 1] + 1))
            start = n


class Own:

    def __init__(self, eng, sem, base=0):
        self.eng, self.sem, self.n, self.base = eng, sem, 0, base

    def did(self, ins):
        ins.then_inc(self.sem, 1)
        self.n += 1
        return self.n

    def wait(self, n=None):
        self.eng.wait_ge(self.sem, self.base + (self.n if n is None else n))


def three_products(nc, out, w_hi, w_lo, x_hi, x_lo, first, last):
    nc.tensor.matmul(out, w_hi, x_hi, start=first, stop=False, skip_group_check=True)
    nc.tensor.matmul(out, w_hi, x_lo, start=False, stop=False, skip_group_check=True)
    return nc.tensor.matmul(out, w_lo, x_hi, start=False, stop=last, skip_group_check=True)


def build(nc, a):
    ctx = ExitStack()
    with ctx:
        def sb(name, shape, dt=F32, c=ctx):
            return c.enter_context(nc.sbuf_tensor(name, shape, dt))

        masks = sb("masks", [P, 4, P])
        small = sb("small", [P, 16 * 5])
        cond = sb("cond", [P, KT])
        resid = sb("resid", [P, TT, D_MODEL])
        modc = sb("modc", [P, 3 * KT])
        row_f = sb("row_f", [P, TT])
        att_f = sb("att_f", [P, TT])
        wba = sb("wba", [P, KT, 2 * V_HEADS])
        wba_in = ctx.enter_context(nc.semaphore("wba_in"))
        raw = [sb(f"raw{i}", [P, HALF, COLS]) for i in range(2)]
        ahead = [ctx.enter_context(nc.semaphore(f"ahead{i}")) for i in range(2)]
        pool_dmas = [ctx.enter_context(nc.semaphore(f"pool_dma{i}")) for i in range(2)]
        with ExitStack() as first:
            tok = sb("tok", [P, TT, 3 * 1024], c=first)
            with ExitStack() as scans:
                xbc = sb("xbc", [P, CT1, SEQ], c=scans)
                dt = sb("dt", [P, TT, SSM_HEADS], c=scans)
                adt = sb("adt", [P, TT, SSM_HEADS], c=scans)
                with ExitStack() as heads:
                    qk = sb("qk", [P, 16, SEQ], c=heads)
                    projections1(nc, a, ahead, raw, masks, small, cond, resid, qk, tok, xbc, dt, adt)
                    attention(nc, a, resid, raw, masks, cond, qk, tok, pool_dmas)
                ssd(nc, a, ahead, raw, att_f, masks, small, tok, xbc, dt, adt)
            output_projection(nc, a, ahead, wba, wba_in, raw, masks, resid, row_f, tok[:, :, 1024:], a["w_out"], False, modc)
        with ExitStack() as second:
            z = sb("z", [P, TT, D_Z2], c=second)
            scan = second.enter_context(ExitStack())
            qkvT = sb("qkvT", [P, D_CONV2 // P, SEQ], c=scan)
            beta = sb("beta", [P, TT, V_HEADS], c=scan)
            g = sb("g", [P, TT, V_HEADS], c=scan)
            hs = second.enter_context(ExitStack())
            h_hi = sb("h_hi", [P, KT, SEQ], F32R, c=hs)
            h_lo = sb("h_lo", [P, KT, SEQ], F32R, c=hs)
            projections2(nc, a, ahead, wba, wba_in, raw, masks, resid, row_f, modc, small, h_hi, h_lo, qkvT, z, beta, g)
            hs.close()
            gated_deltanet(nc, a, ahead, masks, resid, raw, qkvT, z, beta, g)
            scan.close()
            output_projection(nc, a, ahead, wba, wba_in, raw, masks, resid, row_f, z, a["gdn_w_out"], True, modc)


def resid_units(resid):
    both = resid[:].rearrange("p t (k c) -> p (t k) c", c=COLS)
    return [both[:, 0:HALF, :], both[:, HALF:KT, :]]


def spare_buffers(resid):
    spare = resid[:].rearrange("p t d -> p (t d)")
    pre = spare[:, 0:2 * (CONV - 1 + SEQ)].rearrange("p (j t) -> p j t", j=2)
    acc = spare[:, 2048:2048 + 2 * SEQ].rearrange("p (j t) -> p j t", j=2)
    soft = spare[:, 3072:3072 + 6 * TT * SSM_HEADS].rearrange("p (n t h) -> p n t h", n=6, t=TT)
    rows = spare[:, 3456:3456 + SEQ]
    return pre, acc, soft, rows


class ConvStream:

    def __init__(self, nc, sem, pre, acc, cw, banks, dst, bias):
        self.nc, self.pre, self.acc, self.cw, self.banks, self.dst, self.bias = nc, pre, acc, cw, banks, dst, bias
        self.pre_ready = sem("pre_ready")
        self.taps_done = sem("taps_done")
        self.conv_done = sem("conv_done")
        self.tap_step = sem("tap_step")

    def read_and_silu(self, act, b, par, banks_free):
        nc = self.nc
        for pair in range(2):
            tiles = [2 * pair + j for j in range(2)]
            for e in tiles:
                act.wait_ge(self.taps_done, b * 4 + (e + 1))
                nc.scalar.activation(self.pre[:, e % 2, CONV - 1:], self.banks[:, 4 * par + e, :], ACT.Copy)\
                    .then_inc(self.pre_ready, 1)
            if pair:
                act.wait_ge(self.pre_ready, b * 4 + 4)
                act.sem_inc(banks_free, 1)
            for e in tiles:
                act.wait_ge(self.taps_done, b * 4 + (e + 3))
                dst = self.dst[:, bass.ds(b * 4 + e, 1), :].rearrange("p o t -> p (o t)")
                if self.bias:
                    ins = nc.scalar.activation(dst, self.acc[:, e % 2, :], ACT.Silu,
                                               bias=self.cw[:, 4 * b + e, CONV:CONV + 1])
                else:
                    ins = nc.scalar.activation(dst, self.acc[:, e % 2, :], ACT.Silu)
                ins.then_inc(self.conv_done, 1)

    def sum_taps(self, dve, b):
        nc, step = self.nc, 0
        for pair in range(2):
            tiles = [2 * pair + j for j in range(2)]
            step_of = {}
            for k in range(CONV):
                for e in tiles:
                    tap = self.cw[:, bass.ds(b * 4 + e, 1), k:k + 1].rearrange("p o k -> p (o k)")
                    src = self.pre[:, e % 2, k:k + SEQ]
                    acc = self.acc[:, e % 2, :]
                    if k == 0:
                        dve.wait_ge(self.pre_ready, b * 4 + (e + 1))
                        dve.wait_ge(self.conv_done, b * 4 + (e + 1))
                        ins = nc.vector.tensor_scalar(acc, src, tap, None, ALU.mult)
                    else:
                        dve.wait_ge(self.tap_step, b * 12 + step_of[e])
                        ins = nc.vector.scalar_tensor_tensor(out=acc, in0=src, scalar=tap, in1=acc,
                                                             op0=ALU.mult, op1=ALU.add)
                    if k == CONV - 1:
                        ins.then_inc(self.taps_done, 1)
                    else:
                        ins.then_inc(self.tap_step, 1)
                        step += 1
                        step_of[e] = step


class WeightStream:

    def __init__(self, nc, sem, sb, raw, ahead, projection, first=None):
        self.nc, self.raw, self.ahead, self.ahead_count = nc, raw, ahead, 16 * projection
        self.first = first or raw
        self.hi = [sb(f"w_hi{i}", [P, HALF, COLS], F32R) for i in range(2)]
        self.lo = [sb(f"w_lo{i}", [P, HALF, COLS], F32R) for i in range(2)]
        self.landed = [sem(f"landed{i}") for i in range(2)]
        self.hi_ready = sem("hi_ready")
        self.lo_ready = sem("lo_ready")
        self.units_used = sem("units_used")

    @staticmethod
    def load_ahead(sp, ahead, to, w, order=(0, 1)):
        for s in order:
            sp.dma_start(to[s], w[:, HALF * s:HALF * (s + 1), 0:COLS]).then_inc(ahead[s], 16)

    def load(self, sp, s, n, src):
        sp.wait_ge(self.lo_ready, n * 2 + (s + 1))
        sp.dma_start(self.raw[s][:], src).then_inc(self.landed[s], 16)

    def round(self, act, s, n):
        if isinstance(n, int) and n == 0:
            act.wait_ge(self.ahead[s], self.ahead_count)
        else:
            act.wait_ge(self.landed[s], n * 16)
        act.wait_ge(self.units_used, n * 2 + (s + 1))
        self.nc.scalar.activation(self.hi[s][:], self.source(s, n)[:], ACT.Copy).then_inc(self.hi_ready, 1)

    def source(self, s, n):
        return self.first[s] if isinstance(n, int) and n == 0 else self.raw[s]

    def rest(self, engine, queue, s, n):
        queue.wait_ge(self.hi_ready, n * 2 + (s + 1))
        engine.tensor_tensor(self.lo[s][:], self.source(s, n)[:], self.hi[s][:], ALU.subtract)\
            .then_inc(self.lo_ready, 1)

    def wait_unit(self, pe, s, n):
        pe.wait_ge(self.lo_ready, n * 2 + (s + 3))

    def channels(self, pe, n, par, banks, x_hi, x_lo, banks_free):
        pe.wait_ge(banks_free, n + 1)
        for s in range(2):
            self.wait_unit(pe, s, n)
            for e in range(4):
                for kk in range(HALF):
                    k = HALF * s + kk
                    cols = slice(e * P, (e + 1) * P)
                    mm = three_products(self.nc, banks[:, 4 * par + e, :], self.hi[s][:, kk, cols],
                                        self.lo[s][:, kk, cols], x_hi[:, k, :], x_lo[:, k, :], k == 0, k == KT - 1)
            mm.then_inc(self.units_used, 1)

    def tokens(self, pe, n, par, banks, x_hi, x_lo, banks_free):
        pe.wait_ge(banks_free, n + 1)
        for s in range(2):
            self.wait_unit(pe, s, n)
            for t in range(TT):
                for kk in range(HALF):
                    k = HALF * s + kk
                    rows = slice(t * P, (t + 1) * P)
                    mm = three_products(self.nc, banks[:, 4 * par + t, :], x_hi[:, k, rows], x_lo[:, k, rows],
                                        self.hi[s][:, kk, :], self.lo[s][:, kk, :], k == 0, k == KT - 1)
            mm.then_inc(self.units_used, 1)


class StepSizes:

    def __init__(self, nc, sb, sem, soft, raw, bias_row, a_log_row, n_heads, dt, adt):
        self.nc, self.raw, self.bias_row, self.a_log_row, self.dt, self.adt = nc, raw, bias_row, a_log_row, dt, adt
        self.shape = [P, TT, n_heads]
        self.soft = soft
        self.a_exp = sb("a_exp", [P, n_heads])
        self.own_s = sem("soft_step")
        self.abs_ok = sem("abs_ok")
        self.exp_ok = sem("exp_ok")

    def start(self, dve):
        nc, x = self.nc, self.soft[:, 0]
        self.own = own = Own(dve, self.own_s)
        own.did(nc.vector.tensor_tensor(x, self.raw, self.bias_row.unsqueeze(1).broadcast_to(self.shape), ALU.add))
        own.wait()
        nc.vector.scalar_tensor_tensor(out=self.soft[:, 1], in0=x, scalar=-1.0, in1=x, op0=ALU.mult, op1=ALU.max)\
            .then_inc(self.abs_ok, 1)

    def exponentials(self, act):
        act.wait_ge(self.abs_ok, 1)
        self.nc.scalar.activation(self.soft[:, 2], self.soft[:, 1], ACT.Exp, scale=-1.0).then_inc(self.exp_ok, 1)
        self.nc.scalar.activation(self.a_exp[:], self.a_log_row, ACT.Exp).then_inc(self.exp_ok, 1)

    def finish(self, dve):
        nc, own = self.nc, self.own
        x, _, u, z, z2, q = (self.soft[:, n] for n in range(6))
        dve.wait_ge(self.exp_ok, 2)
        own.did(nc.vector.tensor_scalar(q, u, 2.0, None, ALU.add))
        own.wait()
        own.did(nc.vector.reciprocal(z2, q))
        own.wait()
        own.did(nc.vector.tensor_tensor(z, u, z2, ALU.mult))
        own.wait()
        own.did(nc.vector.tensor_tensor(z2, z, z, ALU.mult))
        own.wait()
        series = log1p_series()
        own.did(nc.vector.tensor_scalar(q, z2, series[-1], None, ALU.mult))
        for c in reversed(series[:-1]):
            own.wait()
            own.did(nc.vector.scalar_tensor_tensor(out=q, in0=q, scalar=c, in1=z2, op0=ALU.add, op1=ALU.mult))
        own.wait()
        own.did(nc.vector.scalar_tensor_tensor(out=q, in0=q, scalar=1.0, in1=z, op0=ALU.add, op1=ALU.mult))
        own.wait()
        own.did(nc.vector.tensor_scalar(q, q, 2.0, None, ALU.mult))
        own.wait()
        own.did(nc.vector.scalar_tensor_tensor(out=self.dt, in0=x, scalar=0.0, in1=q, op0=ALU.max, op1=ALU.add))
        own.wait()
        own.did(nc.vector.scalar_tensor_tensor(out=self.adt, in0=self.dt, scalar=-1.0,
                                               in1=self.a_exp[:].unsqueeze(1).broadcast_to(self.shape),
                                               op0=ALU.mult, op1=ALU.mult))


def projections1(nc, a, ahead, raw, masks, small, cond, resid, qk, tok, xbc, dt, adt):
    w_in = a["w_in"][0].rearrange("(k p) c -> p k c", p=P)
    xT = a["xT"].rearrange("(k p) t -> p k t", p=P)
    B_QK, B_V, B_X, B_Z = 4, 2, D_CONV1 // COLS, 4
    N_X = B_QK + B_V
    N_Z = N_X + B_X
    ctx = Phase(nc, "projections1")
    with ctx:
        sb, sem = ctx.sb, ctx.sem
        w = WeightStream(nc, sem, sb, raw, ahead, 1)
        x_hi = sb("x_hi", [P, KT, SEQ], F32R)
        x_lo = sb("x_lo", [P, KT, SEQ], F32R)
        wdt = sb("wdt", [P, KT, SSM_HEADS])
        wdt_hi = sb("wdt_hi", [P, KT, SSM_HEADS], F32R)
        wdt_lo = sb("wdt_lo", [P, KT, SSM_HEADS], F32R)
        dt_raw = sb("dt_raw", [P, TT, SSM_HEADS])
        x_st = resid[:].rearrange("p t (k c) -> p (t k) c", c=SEQ)
        XP = 4
        KP = KT // XP
        cw = sb("cw", [P, CT1, CONV + 1])
        pre, acc, soft, rows = spare_buffers(resid)
        ps = ctx.psum("ps1", [P, 8, COLS], F32)
        banks_free = sem("banks_free")
        consts_in = sem("consts_in")
        cond_ok = sem("cond_ok")
        x_in = [sem(f"x_in{i}") for i in range(XP)]
        wdt_in = sem("wdt_in")
        x_hi_ok = sem("x_hi_ok")
        x_lo_ok = sem("x_lo_ok")
        dt_split = sem("dt_split")
        dt_made = sem("dt_made")
        dt_out = sem("dt_out")
        zeroed = sem("zeroed")
        conv = ConvStream(nc, sem, pre, acc, cw, ps, xbc, True)
        steps = StepSizes(nc, sb, sem, soft, dt_raw[:], small[:, 0:SSM_HEADS], small[:, SSM_HEADS:2 * SSM_HEADS], SSM_HEADS,
                          dt[:], adt[:])

        block = ctx.enter_context(nc.Block())

        @block.sync
        def _(sp):
            for i in range(XP):
                sp.dma_start(x_st[:, KP * i:KP * (i + 1), :], xT[:, KP * i:KP * (i + 1), :]).then_inc(x_in[i], 16)
                if i == 0:
                    with nc.allow_non_contiguous_dma(reason="16 columns of w_in"):
                        sp.dma_start(wdt[:], w_in[:, :, COL_DT:COL_DT + SSM_HEADS]).then_inc(wdt_in, 16)

            def load(n, col):
                for s in range(2):
                    w.load(sp, s, n, w_in[:, HALF * s:HALF * (s + 1), bass.ds(col, COLS)])

            w.load_ahead(sp, ahead, [r[:] for r in raw], w_in)
            sp.dma_start(masks[:], a["masks"]).then_inc(consts_in, 16)
            sp.dma_start(small[:], a["small"].partition_broadcast(P)).then_inc(consts_in, 16)
            sp.dma_start(cw[:], a["conv1"]).then_inc(consts_in, 16)
            sp.dma_start(cond[:], a["c"]).then_inc(consts_in, 16)
            with nc.sync.Fori(1, B_QK + B_V) as n:
                load(n, n * COLS)
            with nc.sync.Fori(0, B_X) as j:
                load(j + N_X, j * COLS + COL_XBC)
            with nc.sync.Fori(0, B_Z) as j:
                load(j + N_Z, j * COLS + (B_QK + B_V) * COLS)

        @block.scalar
        def _(act):
            for i in range(XP):
                ks = slice(KP * i, KP * (i + 1))
                act.wait_ge(x_in[i], 16)
                nc.scalar.activation(x_hi[:, ks, :], x_st[:, ks, :], ACT.Copy).then_inc(x_hi_ok, 1)
                if i == 0:
                    act.wait_ge(wdt_in, 16)
                    nc.scalar.activation(wdt_hi[:], wdt[:], ACT.Copy).then_inc(dt_split, 1)

            def round_block(n):
                for s in range(2):
                    w.round(act, s, n)

            def read_out(n, par, dst, func):
                act.wait_ge(w.units_used, n * 2 + 4)
                nc.scalar.activation(dst, ps[:, 4 * par:4 * par + 4, :], func).then_inc(banks_free, 1)

            w.round(act, 0, 0)
            act.wait_ge(dt_made, 1)
            nc.scalar.activation(rows[0:SSM_HEADS, :], ps[0:SSM_HEADS, 7, :], ACT.Copy).then_inc(dt_out, 1)
            w.round(act, 1, 0)
            act.wait_ge(dt_made, 2)
            nc.scalar.activation(dt_raw[:], ps[:, 6, 0:TT * SSM_HEADS].rearrange("p (t h) -> p t h", t=TT), ACT.Copy)\
                .then_inc(dt_out, 1)
            act.wait_ge(dt_out, 2)
            act.sem_inc(banks_free, 1)
            act.wait_ge(consts_in, 64)
            nc.scalar.activation(cond[:], cond[:], ACT.Silu).then_inc(cond_ok, 1)
            with nc.scalar.Fori(0, B_QK // 2) as i:
                for par in range(2):
                    round_block(i * 2 + (par + 1))
                    read_out(i * 2 + par, par, qk[:, bass.ds((i * 2 + par) * 4, 4), :], ACT.Copy)
            steps.exponentials(act)
            for par in range(2):
                round_block(B_QK + par + 1)
                read_out(B_QK + par, par, tok[:, :, par * COLS:(par + 1) * COLS], ACT.Copy)
            act.wait_ge(zeroed, 1)
            act.sem_inc(conv.conv_done, 2)
            for b in range(B_X):
                n = N_X + b
                round_block(n + 1)
                act.wait_ge(w.units_used, 2 * n + 4)
                conv.read_and_silu(act, b, n % 2, banks_free)
            with nc.scalar.Fori(0, B_Z // 2 - 1) as i:
                for j in range(2):
                    round_block(i * 2 + (N_Z + j + 1))
                    read_out(i * 2 + (N_Z + j), (N_Z + j) % 2,
                             tok[:, :, bass.ds(i * (2 * COLS) + (B_V + j) * COLS, COLS)], ACT.Silu)
            round_block(N_Z + B_Z - 1)
            read_out(N_Z + B_Z - 2, (N_Z + B_Z) % 2, tok[:, :, 4 * COLS:5 * COLS], ACT.Silu)
            read_out(N_Z + B_Z - 1, (N_Z + B_Z - 1) % 2, tok[:, :, 5 * COLS:6 * COLS], ACT.Silu)

        @block.vector
        def _(dve):
            dve.sem_inc(w.lo_ready, 2)
            for i in range(XP):
                ks = slice(KP * i, KP * (i + 1))
                dve.wait_ge(x_hi_ok, i + 1)
                nc.vector.tensor_tensor(x_lo[:, ks, :], x_st[:, ks, :], x_hi[:, ks, :], ALU.subtract)\
                    .then_inc(x_lo_ok, 1)
                if i == 0:
                    dve.wait_ge(dt_split, 1)
                    nc.vector.tensor_tensor(wdt_lo[:], wdt[:], wdt_hi[:], ALU.subtract).then_inc(dt_split, 1)
            for s in range(2):
                w.rest(nc.vector, dve, s, 0)
            dve.wait_ge(x_lo_ok, XP)
            nc.vector.memset(pre, 0.0).then_inc(zeroed, 1)
            for s in range(2):
                w.rest(nc.vector, dve, s, 1)
            dve.wait_ge(dt_out, 2)
            dve.wait_ge(consts_in, 64)
            steps.start(dve)
            with nc.vector.Fori(2, N_X + 1) as n:
                for s in range(2):
                    w.rest(nc.vector, dve, s, n)
            steps.finish(dve)
            dve.sem_inc(conv.taps_done, 2)
            for b in range(B_X):
                for s in range(2):
                    w.rest(nc.vector, dve, s, N_X + 1 + b)
                conv.sum_taps(dve, b)
            with nc.vector.Fori(N_Z + 1, N_Z + B_Z) as n:
                for s in range(2):
                    w.rest(nc.vector, dve, s, n)

        @block.tensor
        def _(pe):
            pe.sem_inc(w.units_used, 2)
            pe.sem_inc(banks_free, 1)
            pe.wait_ge(dt_split, 2)
            for k in range(KT):
                if k % KP == 0:
                    pe.wait_ge(x_lo_ok, k // KP + 1)
                mm = three_products(nc, ps[0:SSM_HEADS, 7, :], wdt_hi[:, k, :], wdt_lo[:, k, :], x_hi[:, k, :],
                                    x_lo[:, k, :], k == 0, k == KT - 1)
            mm.then_inc(dt_made, 1)
            pe.wait_ge(dt_out, 1)
            pe.wait_ge(consts_in, 64)
            for t in range(TT):
                tr = nc.tensor.transpose(ps[:, 6, t * SSM_HEADS:(t + 1) * SSM_HEADS], rows[0:SSM_HEADS, t * P:(t + 1) * P],
                                         masks[0:SSM_HEADS, IDENT, 0:SSM_HEADS])
            tr.then_inc(dt_made, 1)
            with nc.tensor.Fori(0, B_QK // 2) as i:
                for par in range(2):
                    w.channels(pe, i * 2 + par, par, ps, x_hi, x_lo, banks_free)
            for par in range(2):
                w.tokens(pe, B_QK + par, par, ps, x_hi, x_lo, banks_free)
            for b in range(B_X):
                w.channels(pe, N_X + b, (N_X + b) % 2, ps, x_hi, x_lo, banks_free)
            with nc.tensor.Fori(0, B_Z // 2) as i:
                for j in range(2):
                    w.tokens(pe, i * 2 + (N_Z + j), (N_Z + j) % 2, ps, x_hi, x_lo, banks_free)


def attention(nc, a, resid, raw, masks, cond, qk, tok, pool_dmas):
    ctx = Phase(nc, "attention")
    with ctx:
        sb, sem = ctx.sb, ctx.sem
        ident = masks[:, IDENT, :]
        q_pad = sb("q_pad", [P, 2, 2, SEQ])
        k_st = sb("k_st", [P, 2, SEQ])
        v_st = sb("v_st", [P, 2, TT, P])
        bias = sb("bias", [P, 4, SEQ])
        probs = sb("probs", [P, 4, S_LEN])
        probsT = sb("probsT", [P, 2, S_LEN])
        maxes = sb("maxes", [P, 4, TT])
        negmax = sb("negmax", [P, 4, TT])
        sums = sb("sums", [P, 4, TT])
        recip = sb("recip", [P, 2, TT])
        y_raw = sb("y_raw", [P, 2, TT, HD])
        ps_s = ctx.psum("ps_s", [P, 3 * 512], F32)
        ps_t = ctx.psum("ps_t", [P, 3 * 512], F32)
        ps_o = ctx.psum("ps_o", [P, 2, TT, P], F32)
        zeroed = sem("zeroed")
        qk_in = [sem(f"qk_in{i}") for i in range(2)]
        v_in = [sem(f"v_in{i}") for i in range(2)]
        bias_in = [sem(f"bias_in{i}") for i in range(4)]
        scored = sem("scored")
        biased = sem("biased")
        negmax_ok = sem("negmax_ok")
        exped = sem("exped")
        turned = sem("turned")
        turned_out = sem("turned_out")
        valued = sem("valued")
        recip_ok = sem("recip_ok")
        y_norm = sem("y_norm")
        y_done = sem("y_done")
        gate = sem("gate")
        mod_acc = resid[:].rearrange("p t d -> p (t d)")[:, 0:3 * D_MODEL]
        ada = [raw[i][:].rearrange("p k c -> p (k c)")[:, 0:MOD_COLS] for i in range(2)]
        ada_in = pool_dmas
        mod_step = sem("mod_step")
        mod_scaled = sem("mod_scaled")
        mod_gate = sem("mod_gate")
        ITER = ATT_HEADS // 4

        block = ctx.enter_context(nc.Block())

        @block.sync
        def _(sp):
            def stage_qk(j, slot):
                sp.dma_start(q_pad[0:64, slot, 0, :], qk[0:64, bass.ds(j, 1), :]).then_inc(qk_in[slot], 16)
                sp.dma_start(q_pad[64:128, slot, 1, :], qk[64:128, bass.ds(j, 1), :]).then_inc(qk_in[slot], 16)
                sp.dma_start(k_st[:, slot, :], qk[:, bass.ds(j + 8, 1), :]).then_inc(qk_in[slot], 16)

            def stage_v(j, slot):
                sp.dma_start(v_st[:, slot, :, :], tok[:, :, bass.ds(j * P, P)]).then_inc(v_in[slot], 16)

            def stage_bias(h, slot):
                sp.dma_start(bias[:, slot, :], a["att_bias"][bass.ds(h, 1)].rearrange("o p c -> p (o c)"))\
                  .then_inc(bias_in[slot], 16)

            stage_qk(0, 0)
            for h in range(2):
                stage_bias(h, h)
            stage_qk(1, 1)
            for h in range(2, 4):
                stage_bias(h, h)
            for j in range(2):
                stage_v(j, j)
            with nc.sync.Fori(1, ITER) as i:
                for pp in range(2):
                    sp.wait_ge(scored, i * 16 + (8 * pp - 8))
                    stage_qk(i * 2 + pp, pp)
                    sp.wait_ge(biased, i * 16 + (8 * pp - 8))
                    for hh in (2 * pp, 2 * pp + 1):
                        stage_bias(i * 4 + hh, hh)
                    sp.wait_ge(valued, i * 4 + 2 * pp)
                    stage_v(i * 2 + pp, pp)

        def query_tiles():
            return (3, 2, 0, 1)

        @block.tensor
        def _(pe):
            def scores(i, hh, first=False):
                slot = hh // 2
                pe.wait_ge(qk_in[slot], i * 48 + 48)
                if not first:
                    pe.wait_ge(biased, i * 16 + 4 * hh)
                for qt in query_tiles():
                    keys = (qt + 1) * P
                    nc.tensor.matmul(ps_s[:, S_OFF[qt]:S_OFF[qt] + keys],
                                     q_pad[:, slot, hh % 2, qt * P:(qt + 1) * P], k_st[:, slot, 0:keys],
                                     start=True, stop=True).then_inc(scored, 1)

            def turn(i, hh):
                for n, tiles in enumerate(((3,), (2, 0), (1,))):
                    pe.wait_ge(turned_out, i * 12 + (3 * hh + n + 1))
                    for qt in tiles:
                        pe.wait_ge(exped, i * 16 + (4 * hh + 1 + query_tiles().index(qt)))
                        for kt in range(qt + 1):
                            at = S_OFF[qt] + kt * P
                            tr = nc.tensor.transpose(ps_t[:, at:at + P], probs[:, hh, at:at + P], ident)
                    tr.then_inc(turned, 1)

            def values(i, hh):
                pe.wait_ge(v_in[hh // 2], i * 16 + 16)
                pe.wait_ge(y_norm, i * 4 + (hh + 1))
                for n, tiles in enumerate(((3,), (2, 0), (1,))):
                    pe.wait_ge(turned_out, i * 12 + (3 * hh + n + 4))
                    for qt in tiles:
                        for kt in range(qt + 1):
                            at = S_OFF[qt] + kt * P
                            mm = nc.tensor.matmul(ps_o[:, hh % 2, qt, :], probsT[:, hh % 2, at:at + P],
                                                  v_st[:, hh // 2, kt, :], start=(kt == 0), stop=(kt == qt))
                mm.then_inc(valued, 1)

            pe.wait_ge(zeroed, 4)
            scores(0, 0, first=True)
            scores(0, 1)

            def heads(i, last):
                for hh in range(4):
                    turn(i, hh)
                    if hh < 2:
                        scores(i, hh + 2)
                    elif not last:
                        scores(i + 1, hh - 2)
                    values(i, hh)

            with nc.tensor.Fori(0, ITER - 1) as i:
                heads(i, False)
            heads(ITER - 1, True)

        @block.gpsimd
        def _(pool):
            for part in range(2):
                nc.gpsimd.memset(mod_acc[:, part * MOD_COLS:(part + 1) * MOD_COLS], 0.0).then_inc(mod_step, 1)
            rows = a["ada_w"][0].rearrange("(k p) c -> p k c", p=P)

            def load(k, part):
                pool.dma_start(ada[part], rows[:, bass.ds(k, 1), part * MOD_COLS:(part + 1) * MOD_COLS]
                               .rearrange("p k c -> p (k c)")).then_inc(ada_in[part], 16)

            def add(k, part):
                pool.wait_ge(mod_scaled, k * 2 + (part + 1))
                pool.wait_ge(mod_step, k * 2 + (part + 1))
                acc = mod_acc[:, part * MOD_COLS:(part + 1) * MOD_COLS]
                nc.gpsimd.tensor_tensor(acc, acc, ada[part], ALU.add).then_inc(mod_step, 1)

            for part in range(2):
                load(0, part)
            with nc.gpsimd.Fori(0, KT - 1) as k:
                for part in range(2):
                    add(k, part)
                    pool.wait_ge(mod_step, k * 2 + (part + 3))
                    load(k + 1, part)
            for part in range(2):
                add(KT - 1, part)

        @block.vector
        def _(dve):
            for slot in range(2):
                nc.vector.memset(q_pad[64:128, slot, 0, :], 0.0).then_inc(zeroed, 1)
                nc.vector.memset(q_pad[0:64, slot, 1, :], 0.0).then_inc(zeroed, 1)
            dve.sem_inc(turned_out, 3)
            dve.sem_inc(y_norm, 2)

            def add_bias(i, hh):
                dve.wait_ge(bias_in[hh], i * 16 + 16)
                dve.wait_ge(turned, i * 12 + (3 * hh + 3))
                for n, qt in enumerate(query_tiles()):
                    dve.wait_ge(scored, i * 16 + (4 * hh + (3 if n == 1 else n + 1)))
                    dve.sem_inc(gate, 1)
                    keys = (qt + 1) * P
                    at = S_OFF[qt]
                    nc.vector.tensor_tensor_reduce(
                        probs[:, hh, at:at + keys], ps_s[:, at:at + keys], bias[:, hh, SEQ - keys:SEQ],
                        QK_SCALE, -3e38, ALU.add, ALU.max, maxes[:, hh, qt:qt + 1]).then_inc(biased, 1)
                dve.wait_ge(biased, i * 16 + (4 * hh + 4))
                nc.vector.tensor_scalar(negmax[:, hh, :], maxes[:, hh, :], -1.0, None, ALU.mult).then_inc(negmax_ok, 1)

            def turned_to_sbuf(i, hh):
                for n, (at, size) in enumerate(((512, 512), (0, 512), (1024, 256))):
                    dve.wait_ge(turned, i * 12 + (3 * hh + n + 13))
                    if n == 0:
                        dve.wait_ge(valued, i * 4 + (hh + 1))
                    nc.vector.tensor_copy(probsT[:, hh % 2, at:at + size], ps_t[:, at:at + size])\
                        .then_inc(turned_out, 1)

            def finish(i, hh):
                col = (i * 4 + hh) * HD + 1024
                dve.wait_ge(valued, i * 4 + (hh + 3))
                nc.vector.reciprocal(recip[:, hh % 2, :], sums[:, hh, :]).then_inc(recip_ok, 1)
                dve.wait_ge(recip_ok, i * 4 + (hh + 5))
                half = (hh % 2) * HD
                nc.vector.tensor_tensor(y_raw[:, hh % 2, :, :], ps_o[:, hh % 2, :, half:half + HD],
                                        recip[:, hh % 2, :].unsqueeze(2).broadcast_to([P, TT, HD]),
                                        ALU.mult).then_inc(y_norm, 1)
                dve.wait_ge(y_norm, i * 4 + (hh + 3))
                y = tok[:, :, bass.ds(col, HD)]
                nc.vector.tensor_tensor(y, y_raw[:, hh % 2, :, :], y, ALU.mult).then_inc(y_done, 1)

            add_bias(0, 0)
            add_bias(0, 1)

            def heads(i, last):
                for hh in range(4):
                    turned_to_sbuf(i, hh)
                    if hh < 2:
                        add_bias(i, hh + 2)
                    elif not last:
                        add_bias(i + 1, hh - 2)
                    finish(i, hh)

            with nc.vector.Fori(0, ITER - 1) as i:
                heads(i, False)
            heads(ITER - 1, True)

        @block.scalar
        def _(act):
            act.sem_inc(turned, 12)
            act.sem_inc(valued, 2)
            act.sem_inc(recip_ok, 4)

            def exponentials(i, hh):
                act.wait_ge(negmax_ok, i * 4 + (hh + 1))
                for n, qt in enumerate(query_tiles()):
                    keys = (qt + 1) * P
                    at = S_OFF[qt]
                    if n == 0:
                        act.wait_ge(recip_ok, i * 4 + (hh + 1))
                    nc.scalar.activation(probs[:, hh, at:at + keys], probs[:, hh, at:at + keys], ACT.Exp,
                                         bias=negmax[:, hh, qt:qt + 1],
                                         accum_out=sums[:, hh, qt:qt + 1]).then_inc(exped, 1)

            with nc.scalar.Fori(0, ITER) as i:
                for hh in range(4):
                    exponentials(i, hh)
                    part, k = hh % 2, i * 2 + hh // 2
                    act.wait_ge(ada_in[part], k * 16 + 16)
                    act.sem_inc(mod_gate, 1)
                    nc.scalar.activation(ada[part], ada[part], ACT.Copy,
                                         scale=cond[:, bass.ds(k, 1)]).then_inc(mod_scaled, 1)


def ssd(nc, a, ahead, raw, att_f, masks, small, tok, xbc, dt, adt):
    ctx = Phase(nc, "ssd")
    with ctx:
        sb, sem = ctx.sb, ctx.sem
        G, GW = SSM_GROUPS, HPG * HD
        ident, upper, below, ones = (masks[:, m, :] for m in (IDENT, UPPER, BELOW, ONES))
        decays = sb("decays", [P, 3, TT, SSM_HEADS])
        stage = sb("stage", [P, G, 6, P])
        c_st = sb("c_st", [P, G, P])
        steps_in = sb("steps_in", [P, G, HPG, P])
        E = sb("E", [P, G, HPG, P])
        M = sb("M", [P, G, HPG, P])
        cb = sb("cb", [P, G, P])
        xs_tok = sb("xs_tok", [P, G, HPG, HD])
        b_tok = sb("b_tok", [P, G, P])
        xdt = sb("xdt", [P, G, HPG, HD])
        xdte = sb("xdte", [P, G, HPG, HD])
        xskip = sb("xskip", [P, G, HPG, HD])
        state = sb("state", [P, G, HPG, HD])
        y = sb("y", [P, G, HPG, HD])
        ps_x = ctx.psum("ps_x", [P, HPG, HD], F32)
        ps_c = ctx.psum("ps_c", [P, 4, P], F32)
        ps_seg = ctx.psum("ps_seg", [P, HPG, P], F32)
        ps_yd = ctx.psum("ps_yd", [P, HPG, P], F32)
        ps_yo = ctx.psum("ps_yo", [P, HPG, HD], F32)
        ps_st = ctx.psum("ps_st", [P, HPG, HD], F32)
        junk = sb("junk", [P, D_MODEL])
        half_neg = sb("half_neg", [P, TT])
        att_sq = sem("att_sq")
        att_step = sem("att_step")
        sums_ok = sem("sums_ok")
        decays_ok = sem("decays_ok")
        ab_in = [sem(f"ab_in{g}") for g in range(G)]
        c_in = [sem(f"c_in{g}") for g in range(G)]
        steps_ok = sem("steps_ok")
        xs_turned = sem("xs_turned")
        cb_made = sem("cb_made")
        seg_made = sem("seg_made")
        xs_out = sem("xs_out")
        b_out = sem("b_out")
        e_ok = sem("e_ok")
        cb_ok = sem("cb_ok")
        m_ok = sem("m_ok")
        xdt_ok = sem("xdt_ok")
        xdte_ok = sem("xdte_ok")
        xskip_ok = sem("xskip_ok")
        gate, gate_a = sem("gate"), sem("gate_a")
        yd_made = sem("yd_made")
        yo_made = sem("yo_made")
        st_made = sem("st_made")
        y_step = sem("y_step")
        st_step = sem("st_step")

        block = ctx.enter_context(nc.Block())

        def head_row(values):
            return values.unsqueeze(2).broadcast_to([P, HPG, HD])

        @block.sync
        def _(sp):
            def stage_ab(c, g):
                at = bass.ds(c * P, P)
                sp.dma_start(stage[:, g, 0:4, :], xbc[:, 4 * g:4 * g + 4, at]).then_inc(ab_in[g], 16)
                sp.dma_start(stage[:, g, 4:6, :], xbc[:, 8 + g:12:2, at]).then_inc(ab_in[g], 16)

            def stage_c(c, g):
                sp.dma_start(c_st[:, g, :], xbc[:, 10 + g, bass.ds(c * P, P)]).then_inc(c_in[g], 16)

            for g in range(G):
                stage_ab(0, g)
                stage_c(0, g)
            WeightStream.load_ahead(sp, ahead, [r[:] for r in raw], a["w_out"][0].rearrange("(k p) c -> p k c", p=P))
            with nc.sync.Fori(1, TT) as c:
                for g in range(G):
                    sp.wait_ge(cb_made, c * 2 + (g - 1))
                    stage_ab(c, g)
                    sp.wait_ge(yo_made, c * 2 + (g - 1))
                    stage_c(c, g)

        @block.tensor
        def _(pe):
            flat = adt[:].rearrange("p c h -> p (c h)")
            for n, mask in enumerate((upper, below, ones)):
                mm = nc.tensor.matmul(ps_c[:, n, 0:TT * SSM_HEADS], mask, flat, start=True, stop=True)
            mm.then_inc(sums_ok, 1)
            pe.wait_ge(decays_ok, 1)
            pe.sem_inc(st_made, G)
            pe.sem_inc(yd_made, G)
            pe.sem_inc(seg_made, G)

            def ahead(c, g):
                pe.wait_ge(ab_in[g], c * 32 + 32)
                pe.wait_ge(xs_out, c * 2 + (g + 1))
                for t in range(4):
                    tr = nc.tensor.transpose(ps_x[:, 2 * t:2 * t + 2, :].rearrange("p a b -> p (a b)"),
                                             stage[:, g, t, :], ident)
                tr.then_inc(xs_turned, 1)
                pe.wait_ge(b_out, c * 2 + (g + 1))
                pe.wait_ge(cb_ok, c * 2 + (g + 1))
                nc.tensor.transpose(ps_c[:, 0, :], stage[:, g, 4, :], ident)
                nc.tensor.matmul(ps_c[:, 1, :], stage[:, g, 4, :], stage[:, g, 5, :], start=True, stop=True)\
                    .then_inc(cb_made, 1)
                pe.wait_ge(steps_ok, c * 2 + (g + 1))
                pe.wait_ge(e_ok, c * 2 + (g + 1))
                for n in range(2):
                    mm = nc.tensor.matmul(ps_seg[:, 4 * n:4 * n + 4, :].rearrange("p a b -> p (a b)"), below,
                                          steps_in[:, g, 4 * n:4 * n + 4, :].rearrange("p a b -> p (a b)"),
                                          start=True, stop=True)
                mm.then_inc(seg_made, 1)

            def outputs(c, g, last=False):
                pe.wait_ge(c_in[g], c * 16 + 16)
                pe.wait_ge(st_step, c * 4 + (2 * g + 2))
                pe.wait_ge(y_step, c * 8 + (4 * g + 5))
                nc.tensor.matmul(ps_yo[:].rearrange("p a b -> p (a b)"), c_st[:, g, :],
                                 state[:, g, :, :].rearrange("p a b -> p (a b)"), start=True, stop=True)\
                    .then_inc(yo_made, 1)
                if not last:
                    pe.wait_ge(b_out, c * 2 + (g + 2))
                    pe.wait_ge(xdte_ok, c * 2 + (g + 3))
                    pe.wait_ge(st_step, c * 4 + (2 * g + 4))
                    nc.tensor.matmul(ps_st[:].rearrange("p a b -> p (a b)"), b_tok[:, g, :],
                                     xdte[:, g, :, :].rearrange("p a b -> p (a b)"), start=True, stop=True)\
                        .then_inc(st_made, 1)
                pe.wait_ge(m_ok, c * 2 + (g + 3))
                for h in range(HPG):
                    pair = xdt[:, g, h - h % 2:h - h % 2 + 2, :].rearrange("p a b -> p (a b)")
                    mm = nc.tensor.matmul(ps_yd[:, h, :], M[:, g, h, :], pair, start=True, stop=True)
                mm.then_inc(yd_made, 1)

            ahead(0, 0)
            with nc.tensor.Fori(0, TT - 1) as c:
                ahead(c, 1)
                outputs(c, 0)
                ahead(c + 1, 0)
                outputs(c, 1)
            ahead(TT - 1, 1)
            outputs(TT - 1, 0, last=True)
            outputs(TT - 1, 1, last=True)

        @block.scalar
        def _(act):
            act.wait_ge(sums_ok, 1)
            nc.scalar.activation(decays[:].rearrange("p n c h -> p n (c h)"), ps_c[:, 0:3, 0:TT * SSM_HEADS],
                                 ACT.Exp).then_inc(decays_ok, 1)
            act.wait_ge(decays_ok, 1)
            act.sem_inc(xs_out, 1)
            act.sem_inc(b_out, 1)
            act.sem_inc(e_ok, 1)
            act.sem_inc(att_sq, 1)
            with nc.scalar.Fori(0, TT) as c:
                for g in range(G):
                    act.wait_ge(xs_turned, c * 2 + (g + 1))
                    act.wait_ge(xskip_ok, c * 2 + (g + 1))
                    act.wait_ge(xdt_ok, c * 2 + (g + 1))
                    nc.scalar.activation(xs_tok[:, g], ps_x[:], ACT.Copy).then_inc(xs_out, 1)
                    act.wait_ge(cb_made, c * 2 + (g + 1))
                    act.wait_ge(st_made, c * 2 + (g + 1))
                    nc.scalar.activation(b_tok[:, g, :], ps_c[:, 0, :], ACT.Copy).then_inc(b_out, 1)
                    act.wait_ge(seg_made, c * 2 + (g + 3))
                    act.wait_ge(m_ok, c * 2 + (g + 1))
                    nc.scalar.activation(E[:, g], ps_seg[:], ACT.Exp).then_inc(e_ok, 1)
                act.wait_ge(att_sq, c + 1)
                act.sem_inc(gate_a, 1)
                nc.scalar.activation(junk[:], tok[:, bass.ds(c, 1), D_MODEL:2 * D_MODEL].rearrange("p c d -> p (c d)"),
                                     ACT.Square, accum_out=att_f[:, bass.ds(c, 1)]).then_inc(att_sq, 1)
            act.wait_ge(att_step, 3)
            for t in range(TT):
                rows = tok[:, t, D_MODEL:2 * D_MODEL]
                nc.scalar.activation(rows, rows, ACT.Copy, scale=att_f[:, t:t + 1])

        @block.vector
        def _(dve):
            nc.vector.memset(state[:], 0.0).then_inc(st_step, 1)
            dve.sem_inc(cb_ok, 1)
            dve.sem_inc(m_ok, G)
            dve.sem_inc(xdt_ok, G)
            dve.sem_inc(y_step, 7)
            dve.sem_inc(st_step, 3)
            dve.wait_ge(decays_ok, 1)

            def chunk_heads(values, c, g):
                return values[:, bass.ds(c, 1), g * HPG:(g + 1) * HPG].rearrange("p c h -> p (c h)")

            def ahead(c, g):
                dve.wait_ge(xs_out, c * 2 + (g + 2))
                dve.wait_ge(yd_made, c * 2 + (g + 1))
                dve.wait_ge(xdte_ok, c * 2 + (g + 1))
                nc.vector.tensor_tensor(xdt[:, g], xs_tok[:, g], head_row(chunk_heads(dt, c, g)), ALU.mult)\
                    .then_inc(xdt_ok, 1)
                dve.wait_ge(b_out, c * 2 + (g + 2))
                dve.wait_ge(m_ok, c * 2 + (g + 1))
                nc.vector.tensor_tensor(cb[:, g, :], ps_c[:, 1, :], upper, ALU.mult).then_inc(cb_ok, 1)
                dve.wait_ge(cb_ok, c * 2 + (g + 2))
                dve.wait_ge(e_ok, c * 2 + (g + 2))
                nc.vector.tensor_tensor(M[:, g], E[:, g], cb[:, g, :].unsqueeze(1).broadcast_to([P, HPG, P]),
                                        ALU.mult).then_inc(m_ok, 1)

            def outputs(c, g, last=False):
                dve.wait_ge(yo_made, c * 2 + (g + 1))
                nc.vector.tensor_tensor(y[:, g], ps_yo[:], head_row(chunk_heads(decays[:, 0], c, g)), ALU.mult)\
                    .then_inc(y_step, 1)
                if not last:
                    nc.vector.tensor_tensor(state[:, g], state[:, g], head_row(chunk_heads(decays[:, 2], c, g)), ALU.mult)\
                        .then_inc(st_step, 1)
                dve.wait_ge(yd_made, c * 2 + (g + 3))
                dve.wait_ge(y_step, c * 8 + (4 * g + 8))
                own_half = ps_yd[:].rearrange("p h c -> p (h c)").rearrange("p (q j c) -> p q j c", j=4, c=HD)[:, :, 0:4:3, :]
                nc.vector.tensor_tensor(y[:, g].rearrange("p (q j) c -> p q j c", j=2),
                                        own_half, y[:, g].rearrange("p (q j) c -> p q j c", j=2), ALU.add)\
                    .then_inc(y_step, 1)
                if not last:
                    dve.wait_ge(st_made, c * 2 + (g + 3))
                    dve.wait_ge(st_step, c * 4 + (2 * g + 5))
                    nc.vector.tensor_tensor(state[:, g], ps_st[:], state[:, g], ALU.add).then_inc(st_step, 1)
                dve.wait_ge(xskip_ok, c * 2 + (g + 3))
                dve.wait_ge(y_step, c * 8 + (4 * g + 9))
                nc.vector.tensor_tensor(y[:, g], y[:, g], xskip[:, g], ALU.add).then_inc(y_step, 1)
                z = tok[:, bass.ds(c, 1), 2048 + g * GW:2048 + (g + 1) * GW].rearrange("p c (h e) -> p (c h) e", h=HPG)
                dve.wait_ge(y_step, c * 8 + (4 * g + 10))
                nc.vector.tensor_tensor(z, y[:, g], z, ALU.mult).then_inc(y_step, 1)

            ahead(0, 0)
            with nc.vector.Fori(0, TT - 1) as c:
                ahead(c, 1)
                outputs(c, 0)
                ahead(c + 1, 0)
                outputs(c, 1)
            ahead(TT - 1, 1)
            outputs(TT - 1, 0, last=True)
            outputs(TT - 1, 1, last=True)

        @block.gpsimd
        def _(pool):
            pool.sem_inc(xskip_ok, G)
            pool.sem_inc(xdte_ok, G)
            pool.wait_ge(decays_ok, 1)

            def step(c, g):
                heads = slice(g * HPG, (g + 1) * HPG)
                pool.wait_ge(seg_made, c * 2 + (g + 1))
                pool.sem_inc(gate, 1)
                a_row = adt[:, bass.ds(c, 1), heads].rearrange("p c h -> p (c h)")
                nc.gpsimd.tensor_tensor(steps_in[:, g], upper.unsqueeze(1).broadcast_to([P, HPG, P]),
                                        a_row.unsqueeze(2).broadcast_to([P, HPG, P]), ALU.mult)\
                    .then_inc(steps_ok, 1)
                pool.wait_ge(xs_out, c * 2 + (g + 2))
                pool.wait_ge(y_step, c * 8 + (4 * g + 2))
                pool.sem_inc(gate, 1)
                nc.gpsimd.tensor_tensor(xskip[:, g], xs_tok[:, g], head_row(small[:, 2 * SSM_HEADS:3 * SSM_HEADS][:, heads]),
                                        ALU.mult).then_inc(xskip_ok, 1)
                pool.wait_ge(xdt_ok, c * 2 + (g + 3))
                pool.wait_ge(st_made, c * 2 + (g + 1))
                pool.sem_inc(gate, 1)
                e_row = decays[:, 1, bass.ds(c, 1), heads].rearrange("p c h -> p (c h)")
                nc.gpsimd.tensor_tensor(xdte[:, g], xdt[:, g], head_row(e_row), ALU.mult).then_inc(xdte_ok, 1)

            nc.gpsimd.memset(half_neg[:], -0.5).then_inc(att_step, 1)
            with nc.gpsimd.Fori(0, TT) as c:
                for g in range(G):
                    step(c, g)
            pool.wait_ge(att_sq, TT + 1)
            pool.wait_ge(att_step, 1)
            nc.gpsimd.tensor_scalar(att_f[:], att_f[:], 1.0 / D_MODEL, EPS1, ALU.mult, ALU.add).then_inc(att_step, 1)
            pool.wait_ge(att_step, 2)
            nc.gpsimd.tensor_tensor(att_f[:], att_f[:], half_neg[:], ALU.pow).then_inc(att_step, 1)


def output_projection(nc, a, ahead, wba, wba_in, raw, masks, resid, row_f, tokens, w_out, second, modc):
    w_v = w_out[0].rearrange("(k p) c -> p k c", p=P)
    w_next = a["gdn_w_in"][0].rearrange("(k p) c -> p k c", p=P)
    MT = 16
    UNITS = MT // HALF
    NH = D_MODEL // COLS
    ctx = Phase(nc, "output2" if second else "output1")
    with ctx:
        sb, sem = ctx.sb, ctx.sem
        ident = masks[:, IDENT, :]
        first = resid_units(resid) if second else raw
        w = WeightStream(nc, sem, sb, raw, ahead, 4 if second else 2, first)
        m_hi = sb("m_hi", [P, MT, SEQ], F32R)
        m_lo = sb("m_lo", [P, MT, SEQ], F32R)
        m_g = sb("m_g", [P, MT])
        row_g = sb("row_g", [P, D_MODEL])
        row_b = sb("row_b", [P, D_MODEL])
        junk = sb("junk", [P, D_MODEL])
        stats = sb("stats", [P, TT, 2, 6])
        mean_var = sb("mean_var", [P, TT, 2])
        sumsq = sb("sumsq", [P, TT]) if not second else None
        ln_f = sb("ln_f", [P, TT])
        if second:
            junk2 = sb("junk2", [P, D_MODEL])
        else:
            mod_b = sb("mod_b", [P, 3 * KT])
            mod_acc = sb("mod_acc", [P, 3 * D_MODEL])
            mod_in = sem("mod_in")
            mod_sum = sem("mod_sum")
            mod_out = sem("mod_out")
        half_neg = sb("half_neg", [P, 2 * TT])
        ps_m = ctx.psum("ps_m", [P, 4, COLS], F32)
        ps_t = ctx.psum("ps_t", [P, 4, COLS], F32)
        consts_in = sem("consts_in")
        x_in = sem("x_in")
        m_g_in = sem("m_g_in")
        sum_ok = sem("sum_ok")
        pool_step = sem("pool_step")
        factor_ok = sem("factor_ok")
        scaled = sem("scaled")
        turned = sem("turned")
        m_hi_ok = sem("m_hi_ok")
        m_lo_ok = sem("m_lo_ok")
        acc_made = sem("acc_made")
        added = sem("added")
        own_s = sem("own_s")
        gate_row = sem("gate_row")
        last_ok = sem("last_ok")
        var_ok = sem("var_ok")
        normed = sem("normed")
        out_s = sem("out_s")

        block = ctx.enter_context(nc.Block())

        @block.sync
        def _(sp):
            def load_unit(u):
                half, j = divmod(u, UNITS)
                src = w_v[:, HALF * j:HALF * (j + 1), half * COLS:(half + 1) * COLS]
                if not second or u >= 4:
                    sp.wait_ge(w.lo_ready, u - 1)
                sp.dma_start(raw[u % 2][:], src).then_inc(w.landed[u % 2], 16)

            sp.dma_start(m_g[:], a["gdn_g" if second else "mix_g"]).then_inc(m_g_in, 16)
            if second:
                load_unit(2)
                load_unit(3)
                sp.dma_start(row_g[:], a["final_g"].partition_broadcast(P)).then_inc(consts_in, 16)
            else:
                sp.dma_start(mod_acc[:], resid[:].rearrange("p t d -> p (t d)")[:, 0:3 * D_MODEL]).then_inc(mod_in, 16)
                sp.dma_start(mod_b[:], a["ada_b"]).then_inc(mod_in, 16)
                sp.wait_ge(mod_in, 32)
                sp.dma_start(resid[:], a["x"].rearrange("(t p) d -> p t d", p=P)).then_inc(x_in, 16)
                sp.dma_start(row_g[:], a["ln_g"].partition_broadcast(P)).then_inc(consts_in, 16)
                sp.dma_start(row_b[:], a["ln_b"].partition_broadcast(P)).then_inc(consts_in, 16)
            if second:
                sp.wait_ge(w.lo_ready, 2)
                sp.dma_start(resid[:], a["x1"].rearrange("(t p) d -> p t d", p=P)).then_inc(x_in, 16)
            for u in range(4 if second else 2, NH * UNITS):
                load_unit(u)
            if not second:
                with nc.allow_non_contiguous_dma(reason="32 columns"):
                    sp.dma_start(wba[:], w_next[:, :, D_CONV2 + D_Z2:]).then_inc(wba_in, 16)
                for s in range(2):
                    sp.wait_ge(w.lo_ready, NH * UNITS - 1 + s)
                    w.load_ahead(sp, ahead, [r[:] for r in raw], w_next, (s,))
            if second:
                for t in range(TT):
                    sp.wait_ge(last_ok, t + 1)
                    sp.dma_start(a["out"].rearrange("(t p) d -> p t d", p=P)[:, t, :], resid[:, t, :]).then_inc(out_s, 16)
                sp.wait_ge(out_s, 16 * TT)

        TURNS = (8, 4, 4)

        @block.tensor
        def _(pe):
            pe.sem_inc(w.units_used, 2)
            done = 0

            def turn(n):
                nonlocal done
                for e in range(done, done + n):
                    if not second and e >= MT // 2:
                        pe.wait_ge(scaled, TT)
                    if e >= 4:
                        pe.wait_ge(m_lo_ok, e - 3)
                    for t in range(TT):
                        tr = nc.tensor.transpose(ps_t[:, e % 4, t * P:(t + 1) * P], tokens[:, t, e * P:(e + 1) * P], ident)
                    tr.then_inc(turned, 1)
                done += n

            turn(TURNS[0])
            for half in range(NH):
                for j in range(UNITS):
                    u = half * UNITS + j
                    s = u % 2
                    pe.wait_ge(w.lo_ready, u + 1)
                    if half == 0:
                        pe.wait_ge(m_lo_ok, HALF * (j + 1))
                    for t in range(TT):
                        if half and j == 0:
                            pe.wait_ge(added, (half - 1) * TT + t + 1)
                        for kk in range(HALF):
                            k = HALF * j + kk
                            rows = slice(t * P, (t + 1) * P)
                            mm = three_products(nc, ps_m[:, t, :], m_hi[:, k, rows], m_lo[:, k, rows],
                                                w.hi[s][:, kk, :], w.lo[s][:, kk, :], k == 0, k == MT - 1)
                        if j == UNITS - 1 and t < TT - 1:
                            mm.then_inc(acc_made, 1)
                    mm.then_inc(w.units_used, 1)
                    if half == 0 and j < 2:
                        turn(TURNS[j + 1])
                    if second and u == 2:
                        pe.wait_ge(m_lo_ok, MT)
                        pe.wait_ge(gate_row, 1)
                        for b in range(2):
                            mm = nc.tensor.matmul(ps_t[:, b, :], masks[:, ONES, :], junk[:, b * COLS:(b + 1) * COLS],
                                                  start=True, stop=True)
                        mm.then_inc(gate_row, 1)
            if not second:
                pe.wait_ge(mod_in, 32)
                for j in range(3 * KT):
                    mm = nc.tensor.matmul(ps_t[:, 0, j:j + P], mod_acc[:, j * P:(j + 1) * P], masks[:, ONES, :],
                                          start=True, stop=True)
                mm.then_inc(mod_sum, 1)

        @block.scalar
        def _(act):
            def round_unit(u):
                w.round(act, u % 2, u // 2)

            def high(e):
                act.wait_ge(turned, e + 1)
                nc.scalar.activation(m_hi[:, e, :], ps_t[:, e % 4, :], ACT.Identity, scale=m_g[:, e:e + 1]).then_inc(m_hi_ok, 1)

            round_unit(0)
            act.wait_ge(m_g_in, 16)
            for e in range(4):
                high(e)
            if not second:
                for t in range(TT):
                    if t:
                        act.wait_ge(sum_ok, t)
                    nc.scalar.activation(junk[:], tokens[:, t, D_MODEL:], ACT.Square,
                                         accum_out=sumsq[:, t:t + 1]).then_inc(sum_ok, 1)
            round_unit(1)
            for e in range(4, 12):
                high(e)
            round_unit(2)
            for e in range(12, MT):
                high(e)
            for u in range(3, NH * UNITS):
                round_unit(u)
            for t in range(TT):
                if second:
                    act.wait_ge(added, TT + t + 1)
                else:
                    act.wait_ge(normed, t + 1)
                nc.scalar.activation(junk[:], resid[:, t, :], ACT.Square, accum_out=row_f[:, t:t + 1])\
                    .then_inc(sum_ok, 1)
                act.wait_ge(sum_ok, (0 if second else TT) + t + 1)

        @block.gpsimd
        def _(pool):
            nc.gpsimd.memset(half_neg[:], -0.5).then_inc(pool_step, 1)
            steps = 1

            def rsqrt(values, of, scale, eps):
                nonlocal steps
                pool.wait_ge(pool_step, steps)
                nc.gpsimd.tensor_scalar(values, of, scale, eps, ALU.mult, ALU.add).then_inc(pool_step, 1)
                steps += 1
                pool.wait_ge(pool_step, steps)
                nc.gpsimd.tensor_tensor(values, values, half_neg[:, 0:values.shape[-1]], ALU.pow).then_inc(factor_ok, 1)

            if not second:
                pool.wait_ge(sum_ok, TT)
                rsqrt(sumsq[:], sumsq[:], 1.0 / D_MODEL, EPS1)

            def layer_factor(t):
                pool.wait_ge(var_ok, t + 1)
                rsqrt(ln_f[:, t:t + 1], mean_var[:, t, 1:2], 1.0, EPS1)

            def last_factor(t):
                pool.wait_ge(sum_ok, (0 if second else TT) + t + 1)
                rsqrt(row_f[:, t:t + 1], row_f[:, t:t + 1], 1.0 / D_MODEL, EPS2)

            for n in range(TT + 2):
                if not second and n < TT:
                    layer_factor(n)
                if n >= 2:
                    last_factor(n - 2)

        @block.vector
        def _(dve):
            own = Own(dve, own_s)

            def rest(u):
                w.rest(nc.vector, dve, u % 2, u // 2)

            def low(e):
                dve.wait_ge(m_hi_ok, e + 1)
                nc.vector.scalar_tensor_tensor(out=m_lo[:, e, :], in0=ps_t[:, e % 4, :], scalar=m_g[:, e:e + 1],
                                               in1=m_hi[:, e, :], op0=ALU.mult, op1=ALU.subtract).then_inc(m_lo_ok, 1)

            def wait_products(half, t):
                if t < TT - 1:
                    dve.wait_ge(acc_made, (TT - 1) * half + t + 1)
                else:
                    dve.wait_ge(w.units_used, UNITS * (half + 1) + 2)

            def residual(half, tiles):
                cols = slice(half * COLS, (half + 1) * COLS)
                for t in tiles:
                    wait_products(half, t)
                    x = resid[:, t, cols]
                    if second:
                        own.did(nc.vector.tensor_tensor(junk2[:, (t % 2) * COLS:(t % 2 + 1) * COLS], ps_m[:, t, :],
                                                        row_b[:, cols], ALU.mult))
                        own.wait()
                        nc.vector.tensor_tensor(x, x, junk2[:, (t % 2) * COLS:(t % 2 + 1) * COLS], ALU.add)\
                            .then_inc(added, 1)
                    else:
                        nc.vector.scalar_tensor_tensor(out=x, in0=x, scalar=ALPHA, in1=ps_m[:, t, :],
                                                       op0=ALU.mult, op1=ALU.add).then_inc(added, 1)
                if not second:
                    for t in tiles:
                        dve.wait_ge(added, half * TT + t + 1)
                        own.did(nc.vector.bn_stats(stats[:, t, half, :], resid[:, t, cols]))

            rest(0)
            for e in range(4):
                low(e)
            rest(1)
            for e in range(4, 8):
                low(e)
            if not second:
                dve.wait_ge(factor_ok, 1)
                for t in range(TT):
                    rows = tokens[:, t, D_MODEL:]
                    nc.vector.tensor_scalar(rows, rows, sumsq[:, t:t + 1], None, ALU.mult).then_inc(scaled, 1)
            for e in range(8, 12):
                low(e)
            rest(2)
            for e in range(12, MT):
                low(e)
            dve.wait_ge(x_in, 16)
            if second:
                junk_v = junk[:].rearrange("p (j c) -> p j c", c=P)
                nc.vector.tensor_tensor(junk_v, ident.unsqueeze(1).broadcast_to([P, KT, P]),
                                        modc[:, 2 * KT:].unsqueeze(2).broadcast_to([P, KT, P]), ALU.mult).then_inc(gate_row, 1)
            for u in range(3, NH * UNITS):
                rest(u)
                if second and u == 3:
                    dve.wait_ge(gate_row, 2)
                    nc.vector.tensor_copy(row_b[:], ps_t[:, 0:2, :].rearrange("p a b -> p (a b)")).then_inc(gate_row, 1)
                    dve.wait_ge(gate_row, 3)
                if u == UNITS:
                    residual(0, range(TT))

            def before_factor(t):
                residual(1, (t,))
                if not second:
                    own.wait()
                    nc.vector.bn_aggr(mean_var[:, t, :], stats[:, t, :, :].rearrange("p a b -> p (a b)"))\
                        .then_inc(var_ok, 1)
                    dve.wait_ge(var_ok, t + 1)
                    own.did(nc.vector.scalar_tensor_tensor(out=resid[:, t, :], in0=resid[:, t, :],
                                                           scalar=mean_var[:, t, 0:1], in1=row_g[:],
                                                           op0=ALU.subtract, op1=ALU.mult))
                    return own.n

            def after_factor(t, step):
                if second:
                    dve.wait_ge(factor_ok, t + 1)
                    nc.vector.scalar_tensor_tensor(out=resid[:, t, :], in0=resid[:, t, :], scalar=row_f[:, t:t + 1],
                                                   in1=row_g[:], op0=ALU.mult, op1=ALU.mult).then_inc(last_ok, 1)
                else:
                    dve.wait_ge(factor_ok, 2 + t + max(0, t - 2))
                    own.wait(step)
                    nc.vector.scalar_tensor_tensor(out=resid[:, t, :], in0=resid[:, t, :], scalar=ln_f[:, t:t + 1],
                                                   in1=row_b[:], op0=ALU.mult, op1=ALU.add).then_inc(normed, 1)

            dve.wait_ge(consts_in, 16 if second else 32)
            step_of = {}
            for t in range(TT + 1):
                if t < TT:
                    step_of[t] = before_factor(t)
                if t:
                    after_factor(t - 1, step_of[t - 1])
            if not second:
                dve.wait_ge(mod_sum, 1)
                nc.vector.tensor_tensor(modc[:], ps_t[:, 0, 0:3 * KT], mod_b[:], ALU.add).then_inc(mod_out, 1)


def projections2(nc, a, ahead, wba, wba_in, raw, masks, resid, row_f, modc, small, h_hi, h_lo, qkvT, z, beta, g):
    w_in = a["gdn_w_in"][0].rearrange("(k p) c -> p k c", p=P)
    B_CONV, B_Z, N_BA = D_CONV2 // COLS, D_Z2 // COLS, 2 * V_HEADS
    ended = Phase.take_used()
    ctx = Phase(nc, "project2")
    with ctx:
        sb, sem = ctx.sb, ctx.sem
        w = WeightStream(nc, sem, sb, raw, ahead, 3)
        ident = masks[:, IDENT, :]
        g_col = sb("g_col", [P, KT])
        gain = sb("gain", [P, KT])
        xn = z[:, :, 0:D_MODEL]
        h = qkvT[:, 24:32, :]
        BY_POOL = (2, 4, 6)
        g_in = sem("g_in")
        x1_out = sem("x1_out")
        xn_ok = sem("xn_ok")
        gain_ok = sem("gain_ok")
        h_turned = sem("h_turned")
        high_ok = sem("high_ok")
        h_ok = sem("h_ok")
        low_v, low_p = sem("low_v"), sem("low_p")
        wba_hi = sb("wba_hi", [P, KT, N_BA], F32R)
        wba_lo = sb("wba_lo", [P, KT, N_BA], F32R)
        ba = sb("ba", [P, TT, N_BA])
        cw = sb("cw", [P, D_CONV2 // P, CONV])
        pre, acc, soft, rows = spare_buffers(resid)
        ps = ctx.psum("ps", [P, 8, COLS])
        banks_free = sem("banks_free")
        cw_in = sem("cw_in")
        ba_split = sem("ba_split")
        ba_made = sem("ba_made")
        ba_out = sem("ba_out")
        zeroed = sem("zeroed")
        conv = ConvStream(nc, sem, pre, acc, cw, ps, qkvT, False)
        beta_step = sem("beta_step")
        steps = StepSizes(nc, sb, sem, soft, ba[:, :, V_HEADS:], small[:, 3 * V_HEADS:4 * V_HEADS],
                          small[:, 4 * V_HEADS:5 * V_HEADS], V_HEADS, ba[:, :, V_HEADS:], g[:])
        block = ctx.enter_context(nc.Block())

        @block.sync
        def _(sp):
            sp.dma_start(g_col[:], a["norm_g"]).then_inc(g_in, 16)
            sp.dma_start(a["x1"].rearrange("(t p) d -> p t d", p=P), resid[:]).then_inc(x1_out, 16)

            def load(n):
                for s in range(2):
                    w.load(sp, s, n, w_in[:, HALF * s:HALF * (s + 1), bass.ds(n * COLS, COLS)])

            sp.dma_start(cw[:], a["conv2"]).then_inc(cw_in, 16)
            with nc.sync.Fori(1, B_CONV + B_Z) as n:
                load(n)

        @block.scalar
        def _(act):
            act.wait_ge(wba_in, 16)
            nc.scalar.activation(wba_hi[:], wba[:], ACT.Copy).then_inc(ba_split, 1)
            w.round(act, 0, 0)
            act.wait_ge(gain_ok, 1)
            for e in range(KT):
                act.wait_ge(h_turned, e + 1)
                nc.scalar.activation(h_hi[:, e, :], ps[:, e % 4, :], ACT.Identity, scale=gain[:, e:e + 1],
                                     bias=modc[:, e:e + 1]).then_inc(high_ok, 1)
            act.wait_ge(x1_out, 16)
            act.wait_ge(ba_made, 1)
            nc.scalar.activation(rows[0:N_BA, :], ps[0:N_BA, 7, :], ACT.Copy).then_inc(ba_out, 1)
            w.round(act, 1, 0)
            act.wait_ge(ba_made, 2)
            nc.scalar.activation(ba[:], ps[:, 6, 0:TT * N_BA].rearrange("p (t h) -> p t h", t=TT), ACT.Copy)\
                .then_inc(ba_out, 1)
            act.wait_ge(ba_out, 2)
            act.sem_inc(banks_free, 1)
            act.wait_ge(cw_in, 16)
            act.wait_ge(zeroed, 1)
            act.sem_inc(conv.conv_done, 2)
            with nc.scalar.Fori(0, B_CONV // 2) as i:
                for par in range(2):
                    b = i * 2 + par
                    for s in range(2):
                        w.round(act, s, b + 1)
                    act.wait_ge(w.units_used, b * 2 + 4)
                    conv.read_and_silu(act, b, par, banks_free)

            def read_z(j, par):
                act.wait_ge(w.units_used, j * 2 + (2 * B_CONV + 4))
                nc.scalar.activation(z[:, :, bass.ds(j * COLS, COLS)], ps[:, 4 * par:4 * par + 4, :], ACT.Silu)\
                    .then_inc(banks_free, 1)

            for j in range(B_Z):
                if j + 1 < B_Z:
                    for s in range(2):
                        w.round(act, s, B_CONV + j + 1)
                if j == 0:
                    steps.exponentials(act)
                    nc.scalar.activation(beta[:], ba[:, :, 0:V_HEADS], ACT.Exp, scale=-1.0).then_inc(beta_step, 1)
                read_z(j, j % 2)

        @block.vector
        def _(dve):
            dve.sem_inc(w.lo_ready, 2)
            for t in range(TT):
                nc.vector.tensor_scalar(xn[:, t, :], resid[:, t, :], row_f[:, t:t + 1], None, ALU.mult)\
                    .then_inc(xn_ok, 1)
                if t == 0:
                    dve.wait_ge(g_in, 16)
                    nc.vector.scalar_tensor_tensor(out=gain[:], in0=modc[:, KT:2 * KT], scalar=1.0, in1=g_col[:],
                                                   op0=ALU.add, op1=ALU.mult).then_inc(gain_ok, 1)
            dve.wait_ge(ba_split, 1)
            nc.vector.tensor_tensor(wba_lo[:], wba[:], wba_hi[:], ALU.subtract).then_inc(ba_split, 1)
            dve.wait_ge(gain_ok, 1)
            for e in range(KT):
                dve.wait_ge(high_ok, e + 1)
                nc.vector.tensor_scalar(h[:, e, :], ps[:, e % 4, :], gain[:, e:e + 1], modc[:, e:e + 1],
                                        ALU.mult, ALU.add).then_inc(h_ok, 1)
                if e not in BY_POOL:
                    dve.wait_ge(h_ok, e + 1)
                    nc.vector.tensor_tensor(h_lo[:, e, :], h[:, e, :], h_hi[:, e, :], ALU.subtract).then_inc(low_v, 1)
            dve.wait_ge(w.lo_ready, 3)
            w.rest(nc.vector, dve, 1, 0)
            dve.wait_ge(x1_out, 16)
            dve.wait_ge(xn_ok, TT)
            nc.vector.memset(pre, 0.0).then_inc(zeroed, 1)
            dve.sem_inc(conv.taps_done, 2)
            dve.wait_ge(ba_out, 2)
            steps.start(dve)
            dve.wait_ge(cw_in, 16)
            with nc.vector.Fori(0, B_CONV) as b:
                for s in range(2):
                    w.rest(nc.vector, dve, s, b + 1)
                conv.sum_taps(dve, b)
            for s in range(2):
                w.rest(nc.vector, dve, s, B_CONV + 1)
            steps.finish(dve)
            dve.wait_ge(beta_step, 1)
            nc.vector.tensor_scalar(beta[:], beta[:], 1.0, None, ALU.add).then_inc(beta_step, 1)
            dve.wait_ge(beta_step, 2)
            nc.vector.reciprocal(beta[:], beta[:]).then_inc(beta_step, 1)
            with nc.vector.Fori(B_CONV + 2, B_CONV + B_Z) as n:
                for s in range(2):
                    w.rest(nc.vector, dve, s, n)

        @block.gpsimd
        def _(pool):
            clear_semaphores(pool, ended)
            w.rest(nc.gpsimd, pool, 0, 0)
            for e in BY_POOL:
                pool.wait_ge(h_ok, e + 1)
                nc.gpsimd.tensor_tensor(h_lo[:, e, :], h[:, e, :], h_hi[:, e, :], ALU.subtract).then_inc(low_p, 1)

        @block.tensor
        def _(pe):
            pe.sem_inc(w.units_used, 2)
            pe.sem_inc(banks_free, 1)

            def wait_h(e):
                by_pool = sum(k <= e for k in BY_POOL)
                pe.wait_ge(low_v, e + 1 - by_pool)
                if by_pool:
                    pe.wait_ge(low_p, by_pool)

            for e in range(KT):
                if e >= 4:
                    pe.wait_ge(h_ok, e - 3)
                for t in range(TT):
                    if e == 0:
                        pe.wait_ge(xn_ok, t + 1)
                    tr = nc.tensor.transpose(ps[:, e % 4, t * P:(t + 1) * P], xn[:, t, e * P:(e + 1) * P], ident)
                tr.then_inc(h_turned, 1)
            pe.wait_ge(ba_split, 2)
            for k in range(KT):
                wait_h(k)
                mm = three_products(nc, ps[0:N_BA, 7, :], wba_hi[:, k, :], wba_lo[:, k, :], h_hi[:, k, :],
                                    h_lo[:, k, :], k == 0, k == KT - 1)
            mm.then_inc(ba_made, 1)
            pe.wait_ge(ba_out, 1)
            for t in range(TT):
                tr = nc.tensor.transpose(ps[:, 6, t * N_BA:(t + 1) * N_BA], rows[0:N_BA, t * P:(t + 1) * P],
                                         masks[0:N_BA, IDENT, 0:N_BA])
            tr.then_inc(ba_made, 1)
            with nc.tensor.Fori(0, B_CONV // 2) as i:
                for par in range(2):
                    w.channels(pe, i * 2 + par, par, ps, h_hi, h_lo, banks_free)
            with nc.tensor.Fori(0, B_Z // 2) as i:
                for par in range(2):
                    w.tokens(pe, i * 2 + (B_CONV + par), par, ps, h_hi, h_lo, banks_free)


def gated_deltanet(nc, a, ahead, masks, resid, raw, qkvT, z, beta, g):
    ctx = Phase(nc, "gdn")
    with ctx:
        sb, sem = ctx.sb, ctx.sem
        NB, HB = 2, 4
        ident, upper, below, ones = (masks[:, m, :] for m in (IDENT, UPPER, BELOW, ONES))
        flat = lambda t: t.rearrange("p a b -> p (a b)")
        masks2 = sb("masks2", [P, 5, P])
        strict, block32 = masks2[:, 0, :], masks2[:, 1, :]
        decays = sb("decays", [P, 3, TT, V_HEADS])
        dsel = sb("dsel", [P, 3, 2 * HB, TT])
        gsel = sb("gsel", [P, 2 * HB, TT])
        bsel = sb("bsel", [P, 2 * HB, TT])
        st = sb("st", [P, 2, 2, SEQ])
        C = resid[:].rearrange("p t (m c) -> p (t m) c", c=P)
        PT = sb("PT", [P, 8 * HB, P])
        ktok = sb("ktok", [P, HB, TT, P])
        ssq = sb("ssq", [P, HB, TT])
        ssk = sb("ssk", [P, HB, TT])
        kss = sb("kss", [P, HB, TT])
        r2 = sb("r2", [P, HB, TT])
        qe = sb("qe", [P, HB, TT])
        rinv = sb("rinv", [P, HB, TT])
        nbp = sb("nbp", [P, HB, 2, TT])
        sign = sb("sign", [P, TT])
        wsc = sb("wsc", [P, HB, 2, TT])
        wsce = sb("wsce", [P, HB, 2, TT])
        Uc = sb("Uc", [P, 8 * HB, 32])
        Tc = sb("Tc", [P, 8 * HB, 32])
        tmp = sb("tmp", [P, 2 * 64])
        half = sb("half", [P, 2, HB * TT])
        vst = sb("vst", [P, 2, SEQ])
        R = sb("R", [P, 2, P])
        w_sb = sb("w_sb", [P, 2, P])
        we = sb("we", [P, 2, P])
        qt = sb("qt", [P, 2, P])
        S = sb("S", [P, 2, P])
        junk = sb("junk", [P, 2, P])
        sums = sb("sums", [P, 2, 2, TT])
        ms = sb("ms", [P, 2, TT])
        rs = sb("rs", [P, 2, 2, TT])
        space_u = sb("space_u", [P, 2, 8, P])
        space_t = sb("space_t", [P, 2, 1056])
        U = [space_u[:, s] for s in range(2)]
        KKm = space_u[:, 0, 0:4]
        KQm = space_u[:, 0, 4:8]
        Cc = flat(space_u[:, 1]).rearrange("p (m c) -> p m c", c=32)
        T, V = (space_t[:, s, 0:1024].rearrange("p (m c) -> p m c", c=P) for s in range(2))
        Cf, Uf = space_t[:, 0], space_t[:, 1]
        O = [flat(raw[0][:])[:, s * 1024:(s + 1) * 1024].rearrange("p (h c e) -> p h c e", h=2, c=TT) for s in range(2)]
        steps, E = (flat(raw[0][:])[:, s * 1024:(s + 1) * 1024].rearrange("p (m c) -> p m c", c=P) for s in range(2))
        vr = [flat(raw[1][:])[:, s * 1024:(s + 1) * 1024].rearrange("p (h c e) -> p h c e", h=2, c=TT) for s in range(2)]
        psA = ctx.psum("psA", [P, 2, COLS])
        psZ = ctx.psum("psZ", [P, 2, COLS])
        psK = ctx.psum("psK", [P, 4, P])
        psO = ctx.psum("psO", [P, 4, P])
        psW = ctx.psum("psW", [P, 4, P])

        consts_in = sem("consts_in")
        own_p = sem("own_p")
        sums_ok, decays_ok = sem("sums_ok"), sem("decays_ok")
        own_s = sem("own_s")
        pool_s = sem("pool_s")
        sel_ok = sem("sel_ok")
        st_in = [sem(f"st_in{i}") for i in range(2)]
        turned = sem("turned")
        sq_ok = sem("sq_ok")
        tok_out = sem("tok_out")
        kk_made = sem("kk_made")
        kk_out = sem("kk_out")
        steps_ok = sem("steps_ok")
        seg_made = sem("seg_made")
        e_ok = sem("e_ok")
        c_ok = sem("c_ok")
        pt_ok = sem("pt_ok")
        cc_ok = sem("cc_ok")
        kss_ok = sem("kss_ok")
        rinv_ok = sem("rinv_ok")
        scales_ok = sem("scales_ok")
        eye_ok = sem("eye_ok")
        uc_ok = sem("uc_ok")
        vst_in = sem("vst_in")
        vt_made = sem("vt_made")
        vr_ok = sem("vr_ok")
        tx_ok = sem("tx_ok")
        ux_ok = sem("ux_ok")
        v_made, v_out, z_made, u_ok2 = (sem(n) for n in ("v_made", "v_out", "z_made", "u_ok2"))
        t_made, t_out = sem("t_made"), sem("t_out")
        ks_made, qs_made, ds_made, we_ok = (sem(n) for n in ("ks_made", "qs_made", "ds_made", "we_ok"))
        r_ok, qt_ok = sem("r_ok"), sem("qt_ok")
        w_made, w_ok, o_made, o_ok = (sem(n) for n in ("w_made", "w_ok", "o_made", "o_ok"))
        s_ok = sem("s_ok")
        osq_ok = sem("osq_ok")
        rs_ok = sem("rs_ok")
        gate, gate_v = sem("gate"), sem("gate_v")
        z_ok = sem("z_ok")
        heads_out = sem("heads_out")
        S_COUNT = (0, 1, 3, 5)

        block = ctx.enter_context(nc.Block())

        def at(i, per_head, j, k):
            return i * (HB * per_head) + (per_head * j + k)

        def doubling_parts(j):
            parts = []
            for lv in range(3):
                for kind in ("V", "Z", "T"):
                    if kind == "T" and lv == 2:
                        continue
                    parts += [(kind, lv, grp) for grp in range(2)]
            return parts

        def expand_group(engine, j, grp, compact, full, done):
            src = compact[:, 8 * j + 4 * grp:8 * j + 4 * grp + 4, :]
            engine.tensor_tensor(full[:, 4 * grp:4 * grp + 4, :].rearrange("p m (r c) -> p m r c", c=32),
                                 src.unsqueeze(2).broadcast_to([P, 4, 4, 32]),
                                 block32.rearrange("p (r c) -> p r c", c=32).unsqueeze(1).broadcast_to([P, 4, 4, 32]),
                                 ALU.mult).then_inc(done, 1)

        @block.sync
        def _(sp):
            def stage(i, j):
                sp.dma_start(st[:, j % 2, 0, :], qkvT[:, bass.ds(i * HB + j, 1), :].rearrange("p o t -> p (o t)"))\
                    .then_inc(st_in[j % 2], 16)
                sp.dma_start(st[:, j % 2, 1, :], qkvT[:, bass.ds(i * HB + (QK_HEADS + j), 1), :].rearrange("p o t -> p (o t)"))\
                    .then_inc(st_in[j % 2], 16)

            def stage_v(i, j):
                sp.dma_start(vst[:], qkvT[:, bass.ds(i * (2 * HB) + (2 * QK_HEADS + 2 * j), 2), :]).then_inc(vst_in, 16)

            with nc.sync.Fori(0, NB) as i:
                sp.wait_ge(heads_out, i + 1)
                for j in range(2):
                    stage(i, j)
                stage_v(i, 0)
                for j in range(2, HB):
                    sp.wait_ge(kk_made, at(i, 1, j - 2, 1))
                    stage(i, j)
                for j in range(2):
                    sp.wait_ge(kk_made, at(i, 1, j + 2, 1))
                    stage(i, j)
                for j in range(1, HB):
                    sp.wait_ge(vt_made, at(i, 1, j - 1, 1))
                    stage_v(i, j)
                    if j >= 2:
                        sp.wait_ge(qs_made, at(i, 3, j - 2, 3))
                        stage(i, j)
            sp.wait_ge(v_made, NB * HB * 6)
            WeightStream.load_ahead(sp, ahead, resid_units(resid), a["gdn_w_out"][0].rearrange("(k p) c -> p k c", p=P))

        @block.tensor
        def _(pe):
            for n, mask in enumerate((upper, below, ones)):
                mm = nc.tensor.matmul(psA[:, 0, n * P:n * P + TT * V_HEADS], mask, flat(g[:]), start=True, stop=True)
            mm.then_inc(sums_ok, 1)
            pe.wait_ge(decays_ok, 1)

            def build(i, j):
                slot = j % 2
                pe.wait_ge(st_in[slot], i * 128 + 32 * (j // 2 + 1))
                if j:
                    pe.wait_ge(sq_ok, at(i, 8, j - 1, 8))
                    pe.wait_ge(tok_out, at(i, 1, j - 1, 1))
                for x, ps in enumerate((psO, psW)):
                    for c in range(TT):
                        tr = nc.tensor.transpose(ps[:, c, :], st[:, slot, x, c * P:(c + 1) * P], ident)
                tr.then_inc(turned, 1)
                if j:
                    pe.wait_ge(kk_out, at(i, 2, j - 1, 2))
                for c in range(TT):
                    cols = slice(c * P, (c + 1) * P)
                    for x in range(2):
                        mm = nc.tensor.matmul(psA[:, 1 - x, cols], st[:, slot, 1, cols], st[:, slot, x, cols],
                                              start=True, stop=True)
                mm.then_inc(kk_made, 1)
                pe.wait_ge(steps_ok, at(i, 1, j, 1))
                if j:
                    pe.wait_ge(e_ok, at(i, 1, j - 1, 1))
                for n in range(2):
                    mm = nc.tensor.matmul(psZ[:, n, :], below, flat(steps[:, 4 * n:4 * n + 4, :]), start=True, stop=True)
                mm.then_inc(seg_made, 1)

            def turn_v(i, j):
                pe.wait_ge(vst_in, at(i, 16, j, 16))
                if j:
                    pe.wait_ge(u_ok2, at(i, 6, j - 1, 6))
                else:
                    pe.wait_ge(e_ok, at(i, 1, HB - 1, 1))
                for h in range(2):
                    for c in range(TT):
                        tr = nc.tensor.transpose(psZ[:, h, c * P:(c + 1) * P], vst[:, h, c * P:(c + 1) * P], ident)
                tr.then_inc(vt_made, 1)

            def double(i, j, kind, lv, grp):
                bank = psZ if kind == "Z" else psA
                q = 2 * lv + grp + 1
                if kind == "V":
                    if lv == 0:
                        pe.wait_ge(tx_ok, at(i, 2, j, grp + 1))
                        if j:
                            pe.wait_ge(v_out, at(i, 6, j - 1, 4 + grp + 1))
                    else:
                        pe.wait_ge(t_out, at(i, 4, j, q - 2))
                elif kind == "Z":
                    pe.wait_ge(v_out, at(i, 6, j, q))
                    if lv == 0:
                        pe.wait_ge(ux_ok, at(i, 2, j, grp + 1))
                        pe.wait_ge(vr_ok, at(i, 2, j, grp + 1))
                    else:
                        pe.wait_ge(u_ok2, at(i, 6, j, q - 2))
                else:
                    pe.wait_ge(u_ok2, at(i, 6, j, q))
                for c in range(TT):
                    m = 4 * grp + c
                    out = bank[:, grp, c * P:(c + 1) * P]
                    if kind == "V":
                        mm = nc.tensor.matmul(out, C[:, 8 * j + m, :], T[:, m, :], start=True, stop=True)
                    elif kind == "Z":
                        mm = nc.tensor.matmul(out, V[:, m, :], U[j % 2][:, m, :], start=True, stop=True)
                    else:
                        mm = nc.tensor.transpose(out, U[j % 2][:, m, :], ident)
                mm.then_inc({"V": v_made, "Z": z_made, "T": t_made}[kind], 1)

            def chunk_products(i, j, c, fill):
                slot, cols = j % 2, slice(c * P, (c + 1) * P)
                if c:
                    pe.wait_ge(s_ok, at(i, 5, j, S_COUNT[c]))
                    nc.tensor.matmul(flat(psK[:, 0:2, :]), st[:, slot, 1, cols], flat(S[:]), start=True, stop=True)\
                        .then_inc(ks_made, 1)
                    pe.wait_ge(o_ok, at(i, 4, j, c))
                    nc.tensor.matmul(flat(psO[:, 0:2, :]), st[:, slot, 0, cols], flat(S[:]), start=True, stop=True)\
                        .then_inc(qs_made, 1)
                else:
                    pe.wait_ge(st_in[slot], i * 128 + 32 * (j // 2 + 3))
                fill(4 * c)
                if c:
                    pe.wait_ge(r_ok, at(i, 6, j, 2 * c))
                else:
                    pe.wait_ge(vr_ok, at(i, 2, j, 2))
                    pe.wait_ge(u_ok2, at(i, 6, j, 6))
                if c or j:
                    pe.wait_ge(w_ok, at(i, 4, j, c))
                for h in range(2):
                    rhs = R[:, h, :] if c else vr[slot][:, h, 0, :]
                    mm = nc.tensor.matmul(psW[:, h, :], U[slot][:, 4 * h + c, :], rhs, start=True, stop=True)
                mm.then_inc(w_made, 1)
                fill(4 * c + 1)
                if c < TT - 1:
                    pe.wait_ge(we_ok, at(i, 3, j, c + 1))
                    nc.tensor.matmul(flat(psK[:, 2:4, :]), ktok[:, j, c, :], flat(we[:]), start=True, stop=True)\
                        .then_inc(ds_made, 1)
                fill(4 * c + 2)
                pe.wait_ge(w_ok, at(i, 4, j, c + 1))
                if c:
                    pe.wait_ge(qt_ok, at(i, 6, j, 2 * c))
                elif j:
                    pe.wait_ge(o_ok, at(i, 4, j, 0))
                for h in range(2):
                    mm = nc.tensor.matmul(psO[:, 2 + h, :], PT[:, 8 * j + 4 * h + c, :], w_sb[:, h, :], start=True, stop=True)
                mm.then_inc(o_made, 1)
                fill(4 * c + 3)

            with nc.tensor.Fori(0, NB) as i:
                pe.wait_ge(heads_out, i + 1)
                for j in range(HB):
                    build(i, j)
                pe.wait_ge(sq_ok, at(i, 8, HB - 1, 8))
                pe.wait_ge(tok_out, at(i, 1, HB - 1, 1))
                pe.wait_ge(kk_out, at(i, 2, HB - 1, 2))
                pe.wait_ge(pt_ok, at(i, 1, HB - 1, 1))
                turn_v(i, 0)
                for kind, lv, grp in doubling_parts(0):
                    double(i, 0, kind, lv, grp)
                for j in range(HB):
                    parts = doubling_parts(j + 1) if j + 1 < HB else None

                    def fill(n):
                        if parts:
                            if n == 0:
                                turn_v(i, j + 1)
                            double(i, j + 1, *parts[n])

                    for c in range(TT):
                        chunk_products(i, j, c, fill)

        @block.scalar
        def _(act):
            act.dma_start(masks2[:], a["masks2"]).then_inc(consts_in, 16)
            act.wait_ge(sums_ok, 1)
            nc.scalar.activation(decays[:].rearrange("p n c h -> p n (c h)"),
                                 psA[:, 0, :].rearrange("p (n c) -> p n c", c=P)[:, 0:3, 0:TT * V_HEADS],
                                 ACT.Exp).then_inc(decays_ok, 1)

            def squares(i, j):
                act.wait_ge(turned, at(i, 1, j, 1))
                nc.scalar.activation(ktok[:, j], psW[:], ACT.Copy).then_inc(tok_out, 1)
                act.wait_ge(tok_out, at(i, 1, j, 1))
                for ps, to in ((psO, ssq), (psW, ssk)):
                    for c in range(TT):
                        nc.scalar.activation(ps[:, c, :], ps[:, c, :], ACT.Square, accum_out=to[:, j, c:c + 1])\
                            .then_inc(sq_ok, 1)

            def exps(i, j):
                act.wait_ge(seg_made, at(i, 1, j, 1))
                if j:
                    act.wait_ge(c_ok, at(i, 8, j - 1, 8))
                    act.wait_ge(pt_ok, at(i, 1, j - 1, 1))
                else:
                    act.wait_ge(z_ok, i * (8 * HB) + 9)
                nc.scalar.activation(E, psZ[:].rearrange("p n (m c) -> p (n m) c", c=P), ACT.Exp).then_inc(e_ok, 1)

            def compact(i, j):
                act.wait_ge(c_ok, at(i, 8, j, 8))
                for r in range(4):
                    rows = slice(32 * r, 32 * r + 32)
                    nc.scalar.activation(Cc[rows, 8 * j:8 * j + 8, :], C[rows, 8 * j:8 * j + 8, rows], ACT.Copy)\
                        .then_inc(cc_ok, 1)

            def evacuate(i, j, kind, lv, grp):
                q = 2 * lv + grp + 1
                ms4 = slice(4 * grp, 4 * grp + 4)
                src = psA[:, grp, :].rearrange("p (m c) -> p m c", c=P)
                if kind == "V":
                    act.wait_ge(v_made, at(i, 6, j, q))
                    if lv:
                        act.wait_ge(z_made, at(i, 6, j, q - 2))
                    elif j:
                        act.wait_ge(z_made, at(i, 6, j - 1, 4 + q))
                    nc.scalar.activation(V[:, ms4, :], src, ACT.Copy).then_inc(v_out, 1)
                elif kind == "T":
                    act.wait_ge(t_made, at(i, 4, j, q))
                    nc.scalar.activation(T[:, ms4, :], src, ACT.Copy).then_inc(t_out, 1)

            def out_squares(i, j, c):
                act.wait_ge(o_ok, at(i, 4, j, c + 1))
                if j or c:
                    act.wait_ge(osq_ok, at(i, 8, j, 2 * c))
                for h in range(2):
                    nc.scalar.activation(junk[:, h, :], O[j % 2][:, h, c, :], ACT.Square, scale=P ** -0.5,
                                         accum_out=sums[:, j % 2, h, c:c + 1]).then_inc(osq_ok, 1)

            def chunk_part(i, j, c, fill):
                if c:
                    act.wait_ge(qs_made, at(i, 3, j, c))
                    act.wait_ge(o_ok, at(i, 4, j, c))
                    for h in range(2):
                        nc.scalar.activation(qt[:, h, :], psO[:, h, :], ACT.Copy,
                                             scale=dsel[:, 0, 2 * j + h, c:c + 1]).then_inc(qt_ok, 1)
                fill(4 * c)
                fill(4 * c + 1)
                if c:
                    out_squares(i, j, c - 1)
                elif j:
                    out_squares(i, j - 1, TT - 1)
                fill(4 * c + 2)
                fill(4 * c + 3)

            with nc.scalar.Fori(0, NB) as i:
                act.wait_ge(heads_out, i + 1)
                squares(i, 0)
                for j in range(HB):
                    exps(i, j)
                    if j + 1 < HB:
                        squares(i, j + 1)
                    compact(i, j)
                act.wait_ge(scales_ok, i * 3 + 3)
                for kind, lv, grp in doubling_parts(0):
                    evacuate(i, 0, kind, lv, grp)
                for j in range(HB):
                    parts = doubling_parts(j + 1) if j + 1 < HB else None

                    def fill(n):
                        if parts:
                            evacuate(i, j + 1, *parts[n])

                    for c in range(TT):
                        chunk_part(i, j, c, fill)
                out_squares(i, HB - 1, TT - 1)

        @block.gpsimd
        def _(pool):
            for n, e in enumerate((0.5, -0.5)):
                nc.gpsimd.memset(half[:, n, :], e).then_inc(pool_s, 1)
            pool.wait_ge(pool_s, 2)

            def log_decay_steps(i, j):
                if j:
                    pool.wait_ge(seg_made, at(i, 1, j - 1, 1))
                gs = gsel[:, 2 * j:2 * j + 2, :].rearrange("p h c -> p (h c)")
                nc.gpsimd.tensor_tensor(steps, upper.unsqueeze(1).broadcast_to([P, 8, P]),
                                        gs.unsqueeze(2).broadcast_to([P, 8, P]), ALU.mult).then_inc(steps_ok, 1)

            def expand(i, j, compact, full, done):
                for grp in range(2):
                    if done is tx_ok:
                        pool.wait_ge(v_made, at(i, 6, j - 1, 4 + grp + 1))
                    expand_group(nc.gpsimd, j, grp, compact, full, done)

            def norm_factor(i, j):
                pool.wait_ge(osq_ok, at(i, 8, j, 8))
                nc.gpsimd.tensor_tensor(ms[:], sums[:, j % 2], qe[:, j, :].unsqueeze(1).broadcast_to([P, 2, TT]),
                                        ALU.add).then_inc(pool_s, 1)
                pool.wait_ge(pool_s, at(i, 1, j, 3))
                nc.gpsimd.tensor_tensor(rs[:, j % 2], ms[:],
                                        half[:, 1, 0:2 * TT].rearrange("p (h c) -> p h c", c=TT), ALU.pow).then_inc(rs_ok, 1)

            with nc.gpsimd.Fori(0, NB) as i:
                pool.wait_ge(heads_out, i + 1)
                pool.sem_inc(gate, 1)
                nc.gpsimd.memset(Uf, 0.0).then_inc(eye_ok, 1)
                pool.wait_ge(eye_ok, i * 2 + 1)
                pool.sem_inc(gate, 1)
                nc.gpsimd.memset(Uf.rearrange("p (a b) -> p a b", b=33)[:, :, 0], 1.0).then_inc(eye_ok, 1)
                pool.wait_ge(sel_ok, i * 3 + 3)
                pool.wait_ge(z_ok, i * (8 * HB) + 1)
                log_decay_steps(i, 0)
                for j in range(HB):
                    if j + 1 < HB:
                        log_decay_steps(i, j + 1)
                    pool.wait_ge(e_ok, at(i, 1, j, 1))
                    pool.wait_ge(kk_out, at(i, 2, j, 2))
                    nc.gpsimd.tensor_tensor(PT[:, 8 * j:8 * j + 8, :].rearrange("p (h c) e -> p h c e", h=2),
                                            E.rearrange("p (h c) e -> p h c e", h=2),
                                            KQm.unsqueeze(1).broadcast_to([P, 2, TT, P]), ALU.mult).then_inc(pt_ok, 1)
                pool.wait_ge(kss_ok, at(i, 1, HB - 1, 1))
                nc.gpsimd.tensor_tensor(flat(rinv[:]), flat(kss[:]), half[:, 0, :], ALU.pow).then_inc(rinv_ok, 1)
                pool.wait_ge(uc_ok, i * 2 + 1)
                pool.wait_ge(pt_ok, at(i, 1, HB - 1, 1))
                expand(i, 0, Uc, U[0], ux_ok)
                pool.wait_ge(uc_ok, i * 2 + 2)
                expand(i, 1, Tc, T, tx_ok)
                expand(i, 1, Uc, U[1], ux_ok)
                for j in range(HB):
                    if j:
                        norm_factor(i, j - 1)
                    if j + 2 < HB:
                        expand(i, j + 2, Tc, T, tx_ok)
                        pool.wait_ge(w_made, at(i, 4, j, 4))
                        expand(i, j + 2, Uc, U[j % 2], ux_ok)
                norm_factor(i, HB - 1)

        @block.vector
        def _(dve):
            own = Own(dve, own_p)
            dve.sem_inc(z_ok, 9)
            dve.sem_inc(heads_out, 1)
            own.did(nc.vector.memset(sign[:], 1.0))
            own.wait()
            own.did(nc.vector.memset(sign[:, 0:1], -1.0))
            own.wait()
            dve.wait_ge(decays_ok, 1)

            def scale_kq(i, j, own):
                dve.wait_ge(sq_ok, at(i, 8, j, 8))
                nc.vector.tensor_scalar(kss[:, j, :], ssk[:, j, :], EPS2, None, ALU.add).then_inc(kss_ok, 1)
                dve.wait_ge(kss_ok, at(i, 1, j, 1))
                own.did(nc.vector.reciprocal(r2[:, j, :], kss[:, j, :]))
                own.wait()
                own.did(nc.vector.scalar_tensor_tensor(out=nbp[:, j], in0=bsel[:, 2 * j:2 * j + 2, :], scalar=-1.0,
                                                       in1=r2[:, j, :].unsqueeze(1).broadcast_to([P, 2, TT]),
                                                       op0=ALU.mult, op1=ALU.mult))
                dve.wait_ge(kk_made, at(i, 1, j, 1))
                four = psA[:].rearrange("p n (m c) -> p n m c", c=P)
                nc.vector.tensor_tensor(KKm, four[:, 0], strict.unsqueeze(1).broadcast_to([P, TT, P]), ALU.mult)\
                    .then_inc(kk_out, 1)
                if j:
                    dve.wait_ge(pt_ok, at(i, 1, j - 1, 1))
                nc.vector.tensor_tensor(KQm, four[:, 1], upper.unsqueeze(1).broadcast_to([P, TT, P]), ALU.mult)\
                    .then_inc(kk_out, 1)
                dve.wait_ge(kk_out, at(i, 2, j, 2))
                dve.wait_ge(e_ok, at(i, 1, j, 1))
                own.wait()
                for h in range(2):
                    for c in range(TT):
                        nc.vector.scalar_tensor_tensor(out=C[:, 8 * j + 4 * h + c, :], in0=E[:, 4 * h + c, :],
                                                       scalar=nbp[:, j, h, c:c + 1], in1=KKm[:, c, :],
                                                       op0=ALU.mult, op1=ALU.mult).then_inc(c_ok, 1)

            def invert_16(i, own):
                dve.wait_ge(cc_ok, at(i, 4, HB - 1, 4))
                own.did(nc.vector.transpose(Cf[:, 0:1024].rearrange("p (c s) -> p c s", s=32),
                                            Cc.rearrange("p m c -> p c m")))
                dve.wait_ge(eye_ok, i * 2 + 2)
                cd, ud = (f.rearrange("p (a x) -> p a x", a=2)[:, :, 0:512].rearrange("p a (c s) -> p a c s", s=32)
                          for f in (Cf, Uf))
                for s in range(15):
                    later, rows = slice(s + 1, 16), s + 1
                    shape = [P, 2, 15 - s, rows]
                    t = tmp[:, 0:2 * (15 - s) * rows].rearrange("p (a c r) -> p a c r", a=2, r=rows)
                    own.wait()
                    own.did(nc.vector.tensor_tensor(t, cd[:, :, later, s:s + 1].broadcast_to(shape),
                                                    ud[:, :, s:s + 1, 0:rows].broadcast_to(shape), ALU.mult))
                    own.wait()
                    own.did(nc.vector.tensor_tensor(ud[:, :, later, 0:rows], ud[:, :, later, 0:rows], t, ALU.add))
                own.wait()
                blocks = Uf[:, 0:1024].rearrange("p (c s) -> p c s", s=32)
                nc.vector.transpose(Uc[:].rearrange("p m c -> p c m"), blocks).then_inc(uc_ok, 1)
                nc.vector.transpose(Tc[:].rearrange("p m s -> p s m"), blocks.rearrange("p c s -> p s c")).then_inc(uc_ok, 1)
                dve.wait_ge(uc_ok, i * 2 + 2)
                for grp in range(2):
                    expand_group(nc.vector, 0, grp, Tc, T, tx_ok)

            def doubled(i, j, kind, lv, grp):
                if kind == "V" and lv == 0:
                    dve.wait_ge(vt_made, at(i, 1, j, 1))
                    dve.wait_ge(rinv_ok, i + 1)
                    nc.vector.tensor_tensor(vr[j % 2][:, grp], psZ[:, grp, :].rearrange("p (c e) -> p c e", e=P),
                                            rinv[:, j, :].unsqueeze(2).broadcast_to([P, TT, P]), ALU.mult).then_inc(vr_ok, 1)
                elif kind == "Z":
                    dve.wait_ge(z_made, at(i, 6, j, 2 * lv + grp + 1))
                    dve.sem_inc(gate_v, 1)
                    level = masks2[:, 2 + lv, :].bitcast(mybir.dt.int32)
                    nc.vector.copy_predicated(U[j % 2][:, 4 * grp:4 * grp + 4, :], level.unsqueeze(1).broadcast_to([P, 4, P]),
                                              psZ[:, grp, :].rearrange("p (m c) -> p m c", c=P)).then_inc(u_ok2, 1)

            def chunk_part(i, j, c, fill):
                slot = j % 2
                if c:
                    dve.wait_ge(ks_made, at(i, 3, j, c))
                    for h in range(2):
                        nc.vector.scalar_tensor_tensor(out=R[:, h, :], in0=psK[:, h, :],
                                                       scalar=dsel[:, 0, 2 * j + h, c:c + 1], in1=vr[slot][:, h, c, :],
                                                       op0=ALU.mult, op1=ALU.subtract).then_inc(r_ok, 1)
                fill(4 * c)
                dve.wait_ge(w_made, at(i, 4, j, c + 1))
                if c < TT - 1:
                    if c or j:
                        dve.wait_ge(ds_made, at(i, 3, j, c))
                    nc.vector.tensor_tensor(we[:], psW[:, 0:2, :], wsce[:, j, :, c:c + 1].broadcast_to([P, 2, P]), ALU.mult)\
                        .then_inc(we_ok, 1)
                if c or j:
                    dve.wait_ge(o_made, at(i, 4, j, c))
                nc.vector.tensor_tensor(w_sb[:], psW[:, 0:2, :], wsc[:, j, :, c:c + 1].broadcast_to([P, 2, P]), ALU.mult)\
                    .then_inc(w_ok, 1)
                fill(4 * c + 1)
                if c < TT - 1:
                    dve.wait_ge(ds_made, at(i, 3, j, c + 1))
                    if c or j:
                        dve.wait_ge(qs_made, at(i, 3, j, c))
                    if c:
                        dve.wait_ge(s_ok, at(i, 5, j, S_COUNT[c]))
                        for h in range(2):
                            nc.vector.scalar_tensor_tensor(out=S[:, h, :], in0=S[:, h, :],
                                                           scalar=dsel[:, 2, 2 * j + h, c:c + 1], in1=psK[:, 2 + h, :],
                                                           op0=ALU.mult, op1=ALU.add).then_inc(s_ok, 1)
                    else:
                        nc.vector.tensor_copy(S[:], psK[:, 2:4, :]).then_inc(s_ok, 1)
                fill(4 * c + 2)
                dve.wait_ge(o_made, at(i, 4, j, c + 1))
                out = O[slot][:, :, c, :]
                if c:
                    dve.wait_ge(qt_ok, at(i, 6, j, 2 * c))
                    nc.vector.tensor_tensor(out, psO[:, 2:4, :], qt[:], ALU.add).then_inc(o_ok, 1)
                else:
                    nc.vector.tensor_copy(out, psO[:, 2:4, :]).then_inc(o_ok, 1)
                fill(4 * c + 3)

            def finish(i, j):
                dve.wait_ge(rs_ok, at(i, 1, j, 1))
                for h in range(2):
                    for c in range(TT):
                        zz = z[:, c, bass.ds(i * (2 * HB * P) + (2 * j + h) * P, P)]
                        nc.vector.scalar_tensor_tensor(out=zz, in0=O[j % 2][:, h, c, :], scalar=rs[:, j % 2, h, c:c + 1],
                                                       in1=zz, op0=ALU.mult, op1=ALU.mult).then_inc(z_ok, 1)

            OWN_STEPS = 39
            with nc.vector.Fori(0, NB) as i:
                own = Own(dve, own_s, i * OWN_STEPS)
                dve.wait_ge(z_ok, i * (8 * HB) + 9)
                heads = bass.ds(i * (2 * HB), 2 * HB)
                for to, src in ((dsel[:].rearrange("p n h c -> p n c h"), decays[:, :, :, heads]),
                                (gsel[:].rearrange("p h c -> p c h"), g[:, :, heads]),
                                (bsel[:].rearrange("p h c -> p c h"), beta[:, :, heads])):
                    nc.vector.tensor_copy(to, src).then_inc(sel_ok, 1)
                dve.wait_ge(sel_ok, i * 3 + 3)
                dve.wait_ge(consts_in, 16)
                for j in range(HB):
                    scale_kq(i, j, own)
                nc.vector.tensor_scalar(qe[:], ssq[:], EPS2, P * EPS2, ALU.add, ALU.mult).then_inc(scales_ok, 1)
                nc.vector.tensor_tensor(wsc[:], nbp[:], sign[:].unsqueeze(1).unsqueeze(1).broadcast_to([P, HB, 2, TT]),
                                        ALU.mult).then_inc(scales_ok, 1)
                dve.wait_ge(scales_ok, i * 3 + 2)
                nc.vector.tensor_tensor(wsce[:], wsc[:], dsel[:, 1].rearrange("p (j h) c -> p j h c", h=2),
                                        ALU.mult).then_inc(scales_ok, 1)
                invert_16(i, own)
                for kind, lv, grp in doubling_parts(0):
                    doubled(i, 0, kind, lv, grp)
                for j in range(HB):
                    parts = doubling_parts(j + 1) if j + 1 < HB else None

                    def fill(n):
                        if parts:
                            doubled(i, j + 1, *parts[n])

                    for c in range(TT):
                        chunk_part(i, j, c, fill)
                        if c == 1 and j:
                            finish(i, j - 1)
                dve.wait_ge(o_ok, at(i, 4, HB - 1, 4))
                dve.sem_inc(heads_out, 1)
                finish(i, HB - 1)
                assert own.n == OWN_STEPS, own.n


def kernel(**inputs):
    import numpy as _np
    import concourse.bacc as _bacc
    from concourse.bass_utils import run_bass_kernel_spmd as _run

    nc = _bacc.Bacc("TRN2", target_bir_lowering=False, num_devices=1)
    f = {k: _np.ascontiguousarray(v) for k, v in inputs.items()}

    def by_channel(v):
        return _np.ascontiguousarray(v.reshape(-1, P).T)

    def taps(w):
        return _np.ascontiguousarray(w.reshape(w.shape[0], -1, P).transpose(2, 1, 0))

    arrays = {
        "x": f["x"][0],
        "xT": _np.ascontiguousarray(f["x"][0].T),
        "w_in": f["w_in"],
        "masks": square_masks(),
        "masks2": block_masks(),
        "att_bias": attention_bias(),
        "small": _np.concatenate([f["dt_bias"][0], f["a_log"][0], f["d_skip"][0],
                                  f["gdn_dt_bias_2"][0], f["gdn_a_log_2"][0]]),
        "conv1": taps(_np.concatenate([f["conv_w"][0], f["conv_b"]], 0)),
        "mix_g": by_channel(_np.concatenate([f["att_norm_g"][0], f["ssm_norm_g"][0]])),
        "w_out": f["w_out"],
        "ln_g": f["ln_g"][0],
        "ln_b": f["ln_b"][0],
        "c": by_channel(f["c_2"][0]),
        "ada_w": f["ada_w_2"],
        "ada_b": by_channel(f["ada_b_2"][0]),
        "norm_g": by_channel(f["norm_g_2"][0]),
        "gdn_w_in": f["gdn_w_in_2"],
        "conv2": taps(f["gdn_conv_w_2"][0]),
        "gdn_g": by_channel(_np.tile(f["gdn_norm_w_2"][0], V_HEADS)),
        "gdn_w_out": f["gdn_w_out_2"],
        "final_g": f["final_g_2"],
    }
    a = {k: nc.dram_tensor("in_" + k, v.shape, F32, kind="ExternalInput").ap() for k, v in arrays.items()}
    a["x1"] = nc.dram_tensor("x1_kept", (SEQ, D_MODEL), F32, kind="Internal").ap()
    a["out"] = nc.dram_tensor("out_0", (1, SEQ, D_MODEL), F32, kind="ExternalOutput").ap()[0]
    build(nc, a)
    r = _run(nc, [{"in_" + k: v for k, v in arrays.items()}], core_ids=[0])
    return r.results[0]["out_0"]
```
